# Optimizing a Trainium2 kernel written in Bass

```python
import math
import jax, jax.numpy as jnp
from jax import lax
import numpy as np

D_MODEL = 1024
BATCH = 1
SEQ = 1024
DEPTH = 1
DEC_BATCH = 8
DEC_SEQ = 4
PAST_LEN = 256
PAGE_SIZE = 128

CM_WIDTH = 256
CM_GROUPS = 4
CM_GROUP_DIM = CM_WIDTH // CM_GROUPS
CM_CHUNK = 128
POOL_WIDTH = 256
POOL_WINDOWS = (2, 4, 8, 16)
POOL_GROUP_DIM = POOL_WIDTH // len(POOL_WINDOWS)
POOL_MAXW = max(POOL_WINDOWS)
POOL_HIST = POOL_MAXW - 1
FOX_HEADS = 4
FOX_HEAD_DIM = 64
FOX_WIDTH = FOX_HEADS * FOX_HEAD_DIM
Q_BLOCK = 128
SSD_HEADS = 4
SSD_HEAD_DIM = 64
SSD_WIDTH = SSD_HEADS * SSD_HEAD_DIM
SSD_GROUPS = 2
SSD_STATE = 128
SSD_CONV = 4
SSD_CHUNK = 128
SSD_CONV_DIM = SSD_WIDTH + 2 * SSD_GROUPS * SSD_STATE
D_FF = 2816
FFN_CONV = 3
N_BRANCH = 4
EPS = 1e-6
IN_SPLITS = (2 * CM_WIDTH, POOL_WIDTH, 3 * FOX_WIDTH, FOX_HEADS, SSD_WIDTH, SSD_CONV_DIM, SSD_HEADS, N_BRANCH * D_MODEL)
N_IN = sum(IN_SPLITS)

kernel_name = 'hybrid_gated_branch_decoder_step'

def rmsnorm(x, g):
    xf = x.astype(jnp.float32)
    y = xf * lax.rsqrt(jnp.mean(xf * xf, axis=-1, keepdims=True) + EPS)
    return (y * g.astype(jnp.float32)).astype(x.dtype)

def causal_dwconv(xp, w, b):
    c = xp.shape[-1]
    y = lax.conv_general_dilated(xp, w[:, None, :].astype(xp.dtype), (1,), 'VALID',
                                 dimension_numbers=('NWC', 'WIO', 'NWC'), feature_group_count=c)
    return y + b.astype(xp.dtype)

def chunk_spatial_mix(v, ws, bs):
    n, L, _ = v.shape
    Lp = -(-L // CM_CHUNK) * CM_CHUNK
    vp = jnp.pad(v, ((0, 0), (0, Lp - L), (0, 0))).reshape(n, Lp // CM_CHUNK, CM_CHUNK, CM_GROUPS, CM_GROUP_DIM)
    causal = jnp.tril(jnp.ones((CM_CHUNK, CM_CHUNK), ws.dtype))
    s = jnp.einsum('gts,ncsgd->nctgd', ws * causal, vp) + bs.T[None, None, :, :, None]
    return s.reshape(n, Lp, CM_WIDTH)[:, :L]

def multiscale_pool(seq, pos, pool_w, pool_scale):
    n, L, _ = seq.shape
    cs = jnp.cumsum(seq.astype(jnp.float32), axis=1)
    cs_pad = jnp.concatenate([jnp.zeros((n, POOL_MAXW, POOL_WIDTH), jnp.float32), cs], axis=1)
    diffs = []
    for g, w in enumerate(POOL_WINDOWS):
        cols = slice(g * POOL_GROUP_DIM, (g + 1) * POOL_GROUP_DIM)
        start = POOL_MAXW - w
        wsum = cs[:, :, cols] - cs_pad[:, start:start + L, cols]
        count = jnp.minimum(pos + 1, w).astype(jnp.float32)[None, :, None]
        diffs.append(wsum / count - seq[:, :, cols].astype(jnp.float32))
    d = jnp.stack(diffs, axis=2)
    y = jnp.einsum('nlgc,gcd->nlgd', d, pool_w.astype(jnp.float32)).reshape(n, L, POOL_WIDTH)
    return (y * pool_scale.astype(jnp.float32)).astype(seq.dtype)

def fox_attend_block(q, cq, qpos, k, v, ck, kpos):
    s = jnp.einsum('nqhd,nkhd->nhqk', q, k).astype(jnp.float32) * (FOX_HEAD_DIM ** -0.5)
    bias = jnp.swapaxes(cq, 1, 2)[..., :, None] - jnp.swapaxes(ck, 1, 2)[..., None, :]
    mask = kpos[None, :] <= qpos[:, None]
    p = jax.nn.softmax(jnp.where(mask, s + bias, -jnp.inf), axis=-1)
    return jnp.einsum('nhqk,nkhd->nqhd', p.astype(v.dtype), v)

def fox_prompt(q, k, v, c, pos):
    n, L = q.shape[:2]
    nb = L // Q_BLOCK
    qb = jnp.moveaxis(q.reshape(n, nb, Q_BLOCK, FOX_HEADS, FOX_HEAD_DIM), 1, 0)
    cb = jnp.moveaxis(c.reshape(n, nb, Q_BLOCK, FOX_HEADS), 1, 0)
    pb = pos.reshape(nb, Q_BLOCK)
    out = lax.map(lambda a: fox_attend_block(a[0], a[1], a[2], k, v, c, pos), (qb, cb, pb))
    return jnp.moveaxis(out, 0, 1).reshape(n, L, FOX_HEADS, FOX_HEAD_DIM)

def ssd_chunked(xdt, da, bm, cm, h0):
    n, L = xdt.shape[:2]
    T = math.gcd(L, SSD_CHUNK)
    nc = L // T
    R = SSD_HEADS // SSD_GROUPS
    X = xdt.reshape(n, nc, T, SSD_GROUPS, R, SSD_HEAD_DIM)
    A = da.reshape(n, nc, T, SSD_GROUPS, R)
    B = bm.reshape(n, nc, T, SSD_GROUPS, SSD_STATE)
    C = cm.reshape(n, nc, T, SSD_GROUPS, SSD_STATE)
    acs = jnp.cumsum(A, axis=2)
    causal = (jnp.arange(T)[:, None] >= jnp.arange(T)[None, :])[None, None, :, :, None, None]
    seg = acs[:, :, :, None] - acs[:, :, None, :]
    decay = jnp.exp(jnp.where(causal, seg, -jnp.inf))
    cb = jnp.einsum('nctgk,ncsgk->nctsg', C, B)
    y_diag = jnp.einsum('nctsg,nctsgr,ncsgrp->nctgrp', cb, decay, X)
    to_end = jnp.exp(acs[:, :, -1:] - acs)
    chunk_states = jnp.einsum('nctgk,nctgr,nctgrp->ncgrpk', B, to_end, X)
    chunk_decay = jnp.exp(acs[:, :, -1])

    def carry_state(h, inp):
        s_c, d_c = inp
        return h * d_c[..., None, None] + s_c, h

    h_last, h_in = lax.scan(carry_state, h0.reshape(n, SSD_GROUPS, R, SSD_HEAD_DIM, SSD_STATE),
                            (jnp.moveaxis(chunk_states, 1, 0), jnp.moveaxis(chunk_decay, 1, 0)))
    h_in = jnp.moveaxis(h_in, 0, 1)
    y_off = jnp.einsum('nctgk,ncgrpk,nctgr->nctgrp', C, h_in, jnp.exp(acs))
    y = (y_diag + y_off).reshape(n, L, SSD_HEADS, SSD_HEAD_DIM)
    return y, h_last.reshape(n, SSD_HEADS, SSD_HEAD_DIM, SSD_STATE)

def gather_pages(pool, page_table):
    g = pool[page_table]
    return g.reshape(g.shape[0], g.shape[1] * g.shape[2], *g.shape[3:])

def decoder_layer(x, w, pos, past):
    n, L, _ = x.shape
    adt = x.dtype
    f32 = jnp.float32
    h = rmsnorm(x, w['norm1_g'])
    proj = h @ w['w_in']
    split_points = [int(i) for i in np.cumsum(IN_SPLITS)[:-1]]
    a_uv, pool_in, qkv, f_raw, z, xbc, dt_raw, gate_raw = jnp.split(proj, split_points, axis=-1)

    u, va = jnp.split(jax.nn.gelu(a_uv), 2, axis=-1)
    va = rmsnorm(va, w['cm_norm_g'])
    y_a = u * chunk_spatial_mix(va, w['cm_ws'], w['cm_b']).astype(adt)

    if past is None:
        pool_seq, pool_pos = pool_in, pos
    else:
        pool_seq = jnp.concatenate([past['pool'].astype(adt), pool_in], axis=1)
        pool_pos = jnp.arange(POOL_HIST + L) + (pos[0] - POOL_HIST)
    y_b = multiscale_pool(pool_seq, pool_pos, w['pool_w'], w['pool_scale'])[:, -L:]
    new_pool = pool_seq[:, -POOL_HIST:]

    q, k, v = [t.reshape(n, L, FOX_HEADS, FOX_HEAD_DIM) for t in jnp.split(qkv, 3, axis=-1)]
    logf = jax.nn.log_sigmoid((f_raw + w['fox_bf']).astype(f32))
    if past is None:
        y_c = fox_prompt(q, k, v, jnp.cumsum(logf, axis=1), pos)
    else:
        k_all = jnp.concatenate([past['k'].astype(adt), k], axis=1)
        v_all = jnp.concatenate([past['v'].astype(adt), v], axis=1)
        c_all = jnp.cumsum(jnp.concatenate([past['logf'].astype(f32), logf], axis=1), axis=1)
        kpos = jnp.arange(k_all.shape[1])
        y_c = fox_attend_block(q, c_all[:, -L:], pos, k_all, v_all, c_all, kpos)
    y_c = y_c.reshape(n, L, FOX_WIDTH)

    conv_hist = jnp.zeros((n, SSD_CONV - 1, SSD_CONV_DIM), adt) if past is None else past['ssd_conv'].astype(adt)
    xbc_ext = jnp.concatenate([conv_hist, xbc], axis=1)
    xbc_act = jax.nn.silu(causal_dwconv(xbc_ext, w['ssd_conv_w'], w['ssd_conv_b'])).astype(f32)
    xs, bm, cm = jnp.split(xbc_act, [SSD_WIDTH, SSD_WIDTH + SSD_GROUPS * SSD_STATE], axis=-1)
    xs = xs.reshape(n, L, SSD_HEADS, SSD_HEAD_DIM)
    bm = bm.reshape(n, L, SSD_GROUPS, SSD_STATE)
    cm = cm.reshape(n, L, SSD_GROUPS, SSD_STATE)
    dt = jax.nn.softplus((dt_raw + w['ssd_dt_bias']).astype(f32))
    a = -jnp.exp(w['ssd_a_log'].astype(f32))
    h0 = jnp.zeros((n, SSD_HEADS, SSD_HEAD_DIM, SSD_STATE), f32) if past is None else past['ssd'].astype(f32)
    y_s, h_last = ssd_chunked(xs * dt[..., None], dt * a, bm, cm, h0)
    y_s = (y_s + w['ssd_d'].astype(f32)[:, None] * xs).reshape(n, L, SSD_WIDTH)
    y_d = rmsnorm(y_s * jax.nn.silu(z.astype(f32)), w['ssd_norm_g']).astype(adt)

    merged = jnp.zeros_like(x)
    for i, y_i in enumerate((y_a, y_b, y_c, y_d)):
        gate = jax.nn.sigmoid(gate_raw[..., i * D_MODEL:(i + 1) * D_MODEL])
        merged = merged + gate * (y_i.astype(adt) @ w['w_branch'][i])
    x = x + merged @ w['w_out']

    h2 = rmsnorm(x, w['norm2_g'])
    up = h2 @ w['ffn_up']
    ffn_hist = jnp.zeros((n, FFN_CONV - 1, 2 * D_FF), adt) if past is None else past['ffn_conv'].astype(adt)
    up_ext = jnp.concatenate([ffn_hist, up], axis=1)
    g_ff, u_ff = jnp.split(causal_dwconv(up_ext, w['ffn_conv_w'], w['ffn_conv_b']), 2, axis=-1)
    x = x + (jax.nn.silu(g_ff) * u_ff) @ w['ffn_down']

    new_state = dict(k=k, v=v, logf=logf, chunk_v=va, pool=new_pool,
                     ssd_conv=xbc_ext[:, -(SSD_CONV - 1):], ssd=h_last, ffn_conv=up_ext[:, -(FFN_CONV - 1):])
    return x, new_state

def setup_inputs(seed: int = 0) -> dict:
    key = jax.random.key(seed)
    ks = iter(jax.random.split(key, 48))
    f32 = jnp.float32

    def nrm(shape, scale):
        return scale * jax.random.normal(next(ks), shape, f32)

    n_pages = PAST_LEN // PAGE_SIZE
    n_phys = (DEC_BATCH * n_pages * 5 + 3) // 4
    page_table = jax.random.permutation(next(ks), n_phys)[:DEC_BATCH * n_pages].reshape(DEC_BATCH, n_pages).astype(jnp.int32)
    dt0 = jnp.exp(jax.random.uniform(next(ks), (DEPTH, SSD_HEADS), f32, math.log(1e-3), math.log(1e-1)))
    return {
        'x_prompt': nrm((BATCH, SEQ, D_MODEL), 1.0),
        'x_sample': nrm((DEC_BATCH, DEC_SEQ, D_MODEL), 1.0),
        'cache_k': nrm((DEPTH, n_phys, PAGE_SIZE, FOX_HEADS, FOX_HEAD_DIM), 1.0),
        'cache_v': nrm((DEPTH, n_phys, PAGE_SIZE, FOX_HEADS, FOX_HEAD_DIM), 1.0),
        'cache_logf': jax.nn.log_sigmoid(3.0 + nrm((DEPTH, n_phys, PAGE_SIZE, FOX_HEADS), 1.0)),
        'page_table': page_table,
        'state_pool': nrm((DEPTH, DEC_BATCH, POOL_HIST, POOL_WIDTH), 1.0),
        'state_ssd_conv': nrm((DEPTH, DEC_BATCH, SSD_CONV - 1, SSD_CONV_DIM), 1.0),
        'state_ssd': nrm((DEPTH, DEC_BATCH, SSD_HEADS, SSD_HEAD_DIM, SSD_STATE), 0.5),
        'state_ffn_conv': nrm((DEPTH, DEC_BATCH, FFN_CONV - 1, 2 * D_FF), 1.0),
        'norm1_g': 1.0 + nrm((DEPTH, D_MODEL), 0.1),
        'w_in': nrm((DEPTH, D_MODEL, N_IN), D_MODEL ** -0.5),
        'cm_norm_g': 1.0 + nrm((DEPTH, CM_WIDTH), 0.1),
        'cm_ws': nrm((DEPTH, CM_GROUPS, CM_CHUNK, CM_CHUNK), 0.5 * CM_CHUNK ** -0.5),
        'cm_b': 1.0 + nrm((DEPTH, CM_GROUPS, CM_CHUNK), 0.1),
        'pool_w': nrm((DEPTH, len(POOL_WINDOWS), POOL_GROUP_DIM, POOL_GROUP_DIM), POOL_GROUP_DIM ** -0.5),
        'pool_scale': 1.0 + nrm((DEPTH, POOL_WIDTH), 0.1),
        'fox_bf': 3.0 + nrm((DEPTH, FOX_HEADS), 0.5),
        'ssd_conv_w': nrm((DEPTH, SSD_CONV, SSD_CONV_DIM), SSD_CONV ** -0.5),
        'ssd_conv_b': nrm((DEPTH, SSD_CONV_DIM), 0.01),
        'ssd_dt_bias': dt0 + jnp.log(-jnp.expm1(-dt0)),
        'ssd_a_log': jnp.log(jax.random.uniform(next(ks), (DEPTH, SSD_HEADS), f32, 1.0, 16.0)),
        'ssd_d': 1.0 + nrm((DEPTH, SSD_HEADS), 0.1),
        'ssd_norm_g': 1.0 + nrm((DEPTH, SSD_WIDTH), 0.1),
        'w_branch': nrm((DEPTH, N_BRANCH, CM_WIDTH, D_MODEL), CM_WIDTH ** -0.5),
        'w_out': nrm((DEPTH, D_MODEL, D_MODEL), D_MODEL ** -0.5),
        'norm2_g': 1.0 + nrm((DEPTH, D_MODEL), 0.1),
        'ffn_up': nrm((DEPTH, D_MODEL, 2 * D_FF), D_MODEL ** -0.5),
        'ffn_conv_w': nrm((DEPTH, FFN_CONV, 2 * D_FF), FFN_CONV ** -0.5),
        'ffn_conv_b': nrm((DEPTH, 2 * D_FF), 0.01),
        'ffn_down': nrm((DEPTH, D_FF, D_MODEL), D_FF ** -0.5),
        'final_norm_g': 1.0 + nrm((D_MODEL,), 0.1),
    }

def reference(x_prompt, x_sample, cache_k, cache_v, cache_logf, page_table, state_pool, state_ssd_conv,
              state_ssd, state_ffn_conv, norm1_g, w_in, cm_norm_g, cm_ws, cm_b, pool_w, pool_scale, fox_bf,
              ssd_conv_w, ssd_conv_b, ssd_dt_bias, ssd_a_log, ssd_d, ssd_norm_g, w_branch, w_out, norm2_g,
              ffn_up, ffn_conv_w, ffn_conv_b, ffn_down, final_norm_g):
    pos_prompt = jnp.arange(x_prompt.shape[1])
    pos_sample = PAST_LEN + jnp.arange(x_sample.shape[1])
    xp, xs = x_prompt, x_sample
    st_p, st_s = [], []
    for l in range(DEPTH):
        w = dict(norm1_g=norm1_g[l], w_in=w_in[l], cm_norm_g=cm_norm_g[l], cm_ws=cm_ws[l], cm_b=cm_b[l],
                 pool_w=pool_w[l], pool_scale=pool_scale[l], fox_bf=fox_bf[l], ssd_conv_w=ssd_conv_w[l],
                 ssd_conv_b=ssd_conv_b[l], ssd_dt_bias=ssd_dt_bias[l], ssd_a_log=ssd_a_log[l], ssd_d=ssd_d[l],
                 ssd_norm_g=ssd_norm_g[l], w_branch=w_branch[l], w_out=w_out[l], norm2_g=norm2_g[l],
                 ffn_up=ffn_up[l], ffn_conv_w=ffn_conv_w[l], ffn_conv_b=ffn_conv_b[l], ffn_down=ffn_down[l])
        past = dict(k=gather_pages(cache_k[l], page_table), v=gather_pages(cache_v[l], page_table),
                    logf=gather_pages(cache_logf[l], page_table), pool=state_pool[l],
                    ssd_conv=state_ssd_conv[l], ssd=state_ssd[l], ffn_conv=state_ffn_conv[l])
        xp, sp = decoder_layer(xp, w, pos_prompt, None)
        xs, ss = decoder_layer(xs, w, pos_sample, past)
        st_p.append(sp)
        st_s.append(ss)
    y_prompt = rmsnorm(xp, final_norm_g)
    y_sample = rmsnorm(xs, final_norm_g)

    def stacked(states, name):
        return jnp.stack([s[name] for s in states], axis=0)

    k_prompt, v_prompt, logf_prompt = stacked(st_p, 'k'), stacked(st_p, 'v'), stacked(st_p, 'logf')
    k_sample, v_sample, logf_sample = stacked(st_s, 'k'), stacked(st_s, 'v'), stacked(st_s, 'logf')
    chunk_v_sample = stacked(st_s, 'chunk_v')
    pool_prompt, pool_sample = stacked(st_p, 'pool'), stacked(st_s, 'pool')
    ssd_conv_prompt, ssd_conv_sample = stacked(st_p, 'ssd_conv'), stacked(st_s, 'ssd_conv')
    ssd_prompt, ssd_sample = stacked(st_p, 'ssd'), stacked(st_s, 'ssd')
    ffn_conv_prompt, ffn_conv_sample = stacked(st_p, 'ffn_conv'), stacked(st_s, 'ffn_conv')
    return (y_prompt, y_sample, k_prompt, v_prompt, logf_prompt, k_sample, v_sample, logf_sample,
            chunk_v_sample, pool_prompt, pool_sample, ssd_conv_prompt, ssd_conv_sample, ssd_prompt, ssd_sample,
            ffn_conv_prompt, ffn_conv_sample)


_drawn_inputs = setup_inputs


def setup_inputs(seed=0):
    import zlib

    import numpy as np

    out = dict(_drawn_inputs(seed))
    spreads = {}
    factors = {'cache_logf': 3.138, 'ssd_conv_b': 2.81, 'ffn_conv_b': 8.0}
    for name, (base, spread) in spreads.items():
        noise = np.random.default_rng([zlib.crc32(name.encode()), seed]).standard_normal(out[name].shape)
        drawn = base * np.exp(spread * noise) if base else spread * noise
        out[name] = __import__('jax').numpy.asarray(drawn.astype(out[name].dtype))
    for name, factor in factors.items():
        out[name] = (out[name] * factor).astype(out[name].dtype)
    return out
```

```python
import numpy as np
from contextlib import ExitStack

import concourse.bass as bass
from concourse import mybir

F32 = mybir.dt.float32
F32R = mybir.dt.float32r
I32 = mybir.dt.int32
ACT = mybir.ActivationFunctionType
ALU = mybir.AluOpType
AX = mybir.AxisListType

P = 128
D = 1024
KD = D // P
SEQ, NB, NQ = 1024, 8, 4
NS = NB * NQ
T = SEQ + NS
CH = T // 3
NT = SEQ // P
PAST, PAGE = 256, 128
NPG = PAST // PAGE
CMW, PLW = 256, 256
WINDOWS = (2, 4, 8, 16)
PH = 15
NH, HD = 4, 64
SST = 128
CV = 3
XBC = 768
FF = 2816
NFF = FF // P
FH = 2
EPS = 1e-6
NEG = -1e30
COL_POOL, COL_Q, COL_K, COL_V = 512, 768, 1024, 1280
COL_F, COL_Z, COL_XBC, COL_DT, COL_GATE = 1536, 1540, 1796, 2564, 2568
N_IN = 6664

PE_W = PH + SEQ + NB * (PH + NQ)
XE_W = CV + SEQ + NB * (CV + NQ)
FE_W = FH + SEQ + NB * (FH + NQ)

PV_G1, PV_G2, PV_CW, PV_CB, PV_PS, PV_SG, PV_FB, PV_FW = 0, 8, 16, 40, 46, 48, 50, 94
PV_N = 226

_CONSTS = [("ident", 128), ("tri01", 128), ("ssdneg", 128), ("attneg", 128), ("blk01", 32), ("blkneg", 32),
           ("sattneg", 32), ("expand", 128), ("qsel", 4), ("pfix", 30), ("acssel", 512),
           ("pairsel", 256), ("bmask", 32), ("q4", 4), ("rep4", 32), ("gsel", 256), ("bsel", 8),
           ("ones", 1), ("lastsel", 32)]
COFF, CN = {}, 0
for _n, _w in _CONSTS:
    COFF[_n] = (CN, _w)
    CN += _w


def constants():
    c = np.zeros((P, CN), np.float32)

    def put(name, a, row=0):
        o, w = COFF[name]
        a = np.asarray(a, np.float32).reshape(a.shape[0], w)
        c[row:row + a.shape[0], o:o + w] = a

    i = np.arange(P)
    put("ident", np.eye(P))
    put("tri01", i[None, :] >= i[:, None])
    put("ssdneg", np.where(i[None, :] >= i[:, None], 0, NEG))
    put("attneg", np.where(i[None, :] <= i[:, None], 0, NEG))
    s = np.arange(NS)
    same = (s[:, None] // NQ == s[None, :] // NQ) & (s[None, :] >= s[:, None])
    put("blk01", same)
    put("blkneg", np.where(same, 0, NEG))
    r_b, r_q = i // (NH * NQ), i % NQ
    put("sattneg", np.where((r_b[:, None] == s[None, :] // NQ) & (s[None, :] % NQ <= r_q[:, None]), 0, NEG))
    put("expand", i[None, :] // NQ == s[:, None])
    put("qsel", r_q[:, None] == np.arange(NQ)[None, :])
    w = np.array(WINDOWS, np.float32)
    fix = np.zeros((P, 2, PH), np.float32)
    for b in range(2):
        for half in range(2):
            win = WINDOWS[2 * b + half]
            fix[64 * half:64 * half + 64, b] = win / np.minimum(np.arange(PH) + 1, win)
    put("pfix", fix)
    put("acssel", np.repeat(np.eye(NH)[:, :, None], P, 2), row=64)
    pair = np.zeros((NH, 2, P))
    for g in range(2):
        for half in range(2):
            pair[2 * g + half, g, 64 * half:64 * half + 64] = 1
    put("pairsel", pair, row=64)
    put("gsel", pair)
    put("bmask", s[:, None] // NQ == s[None, :] // NH)
    put("q4", s[:, None] % NQ == np.arange(NQ)[None, :])
    put("rep4", np.arange(NQ)[:, None] == s[None, :] % NQ)
    put("ones", np.ones((P, 1)))
    put("lastsel", s[:, None] == s[None, :] // NQ * NQ + NQ - 1)
    put("bsel", s[:, None] // NQ == np.arange(NB)[None, :])
    return c


class Order:

    def __init__(self, eng, own):
        self.eng, self.own, self.n, self.turn = eng, own, {}, {}

    def value(self, sem):
        n = self.n.get(sem.name, 0)
        if sem.name in self.turn:
            i, first, per = self.turn[sem.name]
            return (i - first) * per + n
        return n

    def run(self, ins, sem=None):
        sem = sem or self.own
        if isinstance(sem, tuple):
            ins.then_inc(sem[0], 1)
            self.eng.wait_ge(sem[0], sem[1])
            return
        ins.then_inc(sem, 1)
        self.n[sem.name] = self.n.get(sem.name, 0) + 1
        self.eng.wait_ge(sem, self.value(sem))

    def peel(self):
        self.before = dict(self.n)

    def enter(self, i, first, extra=()):
        per = {name: n - self.before.get(name, 0) for name, n in self.n.items()}
        per.update({s.name: k for s, k in extra})
        self.base = dict(self.n)
        self.turn = {name: (i, first, k) for name, k in per.items()}

    def leave(self, turns):
        for name, (_, _, per) in self.turn.items():
            assert self.n.get(name, 0) - self.base.get(name, 0) == per, (name, self.n[name] - self.base[name], per)
            self.n[name] = self.base.get(name, 0) + per * turns
        self.turn = {}


def decoder_layer(nc, a, o):
    top = ExitStack()

    def sb(scope, name, shape, dt=F32):
        return scope.enter_context(nc.sbuf_tensor(name, shape, dt))

    def sem(name):
        return top.enter_context(nc.semaphore(name))

    cst = sb(top, "cst", [P, CN])
    pv = sb(top, "pv", [P, PV_N])
    eps = sb(top, "eps", [P, 1])
    mark = sb(top, "mark", [P, 3])
    stat7 = sb(top, "stat7", [P, 3, NT + 1])
    h_hi = sb(top, "h_hi", [P, KD, T], F32R)
    h_lo = sb(top, "h_lo", [P, KD, T], F32R)
    y_all = sb(top, "y_all", [P, 2 * 4, T])
    w_raw = [sb(top, f"w_raw{n}", [P, KD, P]) for n in range(2)]
    w_hi = [sb(top, f"w_hi{n}", [P, KD, P], F32R) for n in range(2)]
    w_lo = [sb(top, f"w_lo{n}", [P, KD, P], F32R) for n in range(2)]

    def const(name, rows=slice(0, P), cols=None):
        off, w = COFF[name]
        return cst[rows, off:off + w] if cols is None else cst[rows, off + cols.start:off + cols.stop]

    ident = const("ident")
    ps = [top.enter_context(nc.psum_tensor(f"ps{n}", [P, 3, 512], F32)) for n in range(2)]
    pt = [top.enter_context(nc.psum_tensor(f"pt{n}", [P, 512], F32)) for n in range(2)]

    def flat(n):
        return ps[n][:, :, :].rearrange("p c n -> p (c n)")

    def chunked(n, rows=slice(0, P)):
        return ps[n][rows, :, 0:CH]

    def in_chunks(ap):
        return ap.rearrange("p (c n) -> p c n", c=3)

    s1 = ExitStack()
    stg = [sb(s1, f"stg{n}", [P, T]) for n in range(2)]
    sdt = sb(s1, "sdt", [P, T])
    sdt_t = sb(s1, "sdt_t", [P, NT + 1, 100])
    hist_t = sb(s1, "hist_t", [P, 6 * 24 + 2 * 120])
    stat = sb(s1, "stat", [P, 4, NT + 1])
    ast = sb(s1, "ast", [P, 3, NT * NH])
    qs_new = sb(s1, "qs_new", [P, 2, NS])
    ks_new = sb(s1, "ks_new", [P, 2, NS])
    vs_new = sb(s1, "vs_new", [NS, 256])
    pages = sb(s1, "pages", [1, NB * NPG], I32)

    s1a = ExitStack()
    small = sb(s1a, "small", [P, 4])
    hist_p = sb(s1a, "hist_p", [NB * PH, PLW])
    hist_x = sb(s1a, "hist_x", [NB * CV, XBC])
    s0 = ExitStack()
    x_tok = [sb(s0, f"x_tok{n}", [P, D]) for n in range(3)]
    x_scaled = [sb(s0, f"x_scaled{n}", [P, D]) for n in range(2)]
    h_f = [sb(s0, f"h_f{n}", [P, KD, P]) for n in range(2)]
    vec1 = sb(s0, "vec1", [94, P])
    vec2 = sb(s0, "vec2", [88, P])
    vec3 = sb(s0, "vec3", [44, P])
    junk = sb(s0, "junk", [P, D])
    s0.close()
    va = sb(s1a, "va", [P, NT + 1, CMW])
    u_f = sb(s1a, "u_f", [P, 2, T])
    p_ext = sb(s1a, "p_ext", [P, 2, PE_W + 4])
    win_a = sb(s1a, "win_a", [P, 2, PE_W])
    win_b = sb(s1a, "win_b", [P, 2, PE_W])
    pw = sb(s1a, "pw", [P, 2, P])
    cmb = sb(s1a, "cmb", [NH, P])
    pjunk = sb(s1a, "pjunk", [P, CMW])[:, :]
    ws = win_a[:, 0, 0:4 * P].rearrange("p (g s) -> p g s", g=4)
    wst = win_b[:, 0, 0:4 * P].rearrange("p (g s) -> p g s", g=4)
    wsm = win_b[0:NS, 1, 0:4 * NS].rearrange("p (g s) -> p g s", g=4)
    cmg = win_a[:, 1, 0:CMW]
    p_state = sb(s1a, "p_state", [P, 2, 9 * PH])
    p_out = win_b[:, 1, 512:512 + 2 * PLW].rearrange("p (b n) -> p b n", b=2)
    dk = [win_a[:, 0, 0:T], win_a[:, 1, 0:T], win_b[:, 0, 0:T], win_b[:, 1, 0:T]]
    s1a.close()

    JOBS = [("fdt", 0, None)]
    JOBS += [("pool", b, COL_POOL + b * P) for b in range(2)]
    JOBS += [("va", b, CMW + b * P) for b in range(2)]
    JOBS += [("u", b, b * P) for b in range(2)]
    N1A = len(JOBS)
    JOBS += [("q", b, COL_Q + b * P) for b in range(2)]
    JOBS += [("k", b, COL_K + b * P) for b in range(2)]
    JOBS += [("v", b, COL_V + b * P) for b in range(2)]
    N1B = len(JOBS)
    JOBS += [("xbc", b, COL_XBC + b * P) for b in range(6)]
    JOBS += [("z", b, COL_Z + b * P) for b in range(2)]
    N1C = len(JOBS)
    ring = {j: n for n, j in enumerate([j[:2] for j in JOBS if j[0] != "u"])}
    jobs_a, jobs_b, jobs_c = JOBS[:N1A], JOBS[N1A:N1B], JOBS[N1B:N1C]
    slots = [("x", i) for i in range(NT + 1)] + [j[:2] for j in jobs_a]
    slots += [("mixb", 0), ("mixb", 1), ("mixa", 0), ("mixa", 1)]
    slots += [j[:2] for j in jobs_b]
    slots += [("att", qb, h) for qb in range(NT) for h in range(NH)]
    slots += [j[:2] for j in jobs_c]
    slots += [("ssd", c) for c in range(NT + 1)]
    slot = {s: m for m, s in enumerate(slots)}
    THIRDS = [(0, 4), (4, 8), (8, 9)]
    batches = [("vec",), ("hist",), ("sdt", 0), ("sdt", 1), ("va", 0, 0), ("va", 0, 1), ("va", 0, 2)]
    batches += [("va", 1, 0), ("va", 1, 1), ("va", 1, 2), ("ws",), ("wsm",), ("pstate", 0), ("pstate", 1)]
    batches += [(kind, b, n) for kind in "kv" for b in range(2) for n in range(3)]
    steps = [(qb, h) for qb in range(NT) for h in range(NH)]

    def quads(qb):
        return [(lo, min(lo + 4, qb + 1)) for lo in range(0, qb + 1, 4)]

    for n, (qb, h) in enumerate(steps):
        batches += [("p", n, k) for k in range(len(quads(qb)))]
    batches += [("clog",)]
    for n in range(NB):
        if n >= 1:
            batches.append(("so", n - 1))
        batches += [("sk", n), ("ss", n), ("sp", n)]
        if n == 7:
            batches += [("z", 0, k) for k in range(3)]
    batches += [("so", NB - 1)] + [("z", 1, k) for k in range(3)] + [("xst", 0), ("xst", 1)]
    for c in range(NT + 1):
        batches += [("xb", c)]
        if c == NT:
            for b in range(NB):
                batches += [("sh", b), ("sn", b)]
    batches += [("hp",)] + [("yd", t) for t in range(NT + 1)]
    batch = {}

    ld_const, ld_vec, ld_small, ld_hist = sem("ld_const"), sem("ld_vec"), sem("ld_small"), sem("ld_hist")
    ld_pw, ld_ws = sem("ld_pw"), sem("ld_ws")
    ld_x = [sem(f"ld_x{n}") for n in range(3)]
    ld_w = [sem(f"ld_w{n}") for n in range(2)]
    stored = sem("stored")
    w_split = sem("w_split")
    w_zeroed, small_zeroed, a_zeroed = sem("w_zeroed"), sem("small_zeroed"), sem("a_zeroed")
    pool_own, act_own, dve_own = sem("pool_own"), sem("act_own"), sem("dve_own")
    x_sq, x_normed, h_hi_done, h_split = sem("x_sq"), sem("x_normed"), sem("h_hi_done"), sem("h_split")
    slot_full = sem("slot_full")
    slot_free = [sem(f"slot_free{n}") for n in range(2)]
    pt_full = sem("pt_full")
    pt_free = [sem(f"pt_free{n}") for n in range(2)]
    vec_done, stg_free = sem("vec_done"), sem("stg_free")
    dk_abs, dk_exp, dk_u, dk_ln = sem("dk_abs"), sem("dk_exp"), sem("dk_u"), sem("dk_ln")
    alog_exp, sdt_done = sem("alog_exp"), sem("sdt_done")
    a_sum, a_rms, va_done, u_done = sem("a_sum"), sem("a_rms"), sem("va_done"), sem("u_done")
    wst_done, wsm_done, pd_done = sem("wst_done"), sem("wsm_done"), sem("pd_done")
    pstate_in, pstate_out, y_a_done = sem("pstate_in"), sem("pstate_out"), sem("y_a_done")

    def slot_filled(eng, s):
        eng.wait_ge(slot_full, slot[s] + 1)

    def slot_drained(eng, s):
        eng.wait_ge(slot_free[slot[s] % 2], slot[s] // 2 + 1)

    def slot_open(eng, s):
        if slot[s] >= 2:
            eng.wait_ge(slot_free[slot[s] % 2], slot[s] // 2)

    def free_of(s):
        return slot_free[slot[s] % 2], slot[s] // 2 + 1

    def pt_filled(eng, b):
        eng.wait_ge(pt_full, batch[b] + 1)

    def pt_drained(eng, b):
        eng.wait_ge(pt_free[batch[b] % 2], batch[b] // 2 + 1)

    def pt_open(eng, b):
        if batch[b] >= 2:
            eng.wait_ge(pt_free[batch[b] % 2], batch[b] // 2)

    def pt_of(b):
        return pt[batch[b] % 2]

    def ptf_of(b):
        return pt_free[batch[b] % 2], batch[b] // 2 + 1

    batch.update({b: n for n, b in enumerate(batches)})

    s1b = ExitStack()
    q_a = sb(s1b, "q_a", [HD + 2, NH, SEQ])
    k_a = sb(s1b, "k_a", [HD + 2, NH, SEQ])
    v_tok = sb(s1b, "v_tok", [P, NT + 1, 256])
    k_out = [sb(s1b, f"k_out{n}", [P, 4, P]) for n in range(2)]
    pr = [stg[n][:, 0:SEQ] for n in range(2)]
    pr_t = [sb(s1b, f"pr_t{n}", [P, NT, P]) for n in range(2)]
    ident_r = sb(s1b, "ident_r", [P, P], F32R)
    attneg_r = sb(s1b, "attneg_r", [P, P], F32R)
    s1b.close()

    s1c = ExitStack()
    xc = sb(s1c, "xc", [P, 6, T])
    zt = sb(s1c, "zt", [P, NT + 1, 256])
    xstate = sb(s1c, "xstate", [P, 6, 9 * CV])
    sx = ExitStack()
    x_ext = sb(sx, "x_ext", [P, XE_W + 4])
    x_cv = sb(sx, "x_cv", [P, XE_W])
    k_pg = [sb(sx, f"k_pg{n}", [P, NPG, 256]) for n in range(2)]
    v_pg = sb(sx, "v_pg", [P, NPG, 256])
    q_s = sb(sx, "q_s", [P, 2, NB, NH * NQ])
    kt_s = sb(sx, "kt_s", [P, 2, PAST])
    p_s = sb(sx, "p_s", [NH * NQ, PAST + NS])
    pt_s = sb(sx, "pt_s", [P, 3, NH * NQ])
    lf_pg = sb(sx, "lf_pg", [P, NPG, NB, NH])
    lf_new = sb(sx, "lf_new", [NS, NS])
    c_s = sb(sx, "c_s", [NS, PAST + NQ])
    nc_s = sb(sx, "nc_s", [NS, PAST + NS])
    cq_s = sb(sx, "cq_s", [NS, P])
    sx.close()
    sd = ExitStack()
    seg = [sb(sd, f"seg{n}", [P, NH, P]) for n in range(2)]
    xb = [sb(sd, f"xb{n}", [P, 512]) for n in range(2)]
    xdt = [sb(sd, f"xdt{n}", [P, NH, HD]) for n in range(2)]
    xte = [sb(sd, f"xte{n}", [P, NH, HD]) for n in range(2)]
    xd = [sb(sd, f"xd{n}", [P, NH, HD]) for n in range(2)]
    yoff = sb(sd, "yoff", [P, NH, HD])
    hst = sb(sd, "hst", [P, NH, HD])
    dec = [sb(sd, f"dec{n}", [P, 3, NH]) for n in range(2)]
    xst_out = stg[0][0:9 * CV, 0:XBC]
    h0 = [sb(sd, f"h0_{n}", [P, 2, P]) for n in range(2)]
    h0t = [sb(sd, f"h0t{n}", [P, 2, P]) for n in range(2)]
    ctm = stg[1][:, 0:512].rearrange("p (g b n) -> p g b n", g=2, b=NB)
    h_out = [stg[1][:, 512 + 256 * n:768 + 256 * n].rearrange("p (g k) -> p g k", g=2) for n in range(2)]
    xtm = [sb(sd, f"xtm{n}", [NS, 256]) for n in range(2)]
    sdec = sb(sd, "sdec", [P, 2, NB])
    d_b = sb(sd, "d_b", [P, NH])
    eacs = sb(sd, "eacs", [P, NT + 1, NH])
    sd.close()
    s1c.close()

    att_zeroed, att_rows, v_done = sem("att_zeroed"), sem("att_rows"), sem("v_done")
    k_ready, k_sent = sem("k_ready"), [sem(f"k_sent{n}") for n in range(2)]
    att_max, att_norm, att_pv, att_out = sem("att_max"), sem("att_norm"), sem("att_pv"), sem("att_out")
    qk_ready = sem("qk_ready")
    c_zeroed, sx_ready, clog_in, clog_done = sem("c_zeroed"), sem("sx_ready"), sem("clog_in"), sem("clog_done")
    ld_pages, ld_lf, ld_v = sem("ld_pages"), sem("ld_lf"), sem("ld_v")
    ld_k = [sem(f"ld_k{n}") for n in range(2)]
    ss_max, ss_exp, ss_done = sem("ss_max"), sem("ss_exp"), sem("ss_done")
    x_conv, x_act, xstate_in, xst_ready, z_done = (sem(n) for n in ("x_conv", "x_act", "xstate_in", "xst_ready",
                                                                    "z_done"))
    d_zeroed, ld_d, eacs_done = sem("d_zeroed"), sem("ld_d"), sem("eacs_done")
    seg_in, seg_exp, seg_cb, dec_exp = sem("seg_in"), sem("seg_exp"), sem("seg_cb"), sem("dec_exp")
    xdt_done, xd_done, xte_done, xtm_done = sem("xdt_done"), sem("xd_done"), sem("xte_done"), sem("xtm_done")
    ssd_back, h_next, y_gated, ctm_done = sem("ssd_back"), sem("h_next"), sem("y_gated"), sem("ctm_done")
    ld_h0 = [sem(f"ld_h0_{n}") for n in range(2)]
    h_ready, h_sent, sdec_done = sem("h_ready"), [sem(f"h_sent{n}") for n in range(2)], sem("sdec_done")
    d_rms, yd_ready = sem("d_rms"), sem("yd_ready")

    s1.close()
    merged, x1 = y_all, y_all
    s3 = ExitStack()
    bw_raw = [sb(s3, f"bw_raw{n}", [P, 2, P]) for n in range(2)]
    bw_hi = [sb(s3, f"bw_hi{n}", [P, 2, P], F32R) for n in range(2)]
    bw_lo = [sb(s3, f"bw_lo{n}", [P, 2, P], F32R) for n in range(2)]
    sg = sb(s3, "sg", [P, T])
    y_hi = sb(s3, "y_hi", [P, KD, T], F32R)
    y_lo = sb(s3, "y_lo", [P, KD, T], F32R)
    s3.close()
    s46 = ExitStack()
    hist_f = sb(s46, "hist_f", [9 * FH, 2 * FF])
    fh = sb(s46, "fh", [P, 2 * NFF, NB * FH])
    fstate = sb(s46, "fstate", [P, 2 * NFF, 9 * FH])
    s4 = ExitStack()
    x_res = [sb(s4, f"x_res{n}", [P, NT + 1, P]) for n in range(2)]
    sq = sb(s4, "sq", [P, T])
    ssq = sb(s4, "ssq", [P, T])
    rms = sb(s4, "rms", [P, T])
    h2_f = [sb(s4, f"h2_f{n}", [P, T]) for n in range(2)]
    ones_m = sb(s4, "ones_m", [P, P])
    s4.close()
    f_raw = w_raw + [sb(s46, "w_raw2", [P, KD, P])]
    f_hi = w_hi + [sb(s46, "w_hi2", [P, KD, P], F32R)]
    f_lo = w_lo + [sb(s46, "w_lo2", [P, KD, P], F32R)]
    ext = [sb(s46, f"ext{n}", [P, FE_W + 4]) for n in range(2)]
    cv = [sb(s46, f"cv{n}", [P, FE_W]) for n in range(2)]
    act_hi = sb(s46, "act_hi", [P, 2, T], F32R)
    act_lo = sb(s46, "act_lo", [P, 2, T], F32R)
    s46.close()
    y_out = [f_raw[n][:, :, :].rearrange("p k n -> p (k n)") for n in range(3)]
    gfin = ext[1][:, 0:D]
    squares = cv[0][:, 0:D]

    ld_b = [sem(f"ld_b{n}") for n in range(2)]
    y_hi_done, y_split, b_split = sem("y_hi_done"), sem("y_split"), sem("b_split")
    gate_full, br_full, sg_ready, br_read, merged_done = (sem(n) for n in ("gate_full", "br_full", "sg_ready",
                                                                           "br_read", "merged_done"))
    m_hi_done, m_split, wo_full, wo_read, sq_ready, ssq_done = (sem(n) for n in ("m_hi_done", "m_split", "wo_full",
                                                                "wo_read", "sq_ready", "ssq_done"))
    ld_res, ld_fh, fh_full, fh_done = [sem(f"ld_res{n}") for n in range(2)], sem("ld_fh"), sem("fh_full"), sem("fh_done")
    ones_done, nm_full, nm_rms, h2_ready, h2_hi_done, h2_split = (sem(n) for n in ("ones_done", "nm_full", "nm_rms",
                                                                  "h2_ready", "h2_hi_done", "h2_split"))
    ld_f = [sem(f"ld_f{n}") for n in range(3)]
    up_full, up_read, cv0_done, cv_taps, silu_done, prod_done = (sem(n) for n in ("up_full", "up_read", "cv0_done",
                                                                 "cv_taps", "silu_done", "prod_done"))
    act_hi_done, act_split, dn_full, dn_done = sem("act_hi_done"), sem("act_split"), sem("dn_full"), sem("dn_done")
    out_full, out_free = sem("out_full"), [sem(f"out_free{n}") for n in range(2)]
    ld_gfin, y_sq, y_ready, fs_ready, f_zeroed = (sem(n) for n in ("ld_gfin", "y_sq", "y_ready", "fs_ready", "f_zeroed"))
    y_sent = [sem(f"y_sent{n}") for n in range(3)]
    W3 = N1C
    W4 = W3 + 4 * KD
    W6 = W4 + KD

    block = top.enter_context(nc.Block())
    n_stores = [0]

    N_STORES_1A = 6

    def x_new(cv):
        return cv[:, SEQ + CV:SEQ + CV + NB * (CV + NQ)].rearrange("p (s n) -> p s n", s=NB)[:, :, 0:NQ]

    def free_of_1a(eng):
        slot_drained(eng, ("mixa", 1))
        slot_drained(eng, ("mixb", 1))
        eng.wait_ge(stored, 16 * N_STORES_1A)

    N_STORES_1B = N_STORES_1A + 2
    N_STORES_1 = N_STORES_1B + 2

    def free_of_1b(eng):
        eng.wait_ge(att_out, NT * NH)
        eng.wait_ge(stored, 16 * N_STORES_1B)
        for n in range(2):
            eng.wait_ge(k_sent[n], 16 * 3)

    def free_of_sx(eng):
        eng.wait_ge(x_act, 6)
        pt_drained(eng, ("so", NB - 1))
        pt_drained(eng, ("z", 1, 2))

    def rows_of(i):
        return P if i < NT else NS

    def free_of_s1(eng):
        pt_drained(eng, ("yd", NT))
        eng.wait_ge(stored, 16 * N_STORES_1)
        eng.wait_ge(h_sent[0], 16 * 5)
        eng.wait_ge(h_sent[1], 16 * 4)

    def ffn_kinds(e):
        return (0, e), (1, e + NFF)

    def down_sets():
        return [(m, c) for m in range(KD) for c in range(3)]

    def spaced(x):
        new = x[:, SEQ + FH:FE_W].rearrange("p (s n) -> p s n", s=NB)[:, :, 0:NQ]
        return x[:, 0:SEQ], new

    def packed(x):
        return x[:, 0:SEQ], x[:, SEQ:T].rearrange("p (s n) -> p s n", s=NB)

    @block.sync
    def _(sp):
        def store(dst, src):
            sp.dma_start(dst, src).then_inc(stored, 16)
            n_stores[0] += 1

        def load_weights(n):
            kind, b, col = JOBS[n]
            if n >= 2:
                sp.wait_ge(w_split, n - 1)
            w = a["w_in"][0].rearrange("(k p) n -> p k n", p=P)
            if kind == "fdt":
                sp.wait_ge(w_zeroed, 1)
                sp.dma_start(w_raw[0][:, :, 0:NH], w[:, :, COL_F:COL_F + NH]).then_inc(ld_w[0], 16)
                sp.dma_start(w_raw[0][:, :, 32:32 + NH], w[:, :, COL_DT:COL_DT + NH]).then_inc(ld_w[0], 16)
            else:
                sp.dma_start(w_raw[n % 2][:, :, :], w[:, :, col:col + P]).then_inc(ld_w[n % 2], 16)

        for i in range(NT + 1):
            if i >= 3:
                sp.wait_ge(x_normed, i - 2)
            src = a["x_prompt"][0, i * P:(i + 1) * P, :] if i < NT else a["x_sample"].rearrange("b q d -> (b q) d")
            sp.dma_start(x_tok[i % 3][0:rows_of(i), :], src).then_inc(ld_x[i % 3], 16)
            if i == 2:
                load_weights(0)
                load_weights(1)
        sp.wait_ge(a_zeroed, 1)
        for g in range(4):
            r = slice(64 * (g % 2), 64 * (g % 2) + 64)
            sp.dma_start(pw[r, g // 2, r], a["pool_w"][0, g]).then_inc(ld_pw, 16)
        sp.dma_start(cmb[:, :], a["cm_b"][0]).then_inc(ld_pw, 16)
        for n in range(2, 6):
            load_weights(n)
        sp.wait_ge(pd_done, 1)
        sp.dma_start(ws, a["cm_ws"][0].rearrange("g t s -> t g s")).then_inc(ld_ws, 16)
        sp.dma_start(cmg, a["cm_norm_g"].partition_broadcast(P).rearrange("p a c -> p (a c)")).then_inc(ld_ws, 16)
        load_weights(6)
        load_weights(N1A)
        load_weights(N1A + 1)
        pt_drained(sp, ("sdt", 1))
        store(o["logf_prompt"][0, 0].rearrange("(t p) h -> p t h", p=P), sdt_t[:, 0:NT, 0:NH])
        store(o["logf_sample"][0].rearrange("b q h -> (b q) h"), sdt_t[0:NS, NT, 0:NH])
        sp.wait_ge(pstate_out, 2)
        for lo, n in ((0, 5), (5, 4)):
            part = p_out[:, lo // 5, :]
            if lo == 0:
                store(o["pool_prompt"][0, 0], part[0:PH, :])
                store(o["pool_sample"][0, 0:4].rearrange("b r c -> (b r) c"), part[PH:5 * PH, :])
            else:
                store(o["pool_sample"][0, 4:8].rearrange("b r c -> (b r) c"), part[0:4 * PH, :])
        sp.wait_ge(va_done, 1)
        store(o["chunk_v_sample"][0].rearrange("b q c -> (b q) c"), va[0:NS, NT, :])
        N_STORES_A = n_stores[0]
        load_weights(N1A + 2)
        load_weights(N1A + 3)
        sp.wait_ge(att_zeroed, 1)
        sp.dma_start(q_a[HD:HD + 1, :, :], sdt[96:96 + NH, 0:SEQ]).then_inc(att_rows, 16)
        sp.dma_start(k_a[HD + 1:HD + 2, :, :], sdt[96:96 + NH, 0:SEQ]).then_inc(att_rows, 16)
        load_weights(N1A + 4)
        load_weights(N1A + 5)
        kp = o["k_prompt"][0, 0].rearrange("(t p) h d -> p t (h d)", p=P)
        for b in range(2):
            for n, (lo, hi) in enumerate(THIRDS):
                m = 3 * b + n
                sp.wait_ge(k_ready, m + 1)
                if hi <= NT:
                    dst, src = kp[:, lo:hi, b * P:(b + 1) * P], k_out[m % 2][:, :, :]
                else:
                    dst = o["k_sample"][0].rearrange("b q h d -> (b q) (h d)")[:, b * P:(b + 1) * P]
                    src = k_out[m % 2][0:NS, 0, :]
                sp.dma_start(dst, src).then_inc(k_sent[m % 2], 16)
        load_weights(N1B)
        load_weights(N1B + 1)
        sp.wait_ge(v_done, 1)
        store(o["v_prompt"][0, 0].rearrange("(t p) h d -> p t (h d)", p=P), v_tok[:, 0:NT, :])
        store(o["v_sample"][0].rearrange("b q h d -> (b q) (h d)"), v_tok[0:NS, NT, :])
        sp.dma_start(pages[:, :], a["page_table"].rearrange("(o b) n -> o (b n)", o=1)).then_inc(ld_pages, 16)
        free_of_1b(sp)
        sp.wait_ge(ld_pages, 16)
        n_phys = a["cache_k"].shape[1]
        cache_k, cache_v = (a[n][0].rearrange("n p h d -> n p (h d)") for n in ("cache_k", "cache_v"))

        def page(b, pg):
            return sp.value_load(pages[0:1, b * NPG + pg:b * NPG + pg + 1], min_val=0, max_val=n_phys - 1)

        for b in range(NB):
            for pg in range(NPG):
                sp.dma_start(lf_pg[:, pg, b, :], a["cache_logf"][0][bass.ds(page(b, pg), 1)]
                             .rearrange("o p h -> p (o h)")).then_inc(ld_lf, 16)
        for n in range(NB):
            if n >= 2:
                pt_filled(sp, ("sk", n - 2))
            for pg in range(NPG):
                sp.dma_start(k_pg[n % 2][:, pg, :], cache_k[bass.ds(page(n, pg), 1)]
                             .rearrange("o p c -> p (o c)")).then_inc(ld_k[n % 2], 16)
            if n >= 1:
                pt_filled(sp, ("so", n - 1))
            for pg in range(NPG):
                sp.dma_start(v_pg[:, pg, :], cache_v[bass.ds(page(n, pg), 1)]
                             .rearrange("o p c -> p (o c)")).then_inc(ld_v, 16)
            if n + 2 < NB:
                load_weights(N1B + n + 2)
        free_of_sx(sp)
        sp.dma_start(d_b[:, :], a["ssd_d"].partition_broadcast(P).rearrange("p a h -> p (a h)")).then_inc(ld_d, 16)
        sp.wait_ge(xst_ready, 2)
        store(o["ssd_conv_prompt"][0, 0], xst_out[0:CV, :])
        store(o["ssd_conv_sample"][0].rearrange("b r c -> (b r) c"), xst_out[CV:9 * CV, :])

        def by_pair(x):
            return x.rearrange("(g h) p k -> (h p) g k", g=2)

        for b in range(NB + 1):
            if b < NB:
                if b >= 2:
                    sp.wait_ge(h_ready, b - 1)
                sp.dma_start(h0[b % 2][:, :, :], by_pair(a["state_ssd"][0, b])).then_inc(ld_h0[b % 2], 16)
            if b >= 1:
                sp.wait_ge(h_ready, b)
                sp.dma_start(by_pair(o["ssd_sample"][0, b - 1]), h_out[(b - 1) % 2]).then_inc(h_sent[(b - 1) % 2], 16)
        sp.wait_ge(h_ready, NB + 1)
        sp.dma_start(by_pair(o["ssd_prompt"][0, 0]), h_out[0]).then_inc(h_sent[0], 16)
        sp.wait_ge(h_sent[0], 16 * 5)
        sp.wait_ge(h_sent[1], 16 * 4)
        def ring_of(n):
            return n % 2, n // 2 + 1 + (1 - n % 2)

        def at(expr):
            return expr if isinstance(expr, int) else sp.snap(expr)

        def load_block(base, q, per, i, src):
            n = base + q
            sp.wait_ge(w_split, i * per + (n - 1))
            sp.dma_start(w_raw[n % 2][:, :, :], src).then_inc(ld_w[n % 2], 16)

        w_in = a["w_in"][0].rearrange("(k p) n -> p k n", p=P)
        w_br = a["w_branch"][0].rearrange("i (k p) n -> p i k n", p=P)

        def load_stage3(j):
            first = isinstance(j, int)
            for q in range(4):
                gate_col, br_col = at(j * P + (COL_GATE + q * D)), at(j * P)
                load_block(W3, q, 4, j, w_in[:, :, bass.ds(gate_col, P)])
                if first and q == 0:
                    free_of_s1(sp)
                if first and q >= 2:
                    sp.wait_ge(b_split, q - 1)
                sp.dma_start(bw_raw[q % 2][:, :, :], w_br[:, q, :, bass.ds(br_col, P)]).then_inc(ld_b[q % 2], 16)

        load_stage3(0)
        with sp.Fori(1, KD) as j:
            load_stage3(j)
        w_out = a["w_out"][0].rearrange("(k p) n -> p k n", p=P)

        def load_stage4(i):
            for s in range(2):
                cols = bass.ds(at(i * (2 * P) + s * P), P)
                load_block(W4, s, 2, i, w_out[:, :, cols])
                if isinstance(i, int):
                    sp.wait_ge(merged_done, 3 * KD)
                else:
                    sp.wait_ge(wo_full, i * 2 + (s - 1))
                sp.dma_start(x_res[s][:, 0:NT, :], a["x_prompt"][0].rearrange("(t p) n -> p t n", p=P)
                             [:, :, cols]).then_inc(ld_res[s], 16)
                sp.dma_start(x_res[s][0:NS, NT, :], a["x_sample"].rearrange("b q n -> (b q) n")
                             [:, cols]).then_inc(ld_res[s], 16)

        load_stage4(0)
        sp.dma_start(hist_f[0:NB * FH, :], a["state_ffn_conv"][0].rearrange("b r c -> (b r) c")).then_inc(ld_fh, 16)
        with sp.Fori(1, KD // 2) as i:
            load_stage4(i)
        w_up = a["ffn_up"][0].rearrange("(k p) n -> p k n", p=P)
        w_dn = a["ffn_down"][0].rearrange("(j p) n -> p j n", p=P)

        def load_ffn(f, e, kind, i=0):
            where = at(e) if kind == "d" else at(e * P + (FF if kind == "u" else 0))
            if f >= 3:
                sp.wait_ge(w_split, i * 6 + (W6 + f - 2))
            dst = f_raw[f % 3]
            if kind == "d":
                src = w_dn[:, bass.ds(where, 1), :].rearrange("p o n -> p (o n)")
                dst = dst[:, :, :].rearrange("p k n -> p (k n)")
            else:
                src = w_up[:, :, bass.ds(where, P)]
                dst = dst[:, :, :]
            sp.dma_start(dst, src).then_inc(ld_f[f % 3], 16)

        sp.wait_ge(w_split, W6)
        load_ffn(0, 0, "g")
        load_ffn(1, 0, "u")
        sp.wait_ge(h2_split, KD)
        load_ffn(2, 1, "g")
        load_ffn(3, 1, "u")
        with sp.Fori(0, NFF // 2 - 1) as i:
            for f, (kind, de) in enumerate((("g", 2), ("u", 2), ("d", 0), ("d", 1), ("g", 3), ("u", 3))):
                load_ffn(4 + f, i * 2 + de, kind, i)
        n_ring = 4 + 6 * (NFF // 2 - 1)
        load_ffn(n_ring, NFF - 2, "d")
        load_ffn(n_ring + 1, NFF - 1, "d")
        sp.wait_ge(cv_taps, 2 * NFF)
        sp.dma_start(gfin, a["final_norm_g"].partition_broadcast(P)).then_inc(ld_gfin, 16)
        sp.wait_ge(fs_ready, 4)
        store(o["ffn_conv_prompt"][0, 0], hist_f[0:FH, :])
        store(o["ffn_conv_sample"][0].rearrange("b r c -> (b r) c"), hist_f[FH:9 * FH, :])
        for t in range(NT + 1):
            sp.wait_ge(y_ready, t + 1)
            dst = o["y_prompt"][0, t * P:(t + 1) * P, :] if t < NT else o["y_sample"].rearrange("b q d -> (b q) d")
            sp.dma_start(dst, y_out[t % 3][0:rows_of(t), :]).then_inc(y_sent[t % 3], 16)
        for n in range(3):
            sp.wait_ge(y_sent[n], 16 * 3)
        for n in range(2):
            sp.wait_ge(k_sent[n], 16 * 3)
        sp.wait_ge(stored, 16 * n_stores[0])

    @block.gpsimd
    def _(gp):
        od = Order(gp, pool_own)
        g = nc.gpsimd
        od.run(g.memset(w_raw[0][:, :, :], 0.0), w_zeroed)
        od.run(g.memset(small[:, :], 0.0), small_zeroed)
        od.run(g.memset(sdt[:, :], 0.0))
        od.run(g.memset(sdt_t[:, :, :], 0.0))
        gp.wait_ge(small_zeroed, 1)
        gp.wait_ge(ld_const, 16)
        gp.wait_ge(vec_done, 1)

        def gate_mark():
            g.tensor_tensor(mark[:, 0:1], eps[:, :], eps[:, :], ALU.add).then_inc(pool_own, 1)
            od.n[pool_own.name] += 1

        def split(raw, hi, lo):
            gate_mark()
            od.run(g.tensor_copy(hi, raw))
            od.run(g.tensor_tensor(lo, raw, hi.bitcast(F32), ALU.subtract), w_split)

        def split_job(n):
            s = n % 2
            count = n // 2 + 1 + (1 if s == 0 else 0)
            gp.wait_ge(ld_w[s], 16 * count)
            if n >= 2:
                slot_filled(gp, JOBS[n - 2][:2])
            split(w_raw[s][:, :, :], w_hi[s][:, :, :], w_lo[s][:, :, :])

        split_job(0)
        split_job(1)
        gp.wait_ge(h_split, NT + 1)
        od.run(g.memset(pw[:, :, :], 0.0))
        od.run(g.memset(p_ext[:, :, 0:PH], 0.0))
        od.run(g.memset(va[:, NT, :], 0.0), a_zeroed)
        for n in range(2, N1A):
            split_job(n)
        split_job(N1A)
        split_job(N1A + 1)
        free_of_1a(gp)
        od.run(g.memset(q_a[HD:HD + 2, :, :], -1.0))
        od.run(g.memset(k_a[HD:HD + 2, :, :], 1.0), att_zeroed)
        for n in range(N1A + 2, N1B + 2):
            split_job(n)
        free_of_1b(gp)
        od.run(g.memset(x_ext[:, 0:CV], 0.0))
        od.run(g.memset(q_s[:, :, :, :], 0.0), c_zeroed)
        for n in range(N1B + 2, N1C):
            split_job(n)
        free_of_sx(gp)
        gp.wait_ge(xst_ready, 2)
        od.run(g.memset(hst[:, :, :], 0.0))
        od.run(g.memset(ctm, 0.0), d_zeroed)
        gp.wait_ge(ld_d, 16)
        for c in range(NT + 1):
            r = rows_of(c)
            n = c % 2
            pt_drained(gp, ("xb", c))
            if c >= 2:
                gp.wait_ge(ssd_back, c - 1)
                gp.wait_ge(y_gated, c - 1)
            x = xb[n][0:r, 0:256].rearrange("p (h d) -> p h d", h=NH)
            od.run(g.tensor_tensor(xdt[n][0:r], x, sdt_t[0:r, c, 32:32 + NH].unsqueeze(2).to_broadcast([r, NH, HD]),
                                   ALU.mult), xdt_done)
            od.run(g.tensor_tensor(xd[n][0:r], x, d_b[0:r, :].unsqueeze(2).to_broadcast([r, NH, HD]), ALU.mult),
                   xd_done)
            gp.wait_ge(dec_exp, c + 1)
            od.run(g.tensor_tensor(xte[n][0:r], xdt[n][0:r], dec[n][0:r, 1, :].unsqueeze(2)
                                   .to_broadcast([r, NH, HD]), ALU.mult), xte_done)
        for b in range(NB):
            if b >= 2:
                pt_filled(gp, ("sn", b - 2))
            od.run(g.tensor_scalar(xtm[b % 2][:, :], xte[NT % 2][0:NS].rearrange("p h d -> p (h d)"),
                                   const("bsel", slice(0, NS), slice(b, b + 1)), None, ALU.mult), xtm_done)
        def split_block(base, q, per, i):
            n = base + q
            gp.wait_ge(ld_w[n % 2], i * (8 * per) + 16 * (n // 2 + 1 + (1 - n % 2)))
            split(w_raw[n % 2][:, :, :], w_hi[n % 2][:, :, :], w_lo[n % 2][:, :, :])

        def split_stage3(j):
            first = isinstance(j, int)
            for q in range(4):
                def gate_block():
                    if first and q < 2:
                        slot_filled(gp, JOBS[N1C - 2 + q][:2])
                    else:
                        gp.wait_ge(gate_full, j * 4 + (q - 1))
                    split_block(W3, q, 4, j)

                def branch_block():
                    gp.wait_ge(ld_b[q % 2], j * 32 + 16 * (q // 2 + 1))
                    if not first or q >= 2:
                        gp.wait_ge(br_full, j * 4 + (q - 1))
                    gate_mark()
                    od.run(g.tensor_copy(bw_hi[q % 2][:, :, :], bw_raw[q % 2][:, :, :]))
                    od.run(g.tensor_tensor(bw_lo[q % 2][:, :, :], bw_raw[q % 2][:, :, :], bw_hi[q % 2][:, :, :].bitcast(F32),
                                           ALU.subtract), b_split)

                if first and q == 0:
                    gate_block()
                    free_of_s1(gp)
                    branch_block()
                else:
                    branch_block()
                    gate_block()

        od.peel()
        split_stage3(0)
        with gp.Fori(1, KD) as j:
            od.enter(j, 1)
            split_stage3(j)
        od.leave(KD - 1)

        def split_stage4(i):
            for s in range(2):
                if isinstance(i, int):
                    gp.wait_ge(gate_full, 4 * KD - 1 + s)
                else:
                    gp.wait_ge(wo_full, i * 2 + (s - 1))
                split_block(W4, s, 2, i)

        od.peel()
        split_stage4(0)
        with gp.Fori(1, KD // 2) as i:
            od.enter(i, 1)
            split_stage4(i)
        od.leave(KD // 2 - 1)
        gp.wait_ge(merged_done, 3 * KD)
        od.run(g.memset(ones_m[:, :], 1.0), ones_done)
        def split_ffn(f, i=0):
            gp.wait_ge(ld_f[f % 3], i * 32 + 16 * (f // 3 + 1))
            split(f_raw[f % 3][:, :, :], f_hi[f % 3][:, :, :], f_lo[f % 3][:, :, :])

        gp.wait_ge(wo_full, KD)
        split_ffn(0)
        split_ffn(1)
        gp.wait_ge(h2_split, KD)
        od.run(g.memset(ext[0][:, 0:FH], 0.0))
        od.run(g.memset(ext[1][:, 0:FH], 0.0), f_zeroed)
        split_ffn(2)
        gp.wait_ge(up_full, 1)
        od.peel()
        split_ffn(3)
        with gp.Fori(0, NFF // 2 - 1) as i:
            od.enter(i, 0, [(pool_own, 12), (w_split, 6)])
            gp.wait_ge(up_full, i * 4 + 3)
            split_ffn(4, i)
            split_ffn(5, i)
            gp.wait_ge(up_full, i * 4 + 4)
            split_ffn(6, i)
            gp.wait_ge(up_full, i * 4 + 5)
            split_ffn(7, i)
            gp.wait_ge(up_full, i * 4 + 6)
            split_ffn(8, i)
            gp.wait_ge(dn_full, i * 24 + 24)
            split_ffn(9, i)
        od.leave(NFF // 2 - 1)
        gp.wait_ge(dn_full, 24 * (NFF // 2 - 1))
        split_ffn(4 + 6 * (NFF // 2 - 1))
        gp.wait_ge(up_full, 2 * NFF - 1)
        split_ffn(5 + 6 * (NFF // 2 - 1))

    @block.scalar
    def _(act):
        od = Order(act, act_own)
        sc = nc.scalar
        act.dma_start(cst[:, :], a["consts"]).then_inc(ld_const, 16)
        rows = [("norm1_g", vec1[0:8, :]), ("norm2_g", vec1[8:16, :]), ("ssd_conv_w", vec1[16:40, :]),
                ("ssd_conv_b", vec1[40:46, :]), ("pool_scale", vec1[46:48, :]), ("ssd_norm_g", vec1[48:50, :]),
                ("ffn_conv_b", vec1[50:94, :])]
        for name, dst in rows:
            src = a[name][0]
            src = src.rearrange("t (b p) -> (t b) p", p=P) if name == "ssd_conv_w" else \
                src.rearrange("(b p) -> b p", p=P)
            act.dma_start(dst, src).then_inc(ld_vec, 16)
        fw = a["ffn_conv_w"][0].rearrange("t (b p) -> (t b) p", p=P)
        act.dma_start(vec2[:, :], fw[0:88, :]).then_inc(ld_vec, 16)
        act.dma_start(vec3[:, :], fw[88:132, :]).then_inc(ld_vec, 16)
        act.wait_ge(small_zeroed, 1)
        act.dma_start(small[0:NH, 0:1], a["fox_bf"].rearrange("a h -> h a")).then_inc(ld_small, 16)
        act.dma_start(small[32:32 + NH, 0:1], a["ssd_dt_bias"].rearrange("a h -> h a")).then_inc(ld_small, 16)
        act.dma_start(small[32:32 + NH, 1:2], a["ssd_a_log"].rearrange("a h -> h a")).then_inc(ld_small, 16)
        act.dma_start(hist_p[:, :], a["state_pool"][0].rearrange("b r c -> (b r) c")).then_inc(ld_hist, 16)
        act.dma_start(hist_x[:, :], a["state_ssd_conv"][0].rearrange("b r c -> (b r) c")).then_inc(ld_hist, 16)

        def h_hi_copy(i):
            r = rows_of(i)
            slot_drained(act, ("x", i))
            od.run(sc.activation(h_hi[:, :, i * P:i * P + r], h_f[i % 2][:, :, 0:r], ACT.Copy), h_hi_done)

        act.wait_ge(vec_done, 1)
        for i in range(NT + 1):
            r = rows_of(i)
            act.wait_ge(ld_x[i % 3], 16 * (i // 3 + 1))
            od.run(sc.activation(junk[0:r, :], x_tok[i % 3][0:r, :], ACT.Square, accum_out=stat[0:r, 0, i:i + 1]))
            od.run(sc.activation(stat[0:r, 1, i:i + 1], stat[0:r, 0, i:i + 1], ACT.Sqrt, scale=1.0 / D, bias=eps[0:r, :]),
                   x_sq)
            if i >= 1:
                h_hi_copy(i - 1)
        h_hi_copy(NT)

        act.wait_ge(ld_small, 48)
        od.run(sc.activation(small[32:36, 2:3], small[32:36, 1:2], ACT.Exp), alog_exp)

        def evacuate(job, func, **kw):
            s = job[:2]
            n = ring[s]
            slot_filled(act, s)
            if n >= 2:
                act.wait_ge(stg_free, n - 1)
            r = slice(0, 36) if s[0] == "fdt" else slice(0, P)
            od.run(sc.activation(in_chunks(stg[n % 2][r, :]), chunked(slot[s] % 2, r), func, **kw), free_of(s))

        for job in jobs_a:
            s = job[:2]
            if s[0] == "fdt":
                evacuate(job, ACT.Identity, bias=small[0:36, 0:1])
                act.wait_ge(dk_abs, 1)
                od.run(sc.activation(dk[1][0:36, :], dk[0][0:36, :], ACT.Exp, scale=-1.0), dk_exp)
                act.wait_ge(dk_u, 1)
                od.run(sc.activation(dk[0][0:36, :], dk[2][0:36, :], ACT.Ln), dk_ln)
            elif s[0] == "pool":
                evacuate(job, ACT.Copy)
            elif s[0] == "va":
                evacuate(job, ACT.Gelu_apprx_tanh)
            else:
                slot_filled(act, s)
                od.run(sc.activation(in_chunks(u_f[:, s[1], :]), chunked(slot[s] % 2), ACT.Gelu_apprx_tanh), free_of(s))
        act.wait_ge(a_sum, 1)
        od.run(sc.activation(stat[:, 1, :], stat[:, 0, :], ACT.Sqrt, scale=1.0 / CMW, bias=eps[:, :]), a_rms)
        for b in range(2):
            slot_filled(act, ("mixb", b))
            od.run(sc.activation(in_chunks(y_all[:, 2 + b, :]), chunked(slot[("mixb", b)] % 2), ACT.Copy,
                                 scale=pv[:, PV_PS + b:PV_PS + b + 1]), free_of(("mixb", b)))
        for job in jobs_b:
            evacuate(job, ACT.Copy, scale=HD ** -0.5 if job[0] == "q" else 1.0)
        def exponentials(n):
            s = ("att",) + steps[n]
            nk = (steps[n][0] + 1) * P
            act.wait_ge(att_max, n + 1)
            od.run(sc.activation(pr[n % 2][:, 0:nk], flat(slot[s] % 2)[:, 0:nk], ACT.Exp, bias=ast[:, 0, n:n + 1],
                                 accum_out=ast[:, 1, n:n + 1]), free_of(s))

        exponentials(0)
        for n, (qb, h) in enumerate(steps):
            if n + 1 < len(steps):
                exponentials(n + 1)
            if n >= 2:
                act.wait_ge(att_pv, n - 1)
            for k, (lo, hi) in enumerate(quads(qb)):
                key = ("p", n, k)
                pt_filled(act, key)
                od.run(sc.activation(pr_t[n % 2][:, lo:hi, :], pt_of(key)[:, 0:(hi - lo) * P].rearrange(
                    "p (t q) -> p t q", q=P), ACT.Copy), ptf_of(key))
        def xbc_act(b):
            act.wait_ge(x_conv, b + 1)
            od.run(sc.activation(xc[:, b, 0:SEQ], x_cv[:, 0:SEQ], ACT.Silu))
            od.run(sc.activation(xc[:, b, SEQ:T].rearrange("p (s n) -> p s n", s=NB),
                                 x_new(x_cv), ACT.Silu), x_act)

        free_of_1b(act)
        for n in range(NB):
            job = jobs_c[n]
            evacuate(job, ACT.Silu if job[0] == "z" else ACT.Copy)
            if 1 <= n <= 6:
                xbc_act(n - 1)
            if n < NB:
                key = ("sk", n)
                pt_filled(act, key)
                if n >= 1:
                    pt_filled(act, ("ss", n - 1))
                od.run(sc.activation(kt_s[:, :, :], pt_of(key)[:, :].rearrange("p (k n) -> p k n", k=2), ACT.Copy),
                       ptf_of(key))
            if n < NB:
                act.wait_ge(ss_max, n + 1)
                if n >= 1:
                    pt_filled(act, ("sp", n - 1))
                od.run(sc.activation(p_s[:, :], pt_of(("ss", n))[0:NH * NQ, 0:PAST + NS], ACT.Exp,
                                     bias=ast[0:NH * NQ, 0, n:n + 1], accum_out=ast[0:NH * NQ, 1, n:n + 1]),
                       ptf_of(("ss", n)))
                key = ("sp", n)
                pt_filled(act, key)
                if n >= 1:
                    pt_filled(act, ("so", n - 1))
                od.run(sc.activation(pt_s[:, 0:2, :], pt_of(key)[:, 0:32].rearrange("p (k n) -> p k n", k=2), ACT.Copy))
                od.run(sc.activation(pt_s[0:NS, 2, :], pt_of(key)[0:NS, 32:48], ACT.Copy), ptf_of(key))
        free_of_sx(act)
        od.run(sc.activation(eacs[:, :, :], sdt_t[:, :, 64:64 + NH], ACT.Exp), eacs_done)
        for c in range(NT + 1):
            s = ("ssd", c)
            r = rows_of(c)
            n = c % 2
            key = ("xb", c)
            pt_filled(act, key)
            if c >= 2:
                act.wait_ge(ssd_back, c - 1)
                act.wait_ge(xte_done, c - 1)
            od.run(sc.activation(xb[n][0:r, :], pt_of(key)[0:r, :], ACT.Copy), ptf_of(key))
            slot_filled(act, s)
            act.wait_ge(seg_in, c + 1)
            bc = ps[slot[s] % 2][:, 1, :].rearrange("p (h t) -> p h t", h=NH)
            if c < NT:
                od.run(sc.activation(dec[n][:, 2, :], bc[:, :, P - 1], ACT.Exp))
            else:
                od.run(sc.activation(sdec[:, :, :], ps[slot[s] % 2][:, 1, 100:116].rearrange("p (g b) -> p g b", g=2),
                                     ACT.Exp), sdec_done)
            od.run(sc.activation(dec[n][0:r, 1, :], dec[n][0:r, 0, :], ACT.Exp), dec_exp)
            od.run(sc.activation(seg[n][0:r, :, 0:r], seg[n][0:r, :, 0:r], ACT.Exp), seg_exp)
        for b in range(NB):
            key = ("sh", b)
            pt_filled(act, key)
            if b >= 2:
                pt_filled(act, ("sn", b - 2))
            od.run(sc.activation(h0t[b % 2][:, :, :], pt_of(key)[:, 0:256].rearrange("p (g n) -> p g n", g=2), ACT.Copy),
                   ptf_of(key))
        act.wait_ge(y_gated, NT + 1)
        od.run(sc.activation(stat[:, 1, :], stat[:, 0, :], ACT.Sqrt, scale=1.0 / 256, bias=eps[:, :]), d_rms)
        free_of_s1(act)
        for b in range(KD):
            od.run(sc.activation(y_hi[:, b, :], y_all[:, b, :], ACT.Copy), y_hi_done)

        def gates(j):
            for q in range(4):
                act.wait_ge(gate_full, j * 4 + (q + 1))
                if q == 1:
                    act.wait_ge(br_read, j * 4 + 1)
                elif q >= 2:
                    act.wait_ge(merged_done, j * 3 + (q - 1))
                elif not isinstance(j, int):
                    act.wait_ge(merged_done, j * 3)
                od.run(sc.activation(in_chunks(sg[:, :]), chunked(0), ACT.Sigmoid), sg_ready)

        od.peel()
        gates(0)
        with act.Fori(1, KD) as j:
            od.enter(j, 1)
            gates(j)
        od.leave(KD - 1)
        act.wait_ge(gate_full, 4 * KD)
        for k in range(KD):
            act.wait_ge(merged_done, 3 * (k + 1))
            od.run(sc.activation(h_hi[:, k, :], merged[:, k, :], ACT.Copy), m_hi_done)

        def residual(i):
            for s in range(2):
                act.wait_ge(wo_full, i * 2 + (s + 1))
                x1_block = x1[:, bass.ds(i * 2 + s, 1), :].rearrange("p o n -> p (o n)")
                od.run(sc.activation(in_chunks(x1_block), chunked(s), ACT.Copy))
                if not isinstance(i, int) or s == 1:
                    act.wait_ge(ssq_done, i * 2 + s)
                od.run(sc.activation(in_chunks(sq[:, :]), chunked(s), ACT.Square), wo_read)

        od.peel()
        residual(0)
        with act.Fori(1, KD // 2) as i:
            od.enter(i, 1)
            residual(i)
        od.leave(KD // 2 - 1)
        for n in range(2):
            act.wait_ge(fh_full, n + 1)
            src = pt[n][:, 0:NFF * NB * FH].rearrange("p (b n) -> p b n", b=NFF)
            od.run(sc.activation(fh[:, n * NFF:(n + 1) * NFF, :], src, ACT.Copy), fh_done)
        act.wait_ge(nm_full, 1)
        od.run(sc.activation(in_chunks(rms[:, :]), chunked(0), ACT.Sqrt, scale=1.0 / D, bias=eps[:, :]), nm_rms)
        for k in range(KD):
            act.wait_ge(h2_ready, k + 1)
            od.run(sc.activation(h_hi[:, k, :], h2_f[k % 2][:, :], ACT.Copy), h2_hi_done)
        def param(col, e):
            return pv[:, bass.ds(e + col, 1)]

        def ffn_front(e, s, i, first):
            for k, blk in ffn_kinds(e):
                act.wait_ge(up_full, i * 4 + (2 * s + k + 1))
                if first:
                    act.wait_ge(f_zeroed, 1)
                else:
                    act.wait_ge(cv_taps, i * 4 + (2 * s + k - 1))
                x = ext[k]
                new = x[:, FH + SEQ:FE_W].rearrange("p (s n) -> p s n", s=NB)
                od.run(sc.activation(x[:, FH:FH + 2 * CH].rearrange("p (c n) -> p c n", c=2), ps[k][:, 0:2, 0:CH], ACT.Copy))
                od.run(sc.activation(x[:, FH + 2 * CH:FH + SEQ], ps[k][:, 2, 0:SEQ - 2 * CH], ACT.Copy))
                od.run(sc.activation(new[:, :, FH:FH + NQ], ps[k][:, 2, SEQ - 2 * CH:CH].rearrange("p (s n) -> p s n", s=NB),
                                     ACT.Copy), up_read)
                od.run(sc.activation(new[:, :, 0:FH], fh[:, bass.ds(blk, 1), :].rearrange("p o (s n) -> p (o s) n", s=NB),
                                     ACT.Copy))
                if not first:
                    act.wait_ge(act_split, i * 2 + s)
                od.run(sc.activation(cv[k][:, 0:FE_W - FH], x[:, 0:FE_W - FH], ACT.Identity, scale=param(PV_FW, blk),
                                     bias=param(PV_FB, blk)), cv0_done)
            act.wait_ge(cv_taps, i * 4 + (2 * s + 1))
            od.run(sc.activation(cv[0][:, 0:FE_W - FH], cv[0][:, 0:FE_W - FH], ACT.Silu), silu_done)

        def ffn_upper(s, i, downs):
            act.wait_ge(prod_done, i * 2 + (s + 1))
            if downs is not None:
                act.wait_ge(dn_full, downs)
            for n, (dst, src) in enumerate(zip(packed(act_hi[:, s, :]), spaced(cv[0]))):
                od.run(sc.activation(dst, src, ACT.Copy), act_hi_done if n == 1 else None)

        od.peel()
        for s in range(2):
            ffn_front(s, s, 0, s == 0)
            ffn_upper(s, 0, None)
        with act.Fori(1, NFF // 2) as i:
            od.enter(i, 1)
            for s in range(2):
                ffn_front(i * 2 + s, s, i, False)
                ffn_upper(s, i, i * 24)
        od.leave(NFF // 2 - 1)
        for n in range(4):
            act.wait_ge(out_full, n + 1)
            lo, hi = 12 * n * P, min(12 * (n + 1), 2 * NFF) * P
            od.run(sc.activation(hist_f[:, lo:hi], flat(n % 2)[0:9 * FH, 0:hi - lo], ACT.Copy), (out_free[n % 2], n // 2 + 1))
            act.wait_ge(out_free[n % 2], n // 2 + 1)
            od.run(sc.activation(mark[:, 1:2], eps[:, :], ACT.Copy), fs_ready)
        for t in range(NT + 1):
            r = rows_of(t)
            n = 4 + t
            act.wait_ge(out_full, n + 1)
            act.wait_ge(act_split, NFF)
            od.run(sc.activation(squares[0:r, :], flat(n % 2)[0:r, 0:D], ACT.Square, accum_out=stat7[0:r, 0, t:t + 1]))
            od.run(sc.activation(stat7[0:r, 1, t:t + 1], stat7[0:r, 0, t:t + 1], ACT.Sqrt, scale=1.0 / D, bias=eps[0:r, :]),
                   y_sq)

    @block.vector
    def _(dve):
        od = Order(dve, dve_own)
        v = nc.vector
        od.run(v.memset(eps[:, :], EPS), vec_done)
        pt_filled(dve, ("vec",))
        od.run(v.tensor_copy(pv[:, :], pt_of(("vec",))[:, 0:PV_N]), ptf_of(("vec",)))
        pt_filled(dve, ("hist",))
        od.run(v.tensor_copy(hist_t[:, :], pt_of(("hist",))[:, 0:384]), ptf_of(("hist",)))
        hist_x_t = hist_t[:, 0:144].rearrange("p (b n) -> p b n", b=6)
        hist_p_t = hist_t[:, 144:384].rearrange("p (b n) -> p b n", b=2)

        def h_parts(i):
            r = rows_of(i)
            s = ("x", i)
            slot_filled(dve, s)
            src = flat(slot[s] % 2)[:, 0:D].rearrange("p (k n) -> p k n", k=KD)[:, :, 0:r]
            od.run(v.tensor_tensor(h_f[i % 2][:, :, 0:r], src, pv[:, PV_G1:PV_G1 + KD].unsqueeze(2)
                                   .to_broadcast([P, KD, r]), ALU.mult), free_of(s))
            dve.wait_ge(h_hi_done, i + 1)
            tok = slice(i * P, i * P + r)
            od.run(v.tensor_tensor(h_lo[:, :, tok], h_f[i % 2][:, :, 0:r], h_hi[:, :, tok].bitcast(F32),
                                   ALU.subtract), h_split)

        for i in range(NT + 1):
            r = rows_of(i)
            dve.wait_ge(x_sq, i + 1)
            od.run(v.reciprocal(stat[0:r, 2, i:i + 1], stat[0:r, 1, i:i + 1]))
            od.run(v.tensor_scalar(x_scaled[i % 2][0:r, :], x_tok[i % 3][0:r, :], stat[0:r, 2, i:i + 1], None,
                                   ALU.mult), x_normed)
            if i >= 1:
                h_parts(i - 1)
        h_parts(NT)

        s = ("fdt", 0)
        raw = stg[0]
        slot_drained(dve, s)
        od.run(v.scalar_tensor_tensor(dk[0][0:36, :], raw[0:36, :], -1.0, raw[0:36, :], ALU.mult, ALU.max), dk_abs)
        dve.wait_ge(dk_exp, 1)
        od.run(v.tensor_scalar(dk[2][0:36, :], dk[1][0:36, :], 1.0, None, ALU.add), dk_u)
        od.run(v.tensor_scalar(dk[3][0:36, :], dk[2][0:36, :], 1.0, None, ALU.subtract))
        od.run(v.tensor_tensor(dk[3][0:36, :], dk[1][0:36, :], dk[3][0:36, :], ALU.subtract))
        dve.wait_ge(dk_ln, 1)
        od.run(v.reciprocal(dk[2][0:36, :], dk[2][0:36, :]))
        od.run(v.tensor_tensor(dk[3][0:36, :], dk[3][0:36, :], dk[2][0:36, :], ALU.mult))
        od.run(v.tensor_tensor(dk[3][0:36, :], dk[3][0:36, :], dk[0][0:36, :], ALU.add))
        od.run(v.scalar_tensor_tensor(sdt[0:NH, :], raw[0:NH, :], 0.0, dk[3][0:NH, :], ALU.min, ALU.subtract))
        dtr = slice(32, 32 + NH)
        od.run(v.scalar_tensor_tensor(sdt[dtr, :], raw[dtr, :], 0.0, dk[3][dtr, :], ALU.max, ALU.add), stg_free)
        dve.wait_ge(alog_exp, 1)
        od.run(v.tensor_scalar(small[dtr, 3:4], small[dtr, 2:3], -1.0, None, ALU.mult))
        od.run(v.tensor_scalar(dk[0][dtr, :], sdt[dtr, :], small[dtr, 3:4], None, ALU.mult))
        od.run(v.memset(dk[1][dtr, :], 1.0))
        od.run(v.memset(dk[1][dtr, 0:SEQ].rearrange("p (c t) -> p c t", t=P)[:, :, 0:1], 0.0))
        od.run(v.memset(dk[1][dtr, SEQ:T].rearrange("p (c t) -> p c t", t=NQ)[:, :, 0:1], 0.0))
        od.run(v.tensor_tensor_scan(sdt[64:64 + NH, :], dk[1][dtr, :], dk[0][dtr, :], 0.0, ALU.mult, ALU.add))
        od.run(v.memset(dk[2][0:NH, 0:SEQ], 1.0))
        od.run(v.tensor_tensor_scan(sdt[96:96 + NH, 0:SEQ], dk[2][0:NH, 0:SEQ], sdt[0:NH, 0:SEQ], 0.0,
                                    ALU.mult, ALU.add), sdt_done)
        dve.wait_ge(a_zeroed, 1)
        for b in range(2):
            n = ring[("pool", b)]
            slot_drained(dve, ("pool", b))
            od.run(v.tensor_copy(p_ext[:, b, PH:PH + SEQ], stg[n % 2][:, 0:SEQ]))
            od.run(v.tensor_copy(p_ext[:, b, PH + SEQ:PE_W].rearrange("p (s n) -> p s n", s=NB)[:, :, PH:PH + NQ],
                                 stg[n % 2][:, SEQ:T].rearrange("p (s n) -> p s n", s=NB)), stg_free)
            od.run(v.tensor_copy(p_ext[:, b, PH + SEQ:PE_W].rearrange("p (s n) -> p s n", s=NB)[:, :, 0:PH],
                                 hist_p_t[:, b, :].rearrange("p (s n) -> p s n", s=NB)))
        for b in range(2):
            src = p_ext[:, b, SEQ:SEQ + 9 * (PH + NQ)].rearrange("p (s n) -> p s n", s=9)[:, :, 0:PH]
            od.run(v.tensor_copy(p_state[:, b, :].rearrange("p (s n) -> p s n", s=9), src), pstate_in)
        for n, (lo, hi) in enumerate(((0, 5), (5, 9))):
            pt_filled(dve, ("sdt", n))
            src = pt_of(("sdt", n))[:, 0:500].rearrange("p (t c) -> p t c", c=100)
            if n == 0:
                od.run(v.tensor_copy(sdt_t[:, 0:5, :], src), ptf_of(("sdt", n)))
            else:
                od.run(v.tensor_copy(sdt_t[:, 5:8, :], src[:, 0:3, :]))
                od.run(v.tensor_copy(sdt_t[0:NS, 8, :], src[0:NS, 3, :]), ptf_of(("sdt", n)))
        od.run(v.tensor_tensor(win_a[:, :, 1:PE_W], p_ext[:, :, 1:PE_W], p_ext[:, :, 0:PE_W - 1], ALU.add))
        od.run(v.tensor_tensor(win_b[:, :, 3:PE_W], win_a[:, :, 3:PE_W], win_a[:, :, 1:PE_W - 2], ALU.add))

        def pooled(blk, half, win, src):
            r = slice(64 * half, 64 * half + 64)
            fix = const("pfix", r).rearrange("p (b n) -> p b n", b=2)[:, blk, :]
            od.run(v.tensor_tensor(src[r, blk, PH:2 * PH], src[r, blk, PH:2 * PH], fix, ALU.mult))
            return v.scalar_tensor_tensor(p_ext[r, blk, PH:PE_W], src[r, blk, PH:PE_W], 1.0 / win,
                                          p_ext[r, blk, PH:PE_W], ALU.mult, ALU.subtract)

        dve.wait_ge(pstate_in, 2)
        od.run(pooled(0, 0, WINDOWS[0], win_a))
        od.run(pooled(0, 1, WINDOWS[1], win_b))
        od.run(v.tensor_tensor(win_a[:, 1, 7:PE_W], win_b[:, 1, 7:PE_W], win_b[:, 1, 3:PE_W - 4], ALU.add))
        od.run(v.tensor_tensor(win_b[:, 1, 15:PE_W], win_a[:, 1, 15:PE_W], win_a[:, 1, 7:PE_W - 8], ALU.add))
        od.run(pooled(1, 0, WINDOWS[2], win_a))
        od.run(pooled(1, 1, WINDOWS[3], win_b), pd_done)
        for b in range(2):
            for n, (lo, hi) in enumerate(THIRDS):
                key = ("va", b, n)
                pt_filled(dve, key)
                src = pt_of(key)[:, :].rearrange("p (t c) -> p t c", c=P)
                r = P if hi <= NT else NS
                od.run(v.tensor_copy(va[0:r, lo:hi, b * P:(b + 1) * P], src[0:r, 0:hi - lo, :]), ptf_of(key))
            od.run(v.memset(stat[:, 3, 0:1], 0.0), stg_free)
        for t in range(NT + 1):
            ins = v.tensor_tensor_reduce(out=pjunk, in0=va[:, t, :], in1=va[:, t, :], scale=1.0, scalar=0.0,
                                         op0=ALU.mult, op1=ALU.add, accum_out=stat[:, 0, t:t + 1])
            od.run(ins, a_sum if t == NT else None)
        pt_filled(dve, ("ws",))
        od.run(v.tensor_tensor(wst, pt_of(("ws",))[:, :].rearrange("p (g t) -> p g t", g=4),
                               const("tri01").unsqueeze(1).to_broadcast([P, 4, P]), ALU.mult), ptf_of(("ws",)))
        pt_filled(dve, ("wsm",))
        od.run(v.tensor_tensor(wsm, pt_of(("wsm",))[0:NS, 0:4 * NS].rearrange("p (g t) -> p g t", g=4),
                               const("blk01", slice(0, NS)).unsqueeze(1).to_broadcast([NS, 4, NS]), ALU.mult),
               ptf_of(("wsm",)))
        dve.wait_ge(a_rms, 1)
        od.run(v.reciprocal(stat[:, 2, :], stat[:, 1, :]))
        for t in range(NT + 1):
            od.run(v.scalar_tensor_tensor(va[:, t, :], va[:, t, :], stat[:, 2, t:t + 1], cmg, ALU.mult, ALU.mult),
                   va_done if t == NT else None)
        for n in range(2):
            pt_filled(dve, ("pstate", n))
            k = (5 - n) * PH
            od.run(v.tensor_copy(p_out[0:k, n, :], pt_of(("pstate", n))[0:k, 0:2 * P]), ptf_of(("pstate", n)))
            od.run(v.memset(stat[:, 3, 0:1], 0.0), pstate_out)
        for b in range(2):
            s = ("mixa", b)
            slot_filled(dve, s)
            od.run(v.tensor_tensor(y_all[:, b, 0:SEQ], flat(slot[s] % 2)[:, 0:SEQ], u_f[:, b, 0:SEQ], ALU.mult))
            od.run(v.tensor_tensor(y_all[:, b, SEQ:T], flat(slot[s] % 2)[:, SEQ:T], u_f[:, b, SEQ:T], ALU.mult),
                   free_of(s))
        free_of_1a(dve)
        od.run(v.tensor_copy(ident_r[:, :], ident))
        od.run(v.tensor_copy(attneg_r[:, :], const("attneg")))
        for b in range(2):
            n = ring[("q", b)]
            slot_drained(dve, ("q", b))
            for half in range(2):
                r = slice(64 * half, 64 * half + 64)
                od.run(v.tensor_copy(q_a[0:HD, 2 * b + half, :], stg[n % 2][r, 0:SEQ]))
            od.run(v.tensor_copy(qs_new[:, b, :], stg[n % 2][:, SEQ:T]), stg_free)
        for b in range(2):
            n = ring[("k", b)]
            slot_drained(dve, ("k", b))
            for half in range(2):
                r = slice(64 * half, 64 * half + 64)
                od.run(v.tensor_copy(k_a[0:HD, 2 * b + half, :], stg[n % 2][r, 0:SEQ]))
            od.run(v.tensor_copy(ks_new[:, b, :], stg[n % 2][:, SEQ:T]), qk_ready)
            for m, (lo, hi) in enumerate(THIRDS):
                key = ("k", b, m)
                j = 3 * b + m
                pt_filled(dve, key)
                if j >= 2:
                    dve.wait_ge(k_sent[j % 2], 16 * (j // 2))
                r = P if hi <= NT else NS
                src = pt_of(key)[:, :].rearrange("p (t c) -> p t c", c=P)
                od.run(v.tensor_copy(k_out[j % 2][0:r, 0:hi - lo, :], src[0:r, 0:hi - lo, :]), ptf_of(key))
                od.run(v.memset(stat[:, 3, 0:1], 0.0), k_ready)
            od.run(v.memset(stat[:, 3, 0:1], 0.0), stg_free)

        def turned(kind, b, dst):
            for m, (lo, hi) in enumerate(THIRDS):
                key = (kind, b, m)
                pt_filled(dve, key)
                r = P if hi <= NT else NS
                src = pt_of(key)[:, :].rearrange("p (t c) -> p t c", c=P)
                od.run(v.tensor_copy(dst[0:r, lo:hi, b * P:(b + 1) * P], src[0:r, 0:hi - lo, :]), ptf_of(key))

        turned("v", 0, v_tok)
        od.run(v.memset(stat[:, 3, 0:1], 0.0), stg_free)
        turned("v", 1, v_tok)
        od.run(v.memset(stat[:, 3, 0:1], 0.0), stg_free)
        od.run(v.tensor_copy(vs_new[:, :], v_tok[0:NS, NT, :]), v_done)

        def att_maximum(n):
            qb, h = steps[n]
            s = ("att", qb, h)
            slot_filled(dve, s)
            od.run(v.reduce_max(ast[:, 2, n:n + 1], flat(slot[s] % 2)[:, 0:(qb + 1) * P], AX.X))
            od.run(v.tensor_scalar(ast[:, 0, n:n + 1], ast[:, 2, n:n + 1], -1.0, None, ALU.mult), att_max)

        def normalize(n):
            nk = (steps[n][0] + 1) * P
            slot_drained(dve, ("att",) + steps[n])
            od.run(v.reciprocal(ast[:, 2, n:n + 1], ast[:, 1, n:n + 1]))
            od.run(v.tensor_scalar(pr[n % 2][:, 0:nk], pr[n % 2][:, 0:nk], ast[:, 2, n:n + 1], None, ALU.mult), att_norm)

        def att_output(n):
            qb, h = steps[n]
            r = slice(64 * (h % 2), 64 * (h % 2) + 64)
            dve.wait_ge(att_pv, n + 1)
            od.run(v.tensor_copy(y_all[r, 4 + h // 2, qb * P:(qb + 1) * P], ps[slot[("att", qb, h)] % 2][r, 2, 0:P]), att_out)

        att_maximum(0)
        for n in range(len(steps)):
            normalize(n)
            if n + 1 < len(steps):
                att_maximum(n + 1)
            if n >= 1:
                att_output(n - 1)
        att_output(len(steps) - 1)
        free_of_1b(dve)
        od.run(v.tensor_tensor(lf_new[:, :].rearrange("p (b h) -> p b h", b=NB),
                               sdt_t[0:NS, NT, 0:NH].unsqueeze(1).to_broadcast([NS, NB, NH]),
                               const("bmask", slice(0, NS)).rearrange("p (b h) -> p b h", b=NB), ALU.mult), clog_in)
        dve.wait_ge(c_zeroed, 1)
        for h in range(NH):
            r = slice(64 * (h % 2), 64 * (h % 2) + 64)
            od.run(v.tensor_copy(q_s[r, h // 2, :, h * NQ:(h + 1) * NQ],
                                 qs_new[r, h // 2, :].rearrange("p (b q) -> p b q", b=NB)), sx_ready)
        key = ("clog",)
        pt_filled(dve, key)
        od.run(v.tensor_tensor_scan(c_s[:, :], const("ones", slice(0, NS)).to_broadcast([NS, PAST + NQ]),
                                    pt_of(key)[0:NS, 0:PAST + NQ], 0.0, ALU.mult, ALU.add), ptf_of(key))
        od.run(v.tensor_scalar(nc_s[:, 0:PAST], c_s[:, 0:PAST], -1.0, None, ALU.mult))
        od.run(v.tensor_scalar(nc_s[:, PAST:PAST + NS].rearrange("p (b q) -> p b q", b=NB),
                               c_s[:, PAST:PAST + NQ].unsqueeze(1).to_broadcast([NS, NB, NQ]), -1.0, None, ALU.mult))
        od.run(v.tensor_tensor(cq_s[:, :].rearrange("p (r q) -> p r q", q=NQ),
                               const("expand", slice(0, NS)).rearrange("p (r q) -> p r q", q=NQ),
                               c_s[:, PAST:PAST + NQ].unsqueeze(1).to_broadcast([NS, NS, NQ]), ALU.mult), clog_done)

        def sample_out(n):
            key = ("so", n)
            pt_filled(dve, key)
            for h in range(NH):
                r = slice(64 * (h % 2), 64 * (h % 2) + 64)
                col = (h // 2) * NH * NQ + h * NQ
                od.run(v.tensor_copy(y_all[r, 4 + h // 2, SEQ + n * NQ:SEQ + (n + 1) * NQ], pt_of(key)[r, col:col + NQ]),
                       ptf_of(key) if h == NH - 1 else None)

        def convolve(b):
            n = ring[("xbc", b)]
            slot_drained(dve, ("xbc", b))
            od.run(v.tensor_copy(x_ext[:, CV:CV + SEQ], stg[n % 2][:, 0:SEQ]))
            tail = x_ext[:, CV + SEQ:XE_W].rearrange("p (s n) -> p s n", s=NB)
            od.run(v.tensor_copy(tail[:, :, CV:CV + NQ], stg[n % 2][:, SEQ:T].rearrange("p (s n) -> p s n", s=NB)), stg_free)
            od.run(v.tensor_copy(tail[:, :, 0:CV], hist_x_t[:, b, :].rearrange("p (s n) -> p s n", s=NB)))
            last = x_ext[:, SEQ:SEQ + 9 * (CV + NQ)].rearrange("p (s n) -> p s n", s=9)[:, :, 0:CV]
            od.run(v.tensor_copy(xstate[:, b, :].rearrange("p (s n) -> p s n", s=9), last), xstate_in)
            if b >= 1:
                dve.wait_ge(x_act, b)
            w = XE_W - CV

            def tap(j):
                return pv[:, PV_CW + 6 * j + b:PV_CW + 6 * j + b + 1]

            od.run(v.tensor_scalar(x_cv[:, 0:w], x_ext[:, 0:w], tap(0), pv[:, PV_CB + b:PV_CB + b + 1],
                                   ALU.mult, ALU.add))
            for j in range(1, CV + 1):
                od.run(v.scalar_tensor_tensor(x_cv[:, 0:w], x_ext[:, j:j + w], tap(j), x_cv[:, 0:w], ALU.mult, ALU.add),
                       x_conv if j == CV else None)

        for n in range(NB):
            if n < 6:
                convolve(n)
            if n >= 1:
                sample_out(n - 1)
            if n < NB:
                key = ("ss", n)
                pt_filled(dve, key)
                rs = slice(0, NH * NQ)
                od.run(v.reduce_max(ast[rs, 2, n:n + 1], pt_of(key)[rs, 0:PAST + NS], AX.X))
                od.run(v.tensor_scalar(ast[rs, 0, n:n + 1], ast[rs, 2, n:n + 1], -1.0, None, ALU.mult), ss_max)
                pt_drained(dve, key)
                od.run(v.reciprocal(ast[rs, 2, n:n + 1], ast[rs, 1, n:n + 1]))
                od.run(v.tensor_scalar(p_s[:, :], p_s[:, :], ast[rs, 2, n:n + 1], None, ALU.mult), ss_done)
            if n == NB - 1:
                turned("z", 0, zt)
                od.run(v.memset(stat[:, 3, 0:1], 0.0), stg_free)
        sample_out(NB - 1)
        turned("z", 1, zt)
        od.run(v.memset(stat[:, 3, 0:1], 0.0), stg_free)
        for n, (lo, hi) in enumerate(((0, 4), (4, 6))):
            key = ("xst", n)
            pt_filled(dve, key)
            od.run(v.tensor_copy(xst_out[:, lo * P:hi * P], pt_of(key)[0:9 * CV, 0:(hi - lo) * P]), ptf_of(key))
            od.run(v.memset(stat[:, 3, 0:1], 0.0), xst_ready)

        free_of_sx(dve)

        def decays(c):
            s = ("ssd", c)
            r = rows_of(c)
            n = c % 2
            slot_filled(dve, s)
            if c >= 2:
                dve.wait_ge(ssd_back, c - 1)
            bc = ps[slot[s] % 2][:, 1, :].rearrange("p (h t) -> p h t", h=NH)
            mask = const("ssdneg") if c < NT else const("blkneg", slice(0, NS))
            own = sdt_t[0:r, c, 64:64 + NH]
            last = bc[:, :, P - 1] if c < NT else ps[slot[s] % 2][0:NS, 0, 256:260]
            od.run(v.tensor_tensor(dec[n][0:r, 0, :], last, own, ALU.subtract))
            for h in range(NH):
                od.run(v.scalar_tensor_tensor(seg[n][0:r, h, 0:r], bc[0:r, h, 0:r], own[:, h:h + 1], mask,
                                              ALU.subtract, ALU.min), seg_in if h == NH - 1 else None)

        def new_state(b):
            key = ("sn", b)
            pt_filled(dve, key)
            dve.wait_ge(sdec_done, 1)
            if b >= 2:
                dve.wait_ge(h_sent[b % 2], 16 * (b // 2))
            for g in range(2):
                od.run(v.scalar_tensor_tensor(h_out[b % 2][:, g, :], h0[b % 2][:, g, :], sdec[:, g, b:b + 1],
                                              pt_of(key)[:, g * P:(g + 1) * P], ALU.mult, ALU.add),
                       ptf_of(key) if g == 1 else None)
            od.run(v.memset(stat[:, 3, 0:1], 0.0), h_ready)

        decays(0)
        for c in range(NT + 1):
            s = ("ssd", c)
            r = rows_of(c)
            n = c % 2
            dst = ps[slot[s] % 2]
            dve.wait_ge(seg_exp, c + 1)
            cb = dst[0:r, 0, 0:256].rearrange("p (g t) -> p g t", g=2)[:, :, 0:r].unsqueeze(2).to_broadcast([r, 2, 2, r])
            decay = seg[n][0:r, :, 0:r].rearrange("p (g h) t -> p g h t", g=2)
            od.run(v.tensor_tensor(decay, decay, cb, ALU.mult), seg_cb)
            if c + 1 <= NT:
                decays(c + 1)
            dve.wait_ge(ssd_back, c + 1)
            y_off, y_diag = (dst[0:r, 2, 256 * k:256 * k + 256].rearrange("p (h d) -> p h d", h=NH) for k in range(2))
            if c < NT:
                od.run(v.tensor_tensor(hst[:, :, :], hst[:, :, :], dec[n][:, 2, :].unsqueeze(2)
                                       .to_broadcast([P, NH, HD]), ALU.mult))
                od.run(v.tensor_tensor(hst[:, :, :], hst[:, :, :], dst[:, 0, 256:512].rearrange(
                    "p (h d) -> p h d", h=NH), ALU.add), h_next)
            dve.wait_ge(xd_done, c + 1)
            dve.wait_ge(eacs_done, 1)
            od.run(v.tensor_tensor(xd[n][0:r], xd[n][0:r], y_diag, ALU.add))
            od.run(v.tensor_tensor(yoff[0:r], y_off, eacs[0:r, c, :].unsqueeze(2).to_broadcast([r, NH, HD]), ALU.mult),
                   free_of(s))
            od.run(v.tensor_tensor(xd[n][0:r], xd[n][0:r], yoff[0:r], ALU.add))
            gated = zt[0:r, c, :].rearrange("p (h d) -> p h d", h=NH)
            od.run(v.tensor_tensor(gated, gated, xd[n][0:r], ALU.mult))
            od.run(v.tensor_tensor_reduce(out=yoff[0:r].rearrange("p h d -> p (h d)"), in0=zt[0:r, c, :], in1=zt[0:r, c, :],
                                          scale=1.0, scalar=0.0, op0=ALU.mult, op1=ALU.add,
                                          accum_out=stat[0:r, 0, c:c + 1]), y_gated)
            if c == NT - 1:
                dve.wait_ge(d_zeroed, 1)
                for g in range(2):
                    for b in range(NB):
                        od.run(v.tensor_copy(ctm[:, g, b, b * NQ:(b + 1) * NQ], xc[:, 4 + g, SEQ + b * NQ:SEQ + (b + 1) * NQ]),
                               ctm_done)
                for b in range(NB):
                    new_state(b)
        key = ("hp",)
        pt_filled(dve, key)
        dve.wait_ge(h_sent[0], 16 * 4)
        od.run(v.tensor_copy(h_out[0], pt_of(key)[:, 0:256].rearrange("p (g k) -> p g k", g=2)), ptf_of(key))
        od.run(v.memset(stat[:, 3, 0:1], 0.0), h_ready)
        dve.wait_ge(d_rms, 1)
        od.run(v.reciprocal(stat[:, 2, :], stat[:, 1, :]))
        for t in range(NT + 1):
            r = rows_of(t)
            od.run(v.tensor_scalar(zt[0:r, t, :], zt[0:r, t, :], stat[0:r, 2, t:t + 1], None, ALU.mult), yd_ready)
        for t in range(NT + 1):
            r = rows_of(t)
            key = ("yd", t)
            pt_filled(dve, key)
            od.run(v.tensor_tensor(y_all[:, 6:8, t * P:t * P + r],
                                   pt_of(key)[:, 0:256].rearrange("p (b t) -> p b t", b=2)[:, :, 0:r],
                                   pv[:, PV_SG:PV_SG + 2].unsqueeze(2).to_broadcast([P, 2, r]), ALU.mult), ptf_of(key))
        for b in range(KD):
            dve.wait_ge(y_hi_done, b + 1)
            od.run(v.tensor_tensor(y_lo[:, b, :], y_all[:, b, :], y_hi[:, b, :].bitcast(F32), ALU.subtract), y_split)

        def merge(j):
            for q in range(4):
                dst = merged[:, bass.ds(j, 1), :].rearrange("p o n -> p (o n)")
                dve.wait_ge(br_full, j * 4 + (q + 1))
                dve.wait_ge(sg_ready, j * 4 + (q + 1))
                out = dst if q == 0 else sg[:, :]
                od.run(v.tensor_tensor(in_chunks(out), in_chunks(sg[:, :]), chunked(1), ALU.mult), br_read)
                if q > 0:
                    od.run(v.tensor_tensor(dst, dst, sg[:, :], ALU.add), merged_done)

        od.peel()
        merge(0)
        with dve.Fori(1, KD) as j:
            od.enter(j, 1)
            merge(j)
        od.leave(KD - 1)
        for k in range(KD):
            dve.wait_ge(m_hi_done, k + 1)
            od.run(v.tensor_tensor(h_lo[:, k, :], merged[:, k, :], h_hi[:, k, :].bitcast(F32), ALU.subtract), m_split)

        def sum_squares(i):
            for s in range(2):
                dve.wait_ge(wo_read, i * 2 + (s + 1))
                if isinstance(i, int) and s == 0:
                    od.run(v.tensor_copy(ssq[:, :], sq[:, :]), ssq_done)
                else:
                    od.run(v.tensor_tensor(ssq[:, :], ssq[:, :], sq[:, :], ALU.add), ssq_done)

        od.peel()
        sum_squares(0)
        with dve.Fori(1, KD // 2) as i:
            od.enter(i, 1)
            sum_squares(i)
        od.leave(KD // 2 - 1)
        dve.wait_ge(nm_rms, 1)
        od.run(v.reciprocal(rms[:, :], rms[:, :]))

        def h2_lower(k):
            dve.wait_ge(h2_hi_done, k + 1)
            od.run(v.tensor_tensor(h_lo[:, k, :], h2_f[k % 2][:, :], h_hi[:, k, :].bitcast(F32), ALU.subtract), h2_split)

        for k in range(KD):
            od.run(v.scalar_tensor_tensor(h2_f[k % 2][:, :], x1[:, k, :], pv[:, PV_G2 + k:PV_G2 + k + 1], rms[:, :],
                                          ALU.mult, ALU.mult), h2_ready)
            if k >= 1:
                h2_lower(k - 1)
        h2_lower(KD - 1)
        def ffn_conv(e, s, i, k):
            blk = ffn_kinds(e)[k][1]
            dve.wait_ge(cv0_done, i * 4 + (2 * s + k + 1))
            x, w = ext[k], FE_W - FH
            last = x[:, SEQ:SEQ + 9 * (FH + NQ)].rearrange("p (s n) -> p s n", s=9)[:, :, 0:FH]
            od.run(v.tensor_copy(fstate[:, bass.ds(blk, 1), :].rearrange("p o (s n) -> p (o s) n", s=9), last))
            for j in range(1, FH + 1):
                od.run(v.scalar_tensor_tensor(cv[k][:, 0:w], x[:, j:j + w], pv[:, bass.ds(blk + (PV_FW + 2 * NFF * j), 1)],
                                              cv[k][:, 0:w], ALU.mult, ALU.add), cv_taps if j == FH else None)

        def ffn_product(s, i):
            w = FE_W - FH
            dve.wait_ge(silu_done, i * 2 + (s + 1))
            od.run(v.tensor_tensor(cv[0][:, 0:w], cv[0][:, 0:w], cv[1][:, 0:w], ALU.mult), prod_done)

        def ffn_lower(s, i):
            dve.wait_ge(act_hi_done, i * 2 + (s + 1))
            for n, (dst, src, hi) in enumerate(zip(packed(act_lo[:, s, :]), spaced(cv[0]),
                                                   packed(act_hi[:, s, :].bitcast(F32)))):
                od.run(v.tensor_tensor(dst, src, hi, ALU.subtract), act_split if n == 1 else None)

        def ffn_sums(base):
            for n, (m, c) in enumerate(down_sets()):
                dve.wait_ge(dn_full, base + (n + 1))
                dst = x1[:, m, c * CH:(c + 1) * CH]
                od.run(v.tensor_tensor(dst, dst, pt[n % 2][:, 0:CH], ALU.add), dn_done)

        od.peel()
        for s in range(2):
            ffn_conv(s, s, 0, 0)
            ffn_conv(s, s, 0, 1)
            ffn_product(s, 0)
            ffn_lower(s, 0)
        with dve.Fori(1, NFF // 2) as i:
            od.enter(i, 1, [(dn_done, 24)])
            ffn_conv(i * 2, 0, i, 0)
            ffn_sums((i - 1) * 24)
            ffn_conv(i * 2, 0, i, 1)
            ffn_product(0, i)
            ffn_lower(0, i)
            ffn_conv(i * 2 + 1, 1, i, 0)
            ffn_conv(i * 2 + 1, 1, i, 1)
            ffn_product(1, i)
            ffn_lower(1, i)
        od.leave(NFF // 2 - 1)
        ffn_sums(24 * (NFF // 2 - 1))
        dve.wait_ge(ld_gfin, 16)
        dve.wait_ge(w_split, W6 + 6 * (NFF // 2))
        for t in range(NT + 1):
            r = rows_of(t)
            n = 4 + t
            dve.wait_ge(y_sq, t + 1)
            od.run(v.reciprocal(stat7[0:r, 2, t:t + 1], stat7[0:r, 1, t:t + 1]))
            if t >= 3:
                dve.wait_ge(y_sent[t % 3], 16 * (t // 3))
            od.run(v.scalar_tensor_tensor(y_out[t % 3][0:r, :], flat(n % 2)[0:r, 0:D], stat7[0:r, 2, t:t + 1], gfin[0:r, :],
                                          ALU.mult, ALU.mult), (out_free[n % 2], n // 2 + 1))
            od.run(v.memset(mark[:, 2:3], 0.0), y_ready)

    @block.tensor
    def _(pe):
        mm, tr = nc.tensor.matmul, nc.tensor.transpose

        def product(dst, n, between=None):
            for k in range(KD):
                for piece in (between or {}).get(k, ()):
                    piece()
                for c in range(3):
                    tok = slice(c * CH, (c + 1) * CH)
                    mm(dst[:, c, 0:CH], f_hi[n][:, k, :], h_hi[:, k, tok], start=k == 0, stop=False)
                for c in range(3):
                    tok = slice(c * CH, (c + 1) * CH)
                    mm(dst[:, c, 0:CH], f_hi[n][:, k, :], h_lo[:, k, tok], start=False, stop=False)
                for c in range(3):
                    tok = slice(c * CH, (c + 1) * CH)
                    last = mm(dst[:, c, 0:CH], f_lo[n][:, k, :], h_hi[:, k, tok], start=False, stop=k == KD - 1)
            return last

        def project(n, between=None):
            s = JOBS[n][:2]
            pe.wait_ge(w_split, n + 1)
            slot_open(pe, s)
            product(ps[slot[s] % 2], n % 2, between).then_inc(slot_full, 1)

        def turn(src, keys, block_rows=P):
            for key, (lo, hi) in zip(keys, THIRDS):
                pt_open(pe, key)
                for t in range(lo, hi):
                    r = rows_of(t)
                    last = tr(pt_of(key)[0:r, (t - lo) * P:(t - lo) * P + block_rows],
                              src[:, t * P:t * P + r], ident[0:block_rows, 0:block_rows])
                last.then_inc(pt_full, 1)

        pe.wait_ge(ld_const, 16)
        pe.wait_ge(ld_vec, 16 * 9)
        dst = pt_of(("vec",))
        tr(dst[:, 0:94], vec1[:, :], ident[0:94, 0:94])
        tr(dst[:, 94:182], vec2[:, :], ident[0:88, 0:88])
        tr(dst[:, 182:226], vec3[:, :], ident[0:44, 0:44]).then_inc(pt_full, 1)
        pe.wait_ge(ld_hist, 32)
        dst = pt_of(("hist",))
        for b in range(6):
            tr(dst[:, 24 * b:24 * b + 24], hist_x[:, b * P:(b + 1) * P], ident[0:24, 0:24])
        for b in range(2):
            last = tr(dst[:, 144 + 120 * b:264 + 120 * b], hist_p[:, b * P:(b + 1) * P], ident[0:120, 0:120])
        last.then_inc(pt_full, 1)
        for i in range(NT + 1):
            r = rows_of(i)
            s = ("x", i)
            pe.wait_ge(x_normed, i + 1)
            slot_open(pe, s)
            for k in range(KD):
                last = tr(flat(slot[s] % 2)[:, k * P:k * P + r], x_scaled[i % 2][0:r, k * P:(k + 1) * P],
                          ident[0:r, 0:r])
            last.then_inc(slot_full, 1)
        pe.wait_ge(h_split, NT + 1)
        project(0)
        project(1)
        project(2)
        project(3)
        pe.wait_ge(sdt_done, 1)
        for n, (lo, hi) in enumerate(((0, 5), (5, 9))):
            key = ("sdt", n)
            pt_open(pe, key)
            for t in range(lo, hi):
                r = rows_of(t)
                last = tr(pt_of(key)[0:r, (t - lo) * 100:(t - lo) * 100 + 100], sdt[0:100, t * P:t * P + r],
                          ident[0:100, 0:100])
            last.then_inc(pt_full, 1)
        project(4)
        slot_drained(pe, ("va", 0))
        turn(stg[ring[("va", 0)] % 2], [("va", 0, n) for n in range(3)])
        project(5)
        slot_drained(pe, ("va", 1))
        turn(stg[ring[("va", 1)] % 2], [("va", 1, n) for n in range(3)])
        project(6)
        pe.wait_ge(ld_ws, 32)
        key = ("ws",)
        pt_open(pe, key)
        for g in range(4):
            last = tr(pt_of(key)[:, g * P:(g + 1) * P], ws[:, g, :], ident)
        last.then_inc(pt_full, 1)
        pt_drained(pe, key)
        key = ("wsm",)
        pt_open(pe, key)
        for g in range(4):
            last = mm(pt_of(key)[0:NS, g * NS:(g + 1) * NS], const("rep4", slice(0, NQ)),
                      wst[0:NQ, g, 0:NQ].unsqueeze(1).to_broadcast([NQ, NB, NQ]), start=True, stop=True)
        last.then_inc(pt_full, 1)
        pe.wait_ge(pstate_in, 2)
        for n in range(2):
            key = ("pstate", n)
            pt_open(pe, key)
            for b in range(2):
                lo, k = n * 5 * PH, (5 - n) * PH
                last = tr(pt_of(key)[0:k, b * P:(b + 1) * P], p_state[:, b, lo:lo + k], ident)
            last.then_inc(pt_full, 1)
        pe.wait_ge(ld_pw, 80)
        pe.wait_ge(pd_done, 1)
        for b in range(2):
            s = ("mixb", b)
            slot_open(pe, s)
            dst = ps[slot[s] % 2]
            for c in range(3):
                n = CH if c < 2 else SEQ - 2 * CH
                mm(dst[:, c, 0:n], pw[:, b, :], p_ext[:, b, PH + c * CH:PH + c * CH + n], start=True, stop=True)
            new = p_ext[:, b, PH + SEQ:PE_W].rearrange("p (s n) -> p s n", s=NB)[:, :, PH:PH + NQ]
            mm(dst[:, 2, CH - NS:CH], pw[:, b, :], new, start=True, stop=True).then_inc(slot_full, 1)
        pt_drained(pe, ("wsm",))
        pe.wait_ge(va_done, 1)
        for b in range(2):
            s = ("mixa", b)
            slot_open(pe, s)
            dst = ps[slot[s] % 2]
            sel = const("gsel", slice(0, 4)).rearrange("p (b n) -> p b n", b=2)[:, b, :]
            for c in range(2):
                mm(dst[:, c, :], sel, cmb[:, :].unsqueeze(1).to_broadcast([4, 4, P]), start=True, stop=False,
                   skip_group_check=True)
            mm(dst[:, 2, 0:NS], sel, cmb[:, 0:NQ].unsqueeze(1).to_broadcast([4, NB, NQ]), start=True, stop=False,
               skip_group_check=True)
            for half in range(2):
                g = 2 * b + half
                r = slice(64 * half, 64 * half + 64)
                for t in range(NT):
                    mm(dst[r, t // 4, (t % 4) * P:(t % 4 + 1) * P], va[:, t, g * 64:(g + 1) * 64], wst[:, g, :],
                       start=False, stop=True, skip_group_check=True)
                last = mm(dst[r, 2, 0:NS], va[0:NS, NT, g * 64:(g + 1) * 64], wsm[:, g, :], start=False, stop=True,
                          skip_group_check=True)
            last.then_inc(slot_full, 1)
        for n in range(N1A, N1A + 4):
            project(n)
        slot_drained(pe, ("k", 0))
        turn(stg[ring[("k", 0)] % 2], [("k", 0, m) for m in range(3)])
        project(N1A + 4)
        slot_drained(pe, ("k", 1))
        turn(stg[ring[("k", 1)] % 2], [("k", 1, m) for m in range(3)])
        project(N1A + 5)
        for b in range(2):
            slot_drained(pe, ("v", b))
            turn(stg[ring[("v", b)] % 2], [("v", b, m) for m in range(3)])

        def scores(n):
            qb, h = steps[n]
            s = ("att", qb, h)
            nk = (qb + 1) * P
            slot_open(pe, s)
            dst = flat(slot[s] % 2)
            for lo in range(0, nk, 512):
                hi = min(lo + 512, nk)
                last = mm(dst[:, lo:hi], q_a[:, h, qb * P:(qb + 1) * P], k_a[:, h, lo:hi], start=True, stop=hi < nk,
                          skip_group_check=True)
            mm(dst[:, qb * P:nk], ident_r[:, :], attneg_r[:, :], start=False, stop=True,
               skip_group_check=True).then_inc(slot_full, 1)

        pe.wait_ge(qk_ready, 2)
        pe.wait_ge(att_rows, 32)
        scores(0)
        pe.wait_ge(v_done, 1)

        def turn_probabilities(n):
            qb, h = steps[n]
            pe.wait_ge(att_norm, n + 1)
            for k, (lo, hi) in enumerate(quads(qb)):
                key = ("p", n, k)
                pt_open(pe, key)
                for t in range(lo, hi):
                    last = tr(pt_of(key)[:, (t - lo) * P:(t - lo + 1) * P], pr[n % 2][:, t * P:(t + 1) * P], ident)
                last.then_inc(pt_full, 1)

        def values(n):
            qb, h = steps[n]
            r = slice(64 * (h % 2), 64 * (h % 2) + 64)
            if n >= 2:
                pe.wait_ge(att_out, n - 1)
            for k, (lo, hi) in enumerate(quads(qb)):
                pt_drained(pe, ("p", n, k))
                for t in range(lo, hi):
                    last = mm(ps[slot[("att", qb, h)] % 2][r, 2, 0:P], v_tok[:, t, h * HD:(h + 1) * HD],
                              pr_t[n % 2][:, t, :], start=t == 0, stop=t == qb)
            last.then_inc(att_pv, 1)

        for n, (qb, h) in enumerate(steps):
            if n + 1 < len(steps):
                scores(n + 1)
            turn_probabilities(n)
            if n >= 1:
                values(n - 1)
        values(len(steps) - 1)
        pe.wait_ge(att_out, len(steps))
        project(N1B)
        pe.wait_ge(ld_lf, 16 * NB * NPG)
        pe.wait_ge(clog_in, 1)
        key = ("clog",)
        pt_open(pe, key)
        for pg in range(NPG):
            tr(pt_of(key)[0:NS, pg * PAGE:(pg + 1) * PAGE], lf_pg[:, pg, :, :].rearrange("p b h -> p (b h)"), ident)
        mm(pt_of(key)[0:NS, PAST:PAST + NQ], lf_new[:, :], const("q4", slice(0, NS)), start=True,
           stop=True).then_inc(pt_full, 1)

        def sample_keys(n):
            key = ("sk", n)
            pe.wait_ge(ld_k[n % 2], 16 * NPG * (n // 2 + 1))
            pt_open(pe, key)
            for k in range(2):
                for pg in range(NPG):
                    last = tr(pt_of(key)[:, (k * NPG + pg) * P:(k * NPG + pg + 1) * P], k_pg[n % 2][:, pg, k * P:(k + 1) * P],
                              ident)
            last.then_inc(pt_full, 1)

        def sample_scores(n):
            key = ("ss", n)
            rows, cols = NH * NQ, slice(n * NH * NQ, (n + 1) * NH * NQ)
            pe.wait_ge(clog_done, 1)
            pe.wait_ge(sx_ready, NH)
            pt_drained(pe, ("sk", n))
            pt_open(pe, key)
            dst = pt_of(key)
            mm(dst[0:rows, 0:PAST + NS], const("expand", slice(0, NS), cols), nc_s[:, :], start=True, stop=False,
               skip_group_check=True)
            mm(dst[0:rows, 0:PAST + NS], cq_s[:, cols], const("ones", slice(0, NS)).to_broadcast([NS, PAST + NS]),
               start=False, stop=False, skip_group_check=True)
            for k in range(2):
                mm(dst[0:rows, 0:PAST], q_s[:, k, n, :], kt_s[:, k, :], start=False, stop=k == 1, skip_group_check=True)
                mm(dst[0:rows, PAST:PAST + NS], q_s[:, k, n, :], ks_new[:, k, :], start=False, stop=False,
                   skip_group_check=True)
            mm(dst[0:rows, PAST:PAST + NS], const("ident", cols=cols), const("sattneg"), start=False, stop=True,
               skip_group_check=True).then_inc(pt_full, 1)

        def sample_turn(n):
            key = ("sp", n)
            pe.wait_ge(ss_done, n + 1)
            pt_open(pe, key)
            rows = NH * NQ
            idr = const("ident", slice(0, rows), slice(0, rows))
            for pg in range(NPG):
                tr(pt_of(key)[:, pg * rows:(pg + 1) * rows], p_s[:, pg * P:(pg + 1) * P], idr)
            tr(pt_of(key)[0:NS, 2 * rows:3 * rows], p_s[:, PAST:PAST + NS], idr).then_inc(pt_full, 1)

        def sample_values(n):
            key = ("so", n)
            pe.wait_ge(ld_v, 16 * NPG * (n + 1))
            pt_drained(pe, ("sp", n))
            pt_open(pe, key)
            for k in range(2):
                dst = pt_of(key)[:, k * NH * NQ:(k + 1) * NH * NQ]
                for pg in range(NPG):
                    mm(dst, v_pg[:, pg, k * P:(k + 1) * P], pt_s[:, pg, :], start=pg == 0, stop=False)
                last = mm(dst, vs_new[:, k * P:(k + 1) * P], pt_s[0:NS, 2, :], start=False, stop=True)
            last.then_inc(pt_full, 1)

        for n in range(NB - 1):
            project(N1B + n + 1, {1: [lambda: sample_values(n - 1)] if n >= 1 else [], 2: [lambda: sample_keys(n)],
                                  4: [lambda: sample_scores(n)], 7: [lambda: sample_turn(n)]})
        sample_values(NB - 2)
        sample_keys(NB - 1)
        sample_scores(NB - 1)
        sample_turn(NB - 1)
        slot_drained(pe, ("z", 0))
        turn(stg[ring[("z", 0)] % 2], [("z", 0, m) for m in range(3)])
        sample_values(NB - 1)
        slot_drained(pe, ("z", 1))
        turn(stg[ring[("z", 1)] % 2], [("z", 1, m) for m in range(3)])
        pe.wait_ge(xstate_in, 6)
        for n, (lo, hi) in enumerate(((0, 4), (4, 6))):
            key = ("xst", n)
            pt_open(pe, key)
            for b in range(lo, hi):
                last = tr(pt_of(key)[0:9 * CV, (b - lo) * P:(b - lo + 1) * P], xstate[:, b, :], ident)
            last.then_inc(pt_full, 1)

        def ssd_front(c):
            s = ("ssd", c)
            r = rows_of(c)
            tok = slice(c * P, c * P + r)
            key = ("xb", c)
            pt_open(pe, key)
            for b in range(4):
                last = tr(pt_of(key)[0:r, b * P:(b + 1) * P], xc[:, b, tok], ident)
            last.then_inc(pt_full, 1)
            slot_open(pe, s)
            dst = ps[slot[s] % 2]
            for g in range(2):
                mm(dst[0:r, 0, g * P:g * P + r], xc[:, 2 + g, tok], xc[:, 4 + g, tok], start=True, stop=True)
            sel = const("acssel", slice(64, 64 + NH)).rearrange("p (h n) -> p h n", h=NH)
            for h in range(NH):
                last = mm(dst[0:r, 1, h * P:h * P + r], sel[:, h, 0:r], sdt[64:64 + NH, tok], start=True, stop=True)
            if c == NT:
                mm(dst[0:NS, 0, 256:260], const("lastsel", slice(0, NS)), sdt_t[0:NS, NT, 64:64 + NH], start=True, stop=True)
                pair = const("pairsel", slice(64, 64 + NH)).rearrange("p (g n) -> p g n", g=2)
                ends = sdt[64:64 + NH, SEQ:T].rearrange("p (b q) -> p b q", q=NQ)[:, :, NQ - 1]
                for g in range(2):
                    last = mm(dst[:, 1, 100 + NB * g:100 + NB * (g + 1)], pair[:, g, :], ends, start=True, stop=True)
            last.then_inc(slot_full, 1)

        def ssd_diag(c, first):
            s = ("ssd", c)
            r = rows_of(c)
            pe.wait_ge(xdt_done, c + 1)
            pe.wait_ge(seg_cb, c + 1)
            for h in range(NH):
                last = mm(ps[slot[s] % 2][0:r, 2, 256 + h * HD:256 + (h + 1) * HD], seg[c % 2][0:r, h, 0:r],
                          xdt[c % 2][0:r, h, :], start=first, stop=True, skip_group_check=True)
            return last

        def ssd_back_of(c):
            s = ("ssd", c)
            dst = ps[slot[s] % 2]
            tok = slice(c * P, (c + 1) * P)
            pe.wait_ge(d_zeroed, 1)
            if c >= 1:
                pe.wait_ge(h_next, c)
            for g in range(2):
                mm(dst[:, 2, g * P:(g + 1) * P], xc[:, 4 + g, tok], hst[:, 2 * g:2 * g + 2, :], start=True, stop=True)
            ssd_diag(c, True)
            pe.wait_ge(xte_done, c + 1)
            for g in range(2):
                last = mm(dst[:, 0, 256 + g * P:256 + (g + 1) * P], xb[c % 2][:, 256 + g * P:256 + (g + 1) * P],
                          xte[c % 2][:, 2 * g:2 * g + 2, :], start=True, stop=True)
            last.then_inc(ssd_back, 1)

        free_of_sx(pe)
        ssd_front(0)
        for c in range(NT):
            ssd_front(c + 1)
            ssd_back_of(c)
        dst = ps[slot[("ssd", NT)] % 2]
        pe.wait_ge(ctm_done, 2 * NB)
        for b in range(NB):
            pe.wait_ge(ld_h0[b % 2], 16 * (b // 2 + 1))
            key = ("sh", b)
            pt_open(pe, key)
            for g in range(2):
                last = tr(pt_of(key)[:, g * P:(g + 1) * P], h0[b % 2][:, g, :], ident)
            last.then_inc(pt_full, 1)
            pt_drained(pe, key)
            for g in range(2):
                mm(dst[0:NS, 2, g * P:(g + 1) * P], ctm[:, g, b, :], h0t[b % 2][:, g, :], start=b == 0 and g == 0,
                   stop=b == NB - 1, skip_group_check=True)
            key = ("sn", b)
            pe.wait_ge(xtm_done, b + 1)
            pt_open(pe, key)
            for g in range(2):
                last = mm(pt_of(key)[:, g * P:(g + 1) * P], xtm[b % 2][:, g * P:(g + 1) * P],
                          xb[NT % 2][0:NS, 256 + g * P:256 + (g + 1) * P], start=True, stop=True)
            last.then_inc(pt_full, 1)
        ssd_diag(NT, False).then_inc(ssd_back, 1)
        key = ("hp",)
        pe.wait_ge(h_next, NT)
        pt_open(pe, key)
        for g in range(2):
            last = tr(pt_of(key)[:, g * P:(g + 1) * P], hst[:, 2 * g:2 * g + 2, :].rearrange("p h d -> p (h d)"), ident)
        last.then_inc(pt_full, 1)
        for t in range(NT + 1):
            r = rows_of(t)
            key = ("yd", t)
            pe.wait_ge(yd_ready, t + 1)
            pt_open(pe, key)
            for b in range(2):
                last = tr(pt_of(key)[:, b * P:b * P + r], zt[0:r, t, b * P:(b + 1) * P], ident[0:r, 0:r])
            last.then_inc(pt_full, 1)
        def gate(j, q):
            n = W3 + q
            pe.wait_ge(w_split, j * 4 + (n + 1))
            if isinstance(j, int) and q == 0:
                slot_drained(pe, slots[-2])
                slot_drained(pe, slots[-1])
            else:
                pe.wait_ge(sg_ready, j * 4 + q)
            product(ps[0], n % 2).then_inc(gate_full, 1)

        def branch(j, q):
            pe.wait_ge(b_split, j * 4 + (q + 1))
            if isinstance(j, int):
                pe.wait_ge(y_split, 2 * q + 2)
            if not isinstance(j, int) or q >= 1:
                pe.wait_ge(br_read, j * 4 + q)
            parts = [(bw_hi, y_hi), (bw_hi, y_lo), (bw_lo, y_hi)]
            for k in range(2):
                for n, (w, y) in enumerate(parts):
                    for c in range(3):
                        last = mm(ps[1][:, c, 0:CH], w[q % 2][:, k, :], y[:, 2 * q + k, c * CH:(c + 1) * CH],
                                  start=k == 0 and n == 0, stop=k == 1 and n == 2)
            last.then_inc(br_full, 1)

        for q in range(4):
            gate(0, q)
            branch(0, q)
        with pe.Fori(1, KD) as j:
            for q in range(4):
                gate(j, q)
                branch(j, q)

        def out_block(i, s):
            first = isinstance(i, int)
            n = W4 + s
            pe.wait_ge(w_split, i * 2 + (n + 1))
            if not first:
                pe.wait_ge(wo_read, i * 2 + (s - 1))
            elif s == 0:
                pe.wait_ge(sg_ready, 4 * KD)
            else:
                pe.wait_ge(br_read, 4 * KD)
            stairs = {k: [lambda k=k: pe.wait_ge(m_split, k + 1)] for k in range(KD)} if first and s == 0 else None
            product(ps[s], n % 2, stairs)
            pe.wait_ge(ld_res[s], i * 32 + 32)
            for t in range(NT + 1):
                lo, hi = t * P, t * P + rows_of(t)
                while lo < hi:
                    c = lo // CH
                    end = min(hi, (c + 1) * CH)
                    last = mm(ps[s][:, c, lo - c * CH:end - c * CH], x_res[s][0:rows_of(t), t, :],
                              ident[0:rows_of(t), lo - t * P:end - t * P], start=False, stop=True,
                              skip_group_check=True)
                    lo = end
            last.then_inc(wo_full, 1)

        for s in range(2):
            out_block(0, s)
        with pe.Fori(1, KD // 2) as i:
            for s in range(2):
                out_block(i, s)
        pe.wait_ge(ld_fh, 16)
        pt_drained(pe, batches[-2])
        pt_drained(pe, batches[-1])
        for n in range(2):
            for b in range(NFF):
                blk = n * NFF + b
                last = tr(pt[n][:, b * NB * FH:(b + 1) * NB * FH], hist_f[0:NB * FH, blk * P:(blk + 1) * P],
                          ident[0:NB * FH, 0:NB * FH])
            last.then_inc(fh_full, 1)
        pe.wait_ge(ones_done, 1)
        pe.wait_ge(ssq_done, KD)
        pe.wait_ge(wo_read, KD)
        for c in range(3):
            last = mm(ps[0][:, c, 0:CH], ones_m[:, :], ssq[:, c * CH:(c + 1) * CH], start=True, stop=True)
        last.then_inc(nm_full, 1)

        def up(s, i, f):
            for k in range(2):
                pe.wait_ge(w_split, i * 6 + (W6 + f + k + 1))
                start = isinstance(i, int) and i == 0 and s == 0
                if not start:
                    pe.wait_ge(up_read, i * 4 + (2 * s + k - 1))
                elif k == 0:
                    pe.wait_ge(nm_rms, 1)
                stairs = {q: [lambda q=q: pe.wait_ge(h2_split, q + 1)] for q in range(KD)} \
                    if start and k == 0 else None
                product(ps[k], (f + k) % 3, stairs).then_inc(up_full, 1)

        def down(i, f, base_split):
            pe.wait_ge(act_split, i * 2 + 2)
            pe.wait_ge(w_split, base_split)
            for n, (m, c) in enumerate(down_sets()):
                if isinstance(i, int) and i == 0 and n < 2:
                    pe.wait_ge(fh_done, 2)
                else:
                    pe.wait_ge(dn_done, i * 24 + (n - 1))
                tok = slice(c * CH, (c + 1) * CH)
                for k in range(2):
                    hi, lo = f_hi[(f + k) % 3], f_lo[(f + k) % 3]
                    dst = pt[n % 2][:, 0:CH]
                    mm(dst, hi[:, m, :], act_hi[:, k, tok], start=k == 0, stop=False)
                    mm(dst, hi[:, m, :], act_lo[:, k, tok], start=False, stop=False)
                    last = mm(dst, lo[:, m, :], act_hi[:, k, tok], start=False, stop=k == 1)
                last.then_inc(dn_full, 1)

        up(0, 0, 0)
        up(1, 0, 2)
        up(0, 1, -2)
        down(0, 6, W6 + 4 + 4)
        up(1, 1, 2)
        with pe.Fori(2, NFF // 2) as i:
            up(0, i, -2)
            down(i - 1, 6, i * 6 + (W6 + 4 + 4 - 6))
            up(1, i, 2)
        n_ring = 4 + 6 * (NFF // 2 - 1)
        for n in range(4):
            pe.wait_ge(cv_taps, 2 * NFF)
            pe.wait_ge(up_read, 2 * NFF)
            if n >= 2:
                pe.wait_ge(out_free[n % 2], n // 2)
            lo, hi = 12 * n, min(12 * (n + 1), 2 * NFF)
            for b in range(lo, hi):
                last = tr(flat(n % 2)[0:9 * FH, (b - lo) * P:(b - lo + 1) * P], fstate[:, b, :], ident)
            last.then_inc(out_full, 1)
        down(NFF // 2 - 1, n_ring, W6 + n_ring + 2)
        pe.wait_ge(dn_done, 24 * (NFF // 2))
        for t in range(NT + 1):
            r = rows_of(t)
            n = 4 + t
            pe.wait_ge(out_free[n % 2], n // 2)
            for k in range(KD):
                last = tr(flat(n % 2)[0:r, k * P:(k + 1) * P], x1[:, k, t * P:t * P + r], ident)
            last.then_inc(out_full, 1)

    top.close()


INPUTS = ["x_prompt", "x_sample", "cache_k", "cache_v", "cache_logf", "page_table", "state_pool", "state_ssd_conv",
          "state_ssd", "state_ffn_conv", "norm1_g", "w_in", "cm_norm_g", "cm_ws", "cm_b", "pool_w", "pool_scale",
          "fox_bf", "ssd_conv_w", "ssd_conv_b", "ssd_dt_bias", "ssd_a_log", "ssd_d", "ssd_norm_g", "w_branch",
          "w_out", "norm2_g", "ffn_up", "ffn_conv_w", "ffn_conv_b", "ffn_down", "final_norm_g"]
OUTPUTS = [("y_prompt", (1, SEQ, D)), ("y_sample", (NB, NQ, D)), ("k_prompt", (1, 1, SEQ, NH, HD)),
           ("v_prompt", (1, 1, SEQ, NH, HD)), ("logf_prompt", (1, 1, SEQ, NH)), ("k_sample", (1, NB, NQ, NH, HD)),
           ("v_sample", (1, NB, NQ, NH, HD)), ("logf_sample", (1, NB, NQ, NH)), ("chunk_v_sample", (1, NB, NQ, CMW)),
           ("pool_prompt", (1, 1, PH, PLW)), ("pool_sample", (1, NB, PH, PLW)), ("ssd_conv_prompt", (1, 1, CV, XBC)),
           ("ssd_conv_sample", (1, NB, CV, XBC)), ("ssd_prompt", (1, 1, NH, HD, SST)),
           ("ssd_sample", (1, NB, NH, HD, SST)), ("ffn_conv_prompt", (1, 1, FH, 2 * FF)),
           ("ffn_conv_sample", (1, NB, FH, 2 * FF))]


def kernel(**inputs):
    import concourse.bacc as bacc
    from concourse.bass_utils import run_bass_kernel_spmd

    nc = bacc.Bacc("TRN2", target_bir_lowering=False, num_devices=1)
    arrays, a, o = {}, {}, {}
    given = {name: np.ascontiguousarray(inputs[name]) for name in INPUTS}
    given["consts"] = constants()
    for name, x in given.items():
        arrays[f"in_{name}"] = x
        a[name] = nc.dram_tensor(f"in_{name}", x.shape, mybir.dt.from_np(x.dtype), kind="ExternalInput").ap()
    for name, shape in OUTPUTS:
        o[name] = nc.dram_tensor(f"out_{name}", shape, F32, kind="ExternalOutput").ap()
    decoder_layer(nc, a, o)
    r = run_bass_kernel_spmd(nc, [arrays], core_ids=[0])
    return tuple(r.results[0][f"out_{name}"] for name, _ in OUTPUTS)
```

```python
import numpy as np
from contextlib import ExitStack

import concourse.bass as bass
from concourse import mybir

F32 = mybir.dt.float32
F32R = mybir.dt.float32r
I32 = mybir.dt.int32
ACT = mybir.ActivationFunctionType
ALU = mybir.AluOpType
AX = mybir.AxisListType

P = 128
D = 1024
KD = D // P
SEQ, NB, NQ = 1024, 8, 4
NS = NB * NQ
T = SEQ + NS
CH = T // 3
NT = SEQ // P
PAST, PAGE = 256, 128
NPG = PAST // PAGE
CMW, PLW = 256, 256
WINDOWS = (2, 4, 8, 16)
PH = 15
NH, HD = 4, 64
SST = 128
CV = 3
XBC = 768
FF = 2816
NFF = FF // P
FH = 2
EPS = 1e-6
NEG = -1e30
COL_POOL, COL_Q, COL_K, COL_V = 512, 768, 1024, 1280
COL_F, COL_Z, COL_XBC, COL_DT, COL_GATE = 1536, 1540, 1796, 2564, 2568
N_IN = 6664

PE_W = PH + SEQ + NB * (PH + NQ)
XE_W = CV + SEQ + NB * (CV + NQ)
FE_W = FH + SEQ + NB * (FH + NQ)

PV_G1, PV_G2, PV_CW, PV_CB, PV_PS, PV_SG, PV_FB, PV_FW = 0, 8, 16, 40, 46, 48, 50, 94
PV_N = 226

_CONSTS = [("ident", 128), ("tri01", 128), ("ssdneg", 128), ("attneg", 128), ("blk01", 32), ("blkneg", 32),
           ("sattneg", 32), ("expand", 128), ("pfix", 30), ("acssel", 512),
           ("pairsel", 256), ("bmask", 32), ("q4", 4), ("rep4", 32), ("bsel", 8),
           ("ones", 1), ("lastsel", 32)]
COFF, CN = {}, 0
for _n, _w in _CONSTS:
    COFF[_n] = (CN, _w)
    CN += _w


def constants():
    c = np.zeros((P, CN), np.float32)

    def put(name, a, row=0):
        o, w = COFF[name]
        a = np.asarray(a, np.float32).reshape(a.shape[0], w)
        c[row:row + a.shape[0], o:o + w] = a

    i = np.arange(P)
    put("ident", np.eye(P))
    put("tri01", i[None, :] >= i[:, None])
    put("ssdneg", np.where(i[None, :] >= i[:, None], 0, NEG))
    put("attneg", np.where(i[None, :] <= i[:, None], 0, NEG))
    s = np.arange(NS)
    same = (s[:, None] // NQ == s[None, :] // NQ) & (s[None, :] >= s[:, None])
    put("blk01", same)
    put("blkneg", np.where(same, 0, NEG))
    r_b, r_q = i // (NH * NQ), i % NQ
    put("sattneg", np.where((r_b[:, None] == s[None, :] // NQ) & (s[None, :] % NQ <= r_q[:, None]), 0, NEG))
    put("expand", i[None, :] // NQ == s[:, None])
    w = np.array(WINDOWS, np.float32)
    fix = np.zeros((P, 2, PH), np.float32)
    for b in range(2):
        for half in range(2):
            win = WINDOWS[2 * b + half]
            fix[64 * half:64 * half + 64, b] = win / np.minimum(np.arange(PH) + 1, win)
    put("pfix", fix)
    put("acssel", np.repeat(np.eye(NH)[:, :, None], P, 2), row=64)
    pair = np.zeros((NH, 2, P))
    for g in range(2):
        for half in range(2):
            pair[2 * g + half, g, 64 * half:64 * half + 64] = 1
    put("pairsel", pair, row=64)
    put("pairsel", pair)
    put("bmask", s[:, None] // NQ == s[None, :] // NH)
    put("q4", s[:, None] % NQ == np.arange(NQ)[None, :])
    put("rep4", np.arange(NQ)[:, None] == s[None, :] % NQ)
    put("ones", np.ones((P, 1)))
    put("lastsel", s[:, None] == s[None, :] // NQ * NQ + NQ - 1)
    put("bsel", s[:, None] // NQ == np.arange(NB)[None, :])
    return c


class Order:

    def __init__(self, eng, own):
        self.eng, self.own, self.n, self.turn = eng, own, {}, {}

    def value(self, sem):
        n = self.n.get(sem.name, 0)
        if sem.name in self.turn:
            i, first, per = self.turn[sem.name]
            return (i - first) * per + n
        return n

    def run(self, ins, sem=None):
        sem = sem or self.own
        if isinstance(sem, tuple):
            ins.then_inc(sem[0], 1)
            self.eng.wait_ge(sem[0], sem[1])
            return
        ins.then_inc(sem, 1)
        self.n[sem.name] = self.n.get(sem.name, 0) + 1
        self.eng.wait_ge(sem, self.value(sem))

    def peel(self):
        self.before = dict(self.n)

    def enter(self, i, first, extra=()):
        per = {name: n - self.before.get(name, 0) for name, n in self.n.items()}
        per.update({s.name: k for s, k in extra})
        self.base = dict(self.n)
        self.turn = {name: (i, first, k) for name, k in per.items()}

    def leave(self, turns):
        for name, (_, _, per) in self.turn.items():
            assert self.n.get(name, 0) - self.base.get(name, 0) == per, (name, self.n[name] - self.base[name], per)
            self.n[name] = self.base.get(name, 0) + per * turns
        self.turn = {}


def decoder_layer(nc, a, o):
    top = ExitStack()

    def sb(scope, name, shape, dt=F32):
        return scope.enter_context(nc.sbuf_tensor(name, shape, dt))

    def sem(name):
        return top.enter_context(nc.semaphore(name))

    cst = sb(top, "cst", [P, CN])
    pv = sb(top, "pv", [P, PV_N])
    eps = sb(top, "eps", [P, 1])
    mark = sb(top, "mark", [P, 3])
    stat7 = sb(top, "stat7", [P, 3, NT + 1])
    h_hi = sb(top, "h_hi", [P, KD, T], F32R)
    h_lo = sb(top, "h_lo", [P, KD, T], F32R)
    y_all = sb(top, "y_all", [P, 2 * 4, T])
    w_raw = [sb(top, f"w_raw{n}", [P, KD, P]) for n in range(2)]
    w_hi = [sb(top, f"w_hi{n}", [P, KD, P], F32R) for n in range(2)]
    w_lo = [sb(top, f"w_lo{n}", [P, KD, P], F32R) for n in range(2)]

    def const(name, rows=slice(0, P), cols=None):
        off, w = COFF[name]
        return cst[rows, off:off + w] if cols is None else cst[rows, off + cols.start:off + cols.stop]

    ident = const("ident")
    ps = [top.enter_context(nc.psum_tensor(f"ps{n}", [P, 3, 512], F32)) for n in range(2)]
    pt = [top.enter_context(nc.psum_tensor(f"pt{n}", [P, 512], F32)) for n in range(2)]

    def flat(n):
        return ps[n][:, :, :].rearrange("p c n -> p (c n)")

    def chunked(n, rows=slice(0, P)):
        return ps[n][rows, :, 0:CH]

    def in_chunks(ap):
        return ap.rearrange("p (c n) -> p c n", c=3)

    s1 = ExitStack()
    stg = [sb(s1, f"stg{n}", [P, T]) for n in range(2)]
    sdt = sb(s1, "sdt", [P, T])
    sdt_t = sb(s1, "sdt_t", [P, NT + 1, 100])
    hist_t = sb(s1, "hist_t", [P, 6 * 24 + 2 * 120])
    stat = sb(s1, "stat", [P, 4, NT + 1])
    ast = sb(s1, "ast", [P, 3, NT * NH])
    qs_new = sb(s1, "qs_new", [P, 2, NS])
    ks_new = sb(s1, "ks_new", [P, 2, NS])
    vs_new = sb(s1, "vs_new", [NS, 256])
    pages = sb(s1, "pages", [1, NB * NPG], I32)
    lf_pg = sb(s1, "lf_pg", [P, NPG, NB, NH])
    lf_new = sb(s1, "lf_new", [NS, NS])
    c_s = sb(s1, "c_s", [NS, PAST + NQ])
    nc_s = sb(s1, "nc_s", [NS, PAST + NS])
    cq_s = sb(s1, "cq_s", [NS, P])

    s1a = ExitStack()
    small = sb(s1a, "small", [P, 4])
    hist_p = sb(s1a, "hist_p", [NB * PH, PLW])
    hist_x = sb(s1a, "hist_x", [NB * CV, XBC])
    s0 = ExitStack()
    x_tok = [sb(s0, f"x_tok{n}", [P, D]) for n in range(3)]
    x_scaled = [sb(s0, f"x_scaled{n}", [P, D]) for n in range(2)]
    h_f = [sb(s0, f"h_f{n}", [P, KD, P]) for n in range(2)]
    vec1 = sb(s0, "vec1", [94, P])
    vec2 = sb(s0, "vec2", [88, P])
    vec3 = sb(s0, "vec3", [44, P])
    junk = sb(s0, "junk", [P, D])
    s0.close()
    va = sb(s1a, "va", [P, NT + 1, CMW])
    u_f = sb(s1a, "u_f", [P, 2, T])
    p_ext = sb(s1a, "p_ext", [P, 2, PE_W + 4])
    win_a = sb(s1a, "win_a", [P, 2, PE_W])
    win_b = sb(s1a, "win_b", [P, 2, PE_W])
    pw = sb(s1a, "pw", [P, 2, P])
    cmb = sb(s1a, "cmb", [NH, P])
    pjunk = sb(s1a, "pjunk", [P, CMW])[:, :]
    ws = win_a[:, 0, 0:4 * P].rearrange("p (g s) -> p g s", g=4)
    wst = win_b[:, 0, 0:4 * P].rearrange("p (g s) -> p g s", g=4)
    wsm = win_b[0:NS, 1, 0:4 * NS].rearrange("p (g s) -> p g s", g=4)
    cmg = win_a[:, 1, 0:CMW]
    p_state = sb(s1a, "p_state", [P, 2, 9 * PH])
    p_out = win_b[:, 1, 512:512 + 2 * PLW].rearrange("p (b n) -> p b n", b=2)
    dk = [win_a[:, 0, 0:T], win_a[:, 1, 0:T], win_b[:, 0, 0:T], win_b[:, 1, 0:T]]
    s1a.close()

    JOBS = [("fdt", 0, None)]
    JOBS += [("pool", b, COL_POOL + b * P) for b in range(2)]
    JOBS += [("va", b, CMW + b * P) for b in range(2)]
    JOBS += [("u", b, b * P) for b in range(2)]
    N1A = len(JOBS)
    JOBS += [("q", b, COL_Q + b * P) for b in range(2)]
    JOBS += [("k", b, COL_K + b * P) for b in range(2)]
    JOBS += [("v", b, COL_V + b * P) for b in range(2)]
    N1B = len(JOBS)
    JOBS += [("xbc", b, COL_XBC + b * P) for b in range(6)]
    JOBS += [("z", b, COL_Z + b * P) for b in range(2)]
    N1C = len(JOBS)
    ring = {j: n for n, j in enumerate([j[:2] for j in JOBS if j[0] != "u"])}
    jobs_a, jobs_b, jobs_c = JOBS[:N1A], JOBS[N1A:N1B], JOBS[N1B:N1C]
    slots = [j[:2] for j in jobs_a]
    slots += [("q", 0), ("mixb", 0), ("mixb", 1), ("mixa", 0), ("mixa", 1)]
    slots += [j[:2] for j in jobs_b[1:]]
    slots += [("att", qb, h) for qb in range(NT) for h in range(NH)]
    slots += [j[:2] for j in jobs_c]
    slots += [("ssd", c) for c in range(NT + 1)]
    slot = {s: m for m, s in enumerate(slots)}
    THIRDS = [(0, 4), (4, 8), (8, 9)]
    batches = [("vec",), ("hist",)] + [("x", i, half) for i in range(NT + 1) for half in range(2)]
    batches += [("sdt", 0), ("sdt", 1), ("va", 0, 0), ("va", 0, 1), ("va", 0, 2)]
    batches += [("va", 1, 0), ("va", 1, 1), ("va", 1, 2), ("ws",), ("wsm",), ("pstate", 0), ("pstate", 1)]
    batches += [(kind, b, n) for kind in "kv" for b in range(2) for n in range(3)]
    steps = [(qb, h) for qb in range(NT) for h in range(NH)]

    def quads(qb):
        return [(lo, min(lo + 4, qb + 1)) for lo in range(0, qb + 1, 4)]

    batches += [("clog",)]
    for n, (qb, h) in enumerate(steps):
        batches += [("p", n, k) for k in range(len(quads(qb)))]
    for n in range(NB):
        if n >= 1:
            batches.append(("so", n - 1))
        batches += [("sk", n), ("ss", n), ("sp", n)]
        if n == 7:
            batches += [("z", 0, k) for k in range(3)]
    batches += [("so", NB - 1)] + [("z", 1, k) for k in range(3)] + [("xst", 0), ("xst", 1)]
    for c in range(NT + 1):
        batches += [("xb", c)]
        if c == NT:
            batches += [("sh", 0)]
            for b in range(NB):
                batches += [("sn", b)] + [("sh", b + 1)] * (b + 1 < NB)
    batches += [("hp",)] + [("yd", t) for t in range(NT + 1)]
    batch = {}

    ld_const, ld_vec, ld_small, ld_hist = sem("ld_const"), sem("ld_vec"), sem("ld_small"), sem("ld_hist")
    ld_pw, ld_ws = sem("ld_pw"), sem("ld_ws")
    ld_x = [sem(f"ld_x{n}") for n in range(3)]
    ld_w = [sem(f"ld_w{n}") for n in range(2)]
    stored = sem("stored")
    w_split = sem("w_split")
    w_zeroed, small_zeroed, a_zeroed = sem("w_zeroed"), sem("small_zeroed"), sem("a_zeroed")
    pool_own, act_own, dve_own = sem("pool_own"), sem("act_own"), sem("dve_own")
    x_inv, x_half = sem("x_inv"), sem("x_half")
    x_sq, x_normed, h_hi_done, h_split = sem("x_sq"), sem("x_normed"), sem("h_hi_done"), sem("h_split")
    slot_full = sem("slot_full")
    slot_free = [sem(f"slot_free{n}") for n in range(2)]
    pt_full = sem("pt_full")
    pt_free = [sem(f"pt_free{n}") for n in range(2)]
    vec_done, stg_free = sem("vec_done"), sem("stg_free")
    dk_abs, dk_exp, dk_u, dk_ln = sem("dk_abs"), sem("dk_exp"), sem("dk_u"), sem("dk_ln")
    alog_exp, sdt_done = sem("alog_exp"), sem("sdt_done")
    a_sum, a_rms, va_done = sem("a_sum"), sem("a_rms"), sem("va_done")
    pd_done = sem("pd_done")
    pstate_in, pstate_out = sem("pstate_in"), sem("pstate_out")

    def slot_filled(eng, s):
        eng.wait_ge(slot_full, slot[s] + 1)

    def slot_drained(eng, s):
        eng.wait_ge(slot_free[slot[s] % 2], slot[s] // 2 + 1)

    def slot_open(eng, s):
        if slot[s] >= 2:
            eng.wait_ge(slot_free[slot[s] % 2], slot[s] // 2)

    def free_of(s):
        return slot_free[slot[s] % 2], slot[s] // 2 + 1

    def pt_filled(eng, b):
        eng.wait_ge(pt_full, batch[b] + 1)

    def pt_drained(eng, b):
        eng.wait_ge(pt_free[batch[b] % 2], batch[b] // 2 + 1)

    def pt_open(eng, b):
        if batch[b] >= 2:
            eng.wait_ge(pt_free[batch[b] % 2], batch[b] // 2)

    def pt_of(b):
        return pt[batch[b] % 2]

    def ptf_of(b):
        return pt_free[batch[b] % 2], batch[b] // 2 + 1

    batch.update({b: n for n, b in enumerate(batches)})

    s1b = ExitStack()
    q_a = sb(s1b, "q_a", [HD + 2, NH, SEQ])
    k_a = sb(s1b, "k_a", [HD + 2, NH, SEQ])
    v_tok = sb(s1b, "v_tok", [P, NT + 1, 256])
    k_out = [sb(s1b, f"k_out{n}", [P, 4, P]) for n in range(2)]
    pr = [stg[n][:, 0:SEQ] for n in range(2)]
    pr_t = [sb(s1b, f"pr_t{n}", [P, NT, P]) for n in range(2)]
    ident_r = sb(s1b, "ident_r", [P, P], F32R)
    attneg_r = sb(s1b, "attneg_r", [P, P], F32R)
    s1b.close()

    s1c = ExitStack()
    xc = sb(s1c, "xc", [P, 6, T])
    zt = sb(s1c, "zt", [P, NT + 1, 256])
    xstate = sb(s1c, "xstate", [P, 6, 9 * CV])
    sx = ExitStack()
    x_ext = sb(sx, "x_ext", [P, XE_W + 4])
    x_cv = sb(sx, "x_cv", [P, XE_W])
    k_pg = [sb(sx, f"k_pg{n}", [P, NPG, 256]) for n in range(2)]
    v_pg = sb(sx, "v_pg", [P, NPG, 256])
    q_s = sb(sx, "q_s", [P, 2, NB, NH * NQ])
    kt_s = sb(sx, "kt_s", [P, 2, PAST])
    p_s = sb(sx, "p_s", [NH * NQ, PAST + NS])
    pt_s = sb(sx, "pt_s", [P, 3, NH * NQ])
    sx.close()
    sd = ExitStack()
    seg = [sb(sd, f"seg{n}", [P, NH, P]) for n in range(2)]
    xb = [sb(sd, f"xb{n}", [P, 512]) for n in range(2)]
    xdt = [sb(sd, f"xdt{n}", [P, NH, HD]) for n in range(2)]
    xte = [sb(sd, f"xte{n}", [P, NH, HD]) for n in range(2)]
    xd = [sb(sd, f"xd{n}", [P, NH, HD]) for n in range(2)]
    yoff = sb(sd, "yoff", [P, NH, HD])
    hst = sb(sd, "hst", [P, NH, HD])
    dec = [sb(sd, f"dec{n}", [P, 3, NH]) for n in range(2)]
    xst_out = stg[0][0:9 * CV, 0:XBC]
    h0 = [sb(sd, f"h0_{n}", [P, 2, P]) for n in range(2)]
    h0t = [sb(sd, f"h0t{n}", [P, 2, P]) for n in range(2)]
    ctm = stg[1][:, 0:512].rearrange("p (g b n) -> p g b n", g=2, b=NB)
    h_out = [stg[1][:, 512 + 256 * n:768 + 256 * n].rearrange("p (g k) -> p g k", g=2) for n in range(2)]
    xtm = [c_s[:, 0:256], nc_s[:, 0:256]]
    sdec = sb(sd, "sdec", [P, 2, NB])
    d_b = sb(sd, "d_b", [P, NH])
    eacs = sb(sd, "eacs", [P, NT + 1, NH])
    sd.close()
    s1c.close()

    att_zeroed, att_rows, v_done = sem("att_zeroed"), sem("att_rows"), sem("v_done")
    k_ready, k_sent = sem("k_ready"), [sem(f"k_sent{n}") for n in range(2)]
    att_max, att_norm, att_pv, att_out = sem("att_max"), sem("att_norm"), sem("att_pv"), sem("att_out")
    qk_ready = sem("qk_ready")
    c_zeroed, sx_ready, clog_in, clog_done = sem("c_zeroed"), sem("sx_ready"), sem("clog_in"), sem("clog_done")
    ld_pages, ld_lf, ld_v = sem("ld_pages"), sem("ld_lf"), sem("ld_v")
    ld_k = [sem(f"ld_k{n}") for n in range(2)]
    ss_max, ss_done = sem("ss_max"), sem("ss_done")
    x_conv, x_act, xstate_in, xst_ready = (sem(n) for n in ("x_conv", "x_act", "xstate_in", "xst_ready"))
    d_zeroed, ld_d, eacs_done = sem("d_zeroed"), sem("ld_d"), sem("eacs_done")
    seg_in, seg_exp, seg_cb, dec_exp = sem("seg_in"), sem("seg_exp"), sem("seg_cb"), sem("dec_exp")
    xdt_done, xd_done, xte_done, xtm_done = sem("xdt_done"), sem("xd_done"), sem("xte_done"), sem("xtm_done")
    ssd_back, h_next, y_gated, ctm_done = sem("ssd_back"), sem("h_next"), sem("y_gated"), sem("ctm_done")
    ld_h0 = [sem(f"ld_h0_{n}") for n in range(2)]
    h_ready, h_sent, sdec_done = sem("h_ready"), [sem(f"h_sent{n}") for n in range(2)], sem("sdec_done")
    d_rms, yd_ready = sem("d_rms"), sem("yd_ready")

    s1.close()
    merged, x1 = y_all, y_all
    s3 = ExitStack()
    bw_raw = [sb(s3, f"bw_raw{n}", [P, 2, P]) for n in range(2)]
    bw_hi = [sb(s3, f"bw_hi{n}", [P, 2, P], F32R) for n in range(2)]
    bw_lo = [sb(s3, f"bw_lo{n}", [P, 2, P], F32R) for n in range(2)]
    sg = sb(s3, "sg", [P, T])
    y_hi = sb(s3, "y_hi", [P, KD, T], F32R)
    y_lo = sb(s3, "y_lo", [P, KD, T], F32R)
    s3.close()
    s46 = ExitStack()
    hist_f = sb(s46, "hist_f", [9 * FH, 2 * FF])
    fh = sb(s46, "fh", [P, 2 * NFF, NB * FH])
    fstate = sb(s46, "fstate", [P, 2 * NFF, 9 * FH])
    f_raw = w_raw + [sb(s46, "w_raw2", [P, KD, P])]
    f_hi = w_hi + [sb(s46, "w_hi2", [P, KD, P], F32R)]
    f_lo = w_lo + [sb(s46, "w_lo2", [P, KD, P], F32R)]
    s4 = ExitStack()
    x_res = [sb(s4, f"x_res{n}", [P, NT + 1, P]) for n in range(2)]
    sq = sb(s4, "sq", [P, T])
    ssq = sb(s4, "ssq", [P, T])
    rstd = cst[:, P:P + T]
    ones_m = sb(s4, "ones_m", [P, P])
    s4.close()
    ext = [sb(s46, f"ext{n}", [P, FE_W + 4]) for n in range(2)]
    cv = [sb(s46, f"cv{n}", [P, FE_W]) for n in range(2)]
    act_hi = sb(s46, "act_hi", [P, 2, T], F32R)
    act_lo = sb(s46, "act_lo", [P, 2, T], F32R)
    s46.close()
    y_out = [f_raw[n][:, :, :].rearrange("p k n -> p (k n)") for n in range(3)]
    gfin = ext[1][:, 0:D]
    squares = cv[0][:, 0:D]

    ld_b = [sem(f"ld_b{n}") for n in range(2)]
    y_hi_done, y_split, b_split = sem("y_hi_done"), sem("y_split"), sem("b_split")
    gate_full, br_full, sg_ready, br_read, merged_done = (sem(n) for n in ("gate_full", "br_full", "sg_ready",
                                                                           "br_read", "merged_done"))
    merged_used = sem("merged_used")
    EARLY_H2 = 2
    m_hi_done, m_split, wo_full, wo_read, ssq_done = (sem(n) for n in ("m_hi_done", "m_split", "wo_full", "wo_read",
                                                                       "ssq_done"))
    ld_res, ld_fh, fh_full, fh_done = [sem(f"ld_res{n}") for n in range(2)], sem("ld_fh"), sem("fh_full"), sem("fh_done")
    ones_done, nm_full, nm_rms, h2_hi_done, h2_split = (sem(n) for n in ("ones_done", "nm_full", "nm_rms",
                                                        "h2_hi_done", "h2_split"))
    ld_f = [sem(f"ld_f{n}") for n in range(3)]
    up_full, up_read, cv0_done, cv_taps, silu_done, prod_done = (sem(n) for n in ("up_full", "up_read", "cv0_done",
                                                                 "cv_taps", "silu_done", "prod_done"))
    act_hi_done, act_split, dn_full, dn_done = sem("act_hi_done"), sem("act_split"), sem("dn_full"), sem("dn_done")
    out_full, out_free = sem("out_full"), [sem(f"out_free{n}") for n in range(2)]
    ld_gfin, y_sq, y_ready, fs_ready, f_zeroed = (sem(n) for n in ("ld_gfin", "y_sq", "y_ready", "fs_ready", "f_zeroed"))
    y_sent = [sem(f"y_sent{n}") for n in range(3)]
    W3 = N1C
    W4 = W3 + 4 * KD
    W6 = W4 + KD
    assert W6 % 2 == 1

    def ring_slot(f):
        return (2 - f) % 3


    block = top.enter_context(nc.Block())
    n_stores = [0]

    N_STORES_1A = 6

    def x_new(cv):
        return cv[:, SEQ + CV:SEQ + CV + NB * (CV + NQ)].rearrange("p (s n) -> p s n", s=NB)[:, :, 0:NQ]

    def free_of_1a(eng):
        slot_drained(eng, ("mixa", 1))
        slot_drained(eng, ("mixb", 1))
        eng.wait_ge(stored, 16 * N_STORES_1A)

    N_STORES_1B = N_STORES_1A + 2
    N_STORES_1 = N_STORES_1B + 2

    def free_of_1b(eng):
        eng.wait_ge(att_out, NT * NH)
        eng.wait_ge(stored, 16 * N_STORES_1B)
        for n in range(2):
            eng.wait_ge(k_sent[n], 16 * 3)

    def free_of_sx(eng):
        eng.wait_ge(x_act, 6)
        pt_drained(eng, ("so", NB - 1))
        pt_drained(eng, ("z", 1, 2))

    def rows_of(i):
        return P if i < NT else NS

    def free_of_s1(eng):
        pt_drained(eng, ("yd", NT))
        eng.wait_ge(stored, 16 * N_STORES_1)
        eng.wait_ge(h_sent[0], 16 * 5)
        eng.wait_ge(h_sent[1], 16 * 4)

    def ffn_kinds(e):
        return (0, e), (1, e + NFF)

    def down_sets():
        return [(m, c) for m in range(KD) for c in range(3)]

    LAST_SETS = [(m, c) for c in range(3) for m in range(KD)]
    STATES = [[(0, 12)], [(12, NFF - 1)], [(NFF, NFF + 12)], [(NFF + 12, 2 * NFF - 1)], [(NFF - 1, NFF), (2 * NFF - 1, 2 * NFF)]]
    TAIL = [("sums", 0, 16), ("state", 4), ("tile", 0), ("tile", 1),
            ("sums", 16, 20), ("tile", 2), ("sums", 20, 24)] + [("tile", t) for t in range(3, NT + 1)]
    TAIL_DVE = [("sums", 0, 16), ("tile", 0), ("sums", 16, 20), ("tile", 1), ("sums", 20, 24)] + \
        [("tile", t) for t in range(2, NT + 1)]

    def spaced(x):
        new = x[:, SEQ + FH:FE_W].rearrange("p (s n) -> p s n", s=NB)[:, :, 0:NQ]
        return x[:, 0:SEQ], new

    def packed(x):
        return x[:, 0:SEQ], x[:, SEQ:T].rearrange("p (s n) -> p s n", s=NB)

    @block.sync
    def _(sp):
        def store(dst, src):
            sp.dma_start(dst, src).then_inc(stored, 16)
            n_stores[0] += 1

        def load_weights(n):
            kind, b, col = JOBS[n]
            if n >= 2:
                sp.wait_ge(w_split, n - 1)
            w = a["w_in"][0].rearrange("(k p) n -> p k n", p=P)
            if kind == "fdt":
                sp.wait_ge(w_zeroed, 1)
                sp.dma_start(w_raw[0][:, :, 0:NH], w[:, :, COL_F:COL_F + NH]).then_inc(ld_w[0], 16)
                sp.dma_start(w_raw[0][:, :, 32:32 + NH], w[:, :, COL_DT:COL_DT + NH]).then_inc(ld_w[0], 16)
            else:
                sp.dma_start(w_raw[n % 2][:, :, :], w[:, :, col:col + P]).then_inc(ld_w[n % 2], 16)

        sp.dma_start(pages[:, :], a["page_table"].rearrange("(o b) n -> o (b n)", o=1)).then_inc(ld_pages, 16)
        for i in range(NT + 1):
            if i >= 3:
                sp.wait_ge(x_normed, i - 2)
                sp.wait_ge(x_half, i - 2)
            src = a["x_prompt"][0, i * P:(i + 1) * P, :] if i < NT else a["x_sample"].rearrange("b q d -> (b q) d")
            sp.dma_start(x_tok[i % 3][0:rows_of(i), :], src).then_inc(ld_x[i % 3], 16)
            if i == 2:
                load_weights(0)
                load_weights(1)
        sp.wait_ge(a_zeroed, 1)
        for g in range(4):
            r = slice(64 * (g % 2), 64 * (g % 2) + 64)
            sp.dma_start(pw[r, g // 2, r], a["pool_w"][0, g]).then_inc(ld_pw, 16)
        sp.dma_start(cmb[:, :], a["cm_b"][0]).then_inc(ld_pw, 16)
        for n in range(2, 6):
            load_weights(n)
        sp.wait_ge(pd_done, 1)
        sp.dma_start(ws, a["cm_ws"][0].rearrange("g t s -> t g s")).then_inc(ld_ws, 16)
        sp.dma_start(cmg, a["cm_norm_g"].partition_broadcast(P).rearrange("p a c -> p (a c)")).then_inc(ld_ws, 16)
        load_weights(6)
        load_weights(N1A)
        load_weights(N1A + 1)
        load_weights(N1A + 2)
        pt_drained(sp, ("sdt", 1))
        store(o["logf_prompt"][0, 0].rearrange("(t p) h -> p t h", p=P), sdt_t[:, 0:NT, 0:NH])
        store(o["logf_sample"][0].rearrange("b q h -> (b q) h"), sdt_t[0:NS, NT, 0:NH])
        sp.wait_ge(pstate_out, 2)
        for lo, n in ((0, 5), (5, 4)):
            part = p_out[:, lo // 5, :]
            if lo == 0:
                store(o["pool_prompt"][0, 0], part[0:PH, :])
                store(o["pool_sample"][0, 0:4].rearrange("b r c -> (b r) c"), part[PH:5 * PH, :])
            else:
                store(o["pool_sample"][0, 4:8].rearrange("b r c -> (b r) c"), part[0:4 * PH, :])
        sp.wait_ge(va_done, 1)
        store(o["chunk_v_sample"][0].rearrange("b q c -> (b q) c"), va[0:NS, NT, :])
        N_STORES_A = n_stores[0]
        load_weights(N1A + 3)
        sp.wait_ge(att_zeroed, 1)
        sp.dma_start(q_a[HD:HD + 1, :, :], sdt[96:96 + NH, 0:SEQ]).then_inc(att_rows, 16)
        sp.dma_start(k_a[HD + 1:HD + 2, :, :], sdt[96:96 + NH, 0:SEQ]).then_inc(att_rows, 16)
        load_weights(N1A + 4)
        load_weights(N1A + 5)
        sp.wait_ge(ld_pages, 16)
        n_phys = a["cache_k"].shape[1]
        cache_k, cache_v = (a[n][0].rearrange("n p h d -> n p (h d)") for n in ("cache_k", "cache_v"))

        def page(b, pg):
            return sp.value_load(pages[0:1, b * NPG + pg:b * NPG + pg + 1], min_val=0, max_val=n_phys - 1)

        for b in range(NB):
            for pg in range(NPG):
                sp.dma_start(lf_pg[:, pg, b, :], a["cache_logf"][0][bass.ds(page(b, pg), 1)]
                             .rearrange("o p h -> p (o h)")).then_inc(ld_lf, 16)
        kp = o["k_prompt"][0, 0].rearrange("(t p) h d -> p t (h d)", p=P)
        for b in range(2):
            for n, (lo, hi) in enumerate(THIRDS):
                m = 3 * b + n
                sp.wait_ge(k_ready, m + 1)
                if hi <= NT:
                    dst, src = kp[:, lo:hi, b * P:(b + 1) * P], k_out[m % 2][:, :, :]
                else:
                    dst = o["k_sample"][0].rearrange("b q h d -> (b q) (h d)")[:, b * P:(b + 1) * P]
                    src = k_out[m % 2][0:NS, 0, :]
                sp.dma_start(dst, src).then_inc(k_sent[m % 2], 16)
        load_weights(N1B)
        load_weights(N1B + 1)
        sp.wait_ge(v_done, 1)
        store(o["v_prompt"][0, 0].rearrange("(t p) h d -> p t (h d)", p=P), v_tok[:, 0:NT, :])
        store(o["v_sample"][0].rearrange("b q h d -> (b q) (h d)"), v_tok[0:NS, NT, :])
        free_of_1b(sp)
        for n in range(NB):
            if n >= 2:
                pt_filled(sp, ("sk", n - 2))
            for pg in range(NPG):
                sp.dma_start(k_pg[n % 2][:, pg, :], cache_k[bass.ds(page(n, pg), 1)]
                             .rearrange("o p c -> p (o c)")).then_inc(ld_k[n % 2], 16)
            if n >= 1:
                pt_filled(sp, ("so", n - 1))
            for pg in range(NPG):
                sp.dma_start(v_pg[:, pg, :], cache_v[bass.ds(page(n, pg), 1)]
                             .rearrange("o p c -> p (o c)")).then_inc(ld_v, 16)
            if n + 2 < NB:
                load_weights(N1B + n + 2)
        free_of_sx(sp)
        sp.dma_start(d_b[:, :], a["ssd_d"].partition_broadcast(P).rearrange("p a h -> p (a h)")).then_inc(ld_d, 16)
        sp.wait_ge(xst_ready, 2)
        store(o["ssd_conv_prompt"][0, 0], xst_out[0:CV, :])
        store(o["ssd_conv_sample"][0].rearrange("b r c -> (b r) c"), xst_out[CV:9 * CV, :])

        def by_pair(x):
            return x.rearrange("(g h) p k -> (h p) g k", g=2)

        def at(expr):
            return expr if isinstance(expr, int) else sp.snap(expr)

        def load_block(base, q, per, i, src):
            n = base + q
            sp.wait_ge(w_split, i * per + (n - 1))
            sp.dma_start(w_raw[n % 2][:, :, :], src).then_inc(ld_w[n % 2], 16)

        w_in = a["w_in"][0].rearrange("(k p) n -> p k n", p=P)
        w_br = a["w_branch"][0].rearrange("i (k p) n -> p i k n", p=P)

        for q in range(2):
            load_block(W3, q, 4, 0, w_in[:, :, bass.ds(COL_GATE + q * D, P)])
        for b in range(NB + 2):
            if b >= 2:
                sp.wait_ge(h_ready, b - 1)
            if b < NB:
                sp.dma_start(h0[b % 2][:, :, :], by_pair(a["state_ssd"][0, b])).then_inc(ld_h0[b % 2], 16)
            if b >= 2:
                sp.dma_start(by_pair(o["ssd_sample"][0, b - 2]), h_out[b % 2]).then_inc(h_sent[b % 2], 16)
        sp.wait_ge(h_ready, NB + 1)
        sp.dma_start(by_pair(o["ssd_prompt"][0, 0]), h_out[0]).then_inc(h_sent[0], 16)
        sp.wait_ge(h_sent[0], 16 * 5)
        sp.wait_ge(h_sent[1], 16 * 4)
        def ring_of(n):
            return n % 2, n // 2 + 1 + (1 - n % 2)

        def load_stage3(j):
            first = isinstance(j, int)
            for q in range(4):
                gate_col, br_col = at(j * P + (COL_GATE + q * D)), at(j * P)
                if not first or q >= 2:
                    load_block(W3, q, 4, j, w_in[:, :, bass.ds(gate_col, P)])
                if first and q == 0:
                    free_of_s1(sp)
                if first and q >= 2:
                    sp.wait_ge(b_split, q - 1)
                sp.dma_start(bw_raw[q % 2][:, :, :], w_br[:, q, :, bass.ds(br_col, P)]).then_inc(ld_b[q % 2], 16)

        load_stage3(0)
        with sp.Fori(1, KD) as j:
            load_stage3(j)
        w_out = a["w_out"][0].rearrange("(k p) n -> p k n", p=P)

        def load_stage4(i):
            for s in range(2):
                cols = bass.ds(at(i * (2 * P) + s * P), P)
                load_block(W4, s, 2, i, w_out[:, :, cols])
                if isinstance(i, int):
                    sp.wait_ge(merged_done, 3 * KD)
                else:
                    sp.wait_ge(wo_full, i * 2 + (s - 1))
                sp.dma_start(x_res[s][:, 0:NT, :], a["x_prompt"][0].rearrange("(t p) n -> p t n", p=P)
                             [:, :, cols]).then_inc(ld_res[s], 16)
                sp.dma_start(x_res[s][0:NS, NT, :], a["x_sample"].rearrange("b q n -> (b q) n")
                             [:, cols]).then_inc(ld_res[s], 16)

        load_stage4(0)
        sp.dma_start(hist_f[0:NB * FH, :], a["state_ffn_conv"][0].rearrange("b r c -> (b r) c")).then_inc(ld_fh, 16)
        with sp.Fori(1, KD // 2) as i:
            load_stage4(i)
        w_up = a["ffn_up"][0].rearrange("(k p) n -> p k n", p=P)
        w_dn = a["ffn_down"][0].rearrange("(j p) n -> p j n", p=P)

        def load_ffn(f, e, kind, i=0):
            where = at(e) if kind == "d" else at(e * P + (FF if kind == "u" else 0))
            if f == 1 or f == 2:
                sp.wait_ge(w_split, W6 + f - 2)
            elif f >= 3:
                sp.wait_ge(w_split, i * 6 + (W6 + f - 2))
            dst = f_raw[ring_slot(f)]
            if kind == "d":
                src = w_dn[:, bass.ds(where, 1), :].rearrange("p o n -> p (o n)")
                dst = dst[:, :, :].rearrange("p k n -> p (k n)")
            else:
                src = w_up[:, :, bass.ds(where, P)]
                dst = dst[:, :, :]
            sp.dma_start(dst, src).then_inc(ld_f[ring_slot(f)], 16)

        load_ffn(0, 0, "g")
        load_ffn(1, 0, "u")
        load_ffn(2, 1, "g")
        load_ffn(3, 1, "u")
        with sp.Fori(0, NFF // 2 - 1) as i:
            for f, (kind, de) in enumerate((("g", 2), ("u", 2), ("d", 0), ("d", 1), ("g", 3), ("u", 3))):
                load_ffn(4 + f, i * 2 + de, kind, i)
        n_ring = 4 + 6 * (NFF // 2 - 1)
        load_ffn(n_ring, NFF - 2, "d")
        load_ffn(n_ring + 1, NFF - 1, "d")
        sp.wait_ge(cv_taps, 2 * NFF)
        sp.dma_start(gfin, a["final_norm_g"].partition_broadcast(P)).then_inc(ld_gfin, 16)
        sp.wait_ge(fs_ready, len(STATES))
        store(o["ffn_conv_prompt"][0, 0], hist_f[0:FH, :])
        store(o["ffn_conv_sample"][0].rearrange("b r c -> (b r) c"), hist_f[FH:9 * FH, :])
        for t in range(NT + 1):
            sp.wait_ge(y_ready, t + 1)
            dst = o["y_prompt"][0, t * P:(t + 1) * P, :] if t < NT else o["y_sample"].rearrange("b q d -> (b q) d")
            sp.dma_start(dst, y_out[t % 3][0:rows_of(t), :]).then_inc(y_sent[t % 3], 16)
        for n in range(3):
            sp.wait_ge(y_sent[n], 16 * 3)
        for n in range(2):
            sp.wait_ge(k_sent[n], 16 * 3)
        sp.wait_ge(stored, 16 * n_stores[0])

    @block.gpsimd
    def _(gp):
        od = Order(gp, pool_own)
        g = nc.gpsimd
        od.run(g.memset(w_raw[0][:, :, :], 0.0), w_zeroed)
        od.run(g.memset(small[:, :], 0.0), small_zeroed)
        od.run(g.memset(sdt[:, :], 0.0))
        od.run(g.memset(sdt_t[:, :, :], 0.0))
        gp.wait_ge(small_zeroed, 1)
        gp.wait_ge(ld_const, 16)
        gp.wait_ge(vec_done, 1)

        def gate_mark():
            g.tensor_tensor(mark[:, 0:1], eps[:, :], eps[:, :], ALU.add).then_inc(pool_own, 1)
            od.n[pool_own.name] += 1

        def split(raw, hi, lo):
            gate_mark()
            od.run(g.tensor_copy(hi, raw))
            od.run(g.tensor_tensor(lo, raw, hi.bitcast(F32), ALU.subtract), w_split)

        def split_job(n):
            s = n % 2
            count = n // 2 + 1 + (1 if s == 0 else 0)
            gp.wait_ge(ld_w[s], 16 * count)
            if n >= 2:
                slot_filled(gp, JOBS[n - 2][:2])
            split(w_raw[s][:, :, :], w_hi[s][:, :, :], w_lo[s][:, :, :])

        split_job(0)
        split_job(1)
        gp.wait_ge(h_split, NT + 1)
        od.run(g.memset(pw[:, :, :], 0.0))
        od.run(g.memset(p_ext[:, :, 0:PH], 0.0))
        od.run(g.memset(va[:, NT, :], 0.0), a_zeroed)
        for n in range(2, N1A):
            split_job(n)
        split_job(N1A)
        split_job(N1A + 1)
        split_job(N1A + 2)
        free_of_1a(gp)
        od.run(g.memset(q_a[HD:HD + 2, :, :], -1.0))
        od.run(g.memset(k_a[HD:HD + 2, :, :], 1.0), att_zeroed)
        for n in range(N1A + 3, N1B + 2):
            split_job(n)
        free_of_1b(gp)
        od.run(g.memset(x_ext[:, 0:CV], 0.0))
        od.run(g.memset(q_s[:, :, :, :], 0.0), c_zeroed)
        for n in range(N1B + 2, N1C):
            split_job(n)
        free_of_sx(gp)
        gp.wait_ge(xst_ready, 2)
        od.run(g.memset(hst[:, :, :], 0.0))
        od.run(g.memset(ctm, 0.0), d_zeroed)
        gp.wait_ge(ld_d, 16)
        for c in range(NT + 1):
            r = rows_of(c)
            n = c % 2
            pt_drained(gp, ("xb", c))
            if c >= 2:
                gp.wait_ge(ssd_back, c - 1)
                gp.wait_ge(y_gated, c - 1)
            x = xb[n][0:r, 0:256].rearrange("p (h d) -> p h d", h=NH)
            od.run(g.tensor_tensor(xdt[n][0:r], x, sdt_t[0:r, c, 32:32 + NH].unsqueeze(2).to_broadcast([r, NH, HD]),
                                   ALU.mult), xdt_done)
            od.run(g.tensor_tensor(xd[n][0:r], x, d_b[0:r, :].unsqueeze(2).to_broadcast([r, NH, HD]), ALU.mult),
                   xd_done)
            gp.wait_ge(dec_exp, c + 1)
            od.run(g.tensor_tensor(xte[n][0:r], xdt[n][0:r], dec[n][0:r, 1, :].unsqueeze(2)
                                   .to_broadcast([r, NH, HD]), ALU.mult), xte_done)
        for b in range(NB):
            if b >= 2:
                pt_filled(gp, ("sn", b - 2))
            od.run(g.tensor_scalar(xtm[b % 2][:, :], xte[NT % 2][0:NS].rearrange("p h d -> p (h d)"),
                                   const("bsel", slice(0, NS), slice(b, b + 1)), None, ALU.mult), xtm_done)
        def split_block(base, q, per, i):
            n = base + q
            gp.wait_ge(ld_w[n % 2], i * (8 * per) + 16 * (n // 2 + 1 + (1 - n % 2)))
            split(w_raw[n % 2][:, :, :], w_hi[n % 2][:, :, :], w_lo[n % 2][:, :, :])

        def split_stage3(j):
            first = isinstance(j, int)
            for q in range(4):
                def gate_block():
                    if first and q < 2:
                        slot_filled(gp, JOBS[N1C - 2 + q][:2])
                    else:
                        gp.wait_ge(gate_full, j * 4 + (q - 1))
                    split_block(W3, q, 4, j)

                def branch_block(q=q):
                    gp.wait_ge(ld_b[q % 2], j * 32 + 16 * (q // 2 + 1))
                    if not first or q >= 2:
                        gp.wait_ge(br_full, j * 4 + (q - 1))
                    gate_mark()
                    od.run(g.tensor_copy(bw_hi[q % 2][:, :, :], bw_raw[q % 2][:, :, :]))
                    od.run(g.tensor_tensor(bw_lo[q % 2][:, :, :], bw_raw[q % 2][:, :, :], bw_hi[q % 2][:, :, :].bitcast(F32),
                                           ALU.subtract), b_split)

                if first and q < 2:
                    gate_block()
                    if q == 1:
                        free_of_s1(gp)
                        branch_block(0)
                        branch_block(1)
                else:
                    branch_block()
                    gate_block()

        od.peel()
        split_stage3(0)
        with gp.Fori(1, KD) as j:
            od.enter(j, 1)
            split_stage3(j)
        od.leave(KD - 1)

        def split_stage4(i):
            for s in range(2):
                if isinstance(i, int):
                    gp.wait_ge(gate_full, 4 * KD - 1 + s)
                else:
                    gp.wait_ge(wo_full, i * 2 + (s - 1))
                split_block(W4, s, 2, i)

        od.peel()
        split_stage4(0)
        with gp.Fori(1, KD // 2) as i:
            od.enter(i, 1)
            split_stage4(i)
        od.leave(KD // 2 - 1)
        gp.wait_ge(merged_done, 3 * KD)
        od.run(g.memset(ones_m[:, :], 1.0), ones_done)
        def split_ffn(f, i=0):
            n = ring_slot(f)
            gp.wait_ge(ld_f[n], i * 32 + 16 * (f // 3 + 1))
            split(f_raw[n][:, :, :], f_hi[n][:, :, :], f_lo[n][:, :, :])

        split_ffn(0)
        gp.wait_ge(wo_full, KD - 1)
        split_ffn(1)
        gp.wait_ge(wo_full, KD)
        split_ffn(2)
        gp.wait_ge(nm_full, 1)
        od.run(g.memset(ext[0][:, 0:FH], 0.0))
        od.run(g.memset(ext[1][:, 0:FH], 0.0), f_zeroed)
        gp.wait_ge(up_full, 1)
        od.peel()
        split_ffn(3)
        with gp.Fori(0, NFF // 2 - 1) as i:
            od.enter(i, 0, [(pool_own, 12), (w_split, 6)])
            gp.wait_ge(up_full, i * 4 + 3)
            split_ffn(4, i)
            split_ffn(5, i)
            gp.wait_ge(up_full, i * 4 + 4)
            split_ffn(6, i)
            gp.wait_ge(up_full, i * 4 + 5)
            split_ffn(7, i)
            gp.wait_ge(up_full, i * 4 + 6)
            split_ffn(8, i)
            gp.wait_ge(dn_full, i * 24 + 24)
            split_ffn(9, i)
        od.leave(NFF // 2 - 1)
        gp.wait_ge(dn_full, 24 * (NFF // 2 - 1))
        split_ffn(4 + 6 * (NFF // 2 - 1))
        gp.wait_ge(up_full, 2 * NFF - 1)
        split_ffn(5 + 6 * (NFF // 2 - 1))

    @block.scalar
    def _(act):
        od = Order(act, act_own)
        sc = nc.scalar
        act.dma_start(cst[:, :], a["consts"]).then_inc(ld_const, 16)
        rows = [("norm1_g", vec1[0:8, :]), ("norm2_g", vec1[8:16, :]), ("ssd_conv_w", vec1[16:40, :]),
                ("ssd_conv_b", vec1[40:46, :]), ("pool_scale", vec1[46:48, :]), ("ssd_norm_g", vec1[48:50, :]),
                ("ffn_conv_b", vec1[50:94, :])]
        for name, dst in rows:
            src = a[name][0]
            src = src.rearrange("t (b p) -> (t b) p", p=P) if name == "ssd_conv_w" else \
                src.rearrange("(b p) -> b p", p=P)
            act.dma_start(dst, src).then_inc(ld_vec, 16)
        fw = a["ffn_conv_w"][0].rearrange("t (b p) -> (t b) p", p=P)
        act.dma_start(vec2[:, :], fw[0:88, :]).then_inc(ld_vec, 16)
        act.dma_start(vec3[:, :], fw[88:132, :]).then_inc(ld_vec, 16)
        act.wait_ge(small_zeroed, 1)
        act.dma_start(small[0:NH, 0:1], a["fox_bf"].rearrange("a h -> h a")).then_inc(ld_small, 16)
        act.dma_start(small[32:32 + NH, 0:1], a["ssd_dt_bias"].rearrange("a h -> h a")).then_inc(ld_small, 16)
        act.dma_start(small[32:32 + NH, 1:2], a["ssd_a_log"].rearrange("a h -> h a")).then_inc(ld_small, 16)
        act.dma_start(hist_p[:, :], a["state_pool"][0].rearrange("b r c -> (b r) c")).then_inc(ld_hist, 16)
        act.dma_start(hist_x[:, :], a["state_ssd_conv"][0].rearrange("b r c -> (b r) c")).then_inc(ld_hist, 16)

        def h_hi_copy(i):
            r = rows_of(i)
            for half in range(2):
                pt_drained(act, ("x", i, half))
            od.run(sc.activation(h_hi[:, :, i * P:i * P + r], h_f[i % 2][:, :, 0:r], ACT.Copy), h_hi_done)

        act.wait_ge(vec_done, 1)
        def root_mean_square(i):
            r = rows_of(i)
            act.wait_ge(ld_x[i % 3], 16 * (i // 3 + 1))
            od.run(sc.activation(junk[0:r, :], x_tok[i % 3][0:r, :], ACT.Square, accum_out=stat[0:r, 0, i:i + 1]))
            od.run(sc.activation(stat[0:r, 1, i:i + 1], stat[0:r, 0, i:i + 1], ACT.Sqrt, scale=1.0 / D, bias=eps[0:r, :]),
                   x_sq)

        root_mean_square(0)
        for i in range(NT + 1):
            r = rows_of(i)
            act.wait_ge(x_inv, i + 1)
            if i >= 2:
                pt_filled(act, ("x", i - 2, 1))
            od.run(sc.activation(x_scaled[i % 2][0:r, 0:D // 2], x_tok[i % 3][0:r, 0:D // 2], ACT.Copy,
                                 scale=stat[0:r, 2, i:i + 1]), x_half)
            if i < NT:
                root_mean_square(i + 1)
            if i >= 1:
                h_hi_copy(i - 1)
        h_hi_copy(NT)

        act.wait_ge(ld_small, 48)
        od.run(sc.activation(small[32:36, 2:3], small[32:36, 1:2], ACT.Exp), alog_exp)

        def evacuate(job, func, **kw):
            s = job[:2]
            n = ring[s]
            slot_filled(act, s)
            if n >= 2:
                act.wait_ge(stg_free, n - 1)
            r = slice(0, 36) if s[0] == "fdt" else slice(0, P)
            od.run(sc.activation(in_chunks(stg[n % 2][r, :]), chunked(slot[s] % 2, r), func, **kw), free_of(s))

        for job in jobs_a:
            s = job[:2]
            if s[0] == "fdt":
                evacuate(job, ACT.Identity, bias=small[0:36, 0:1])
                act.wait_ge(dk_abs, 1)
                od.run(sc.activation(dk[1][0:36, :], dk[0][0:36, :], ACT.Exp, scale=-1.0), dk_exp)
                act.wait_ge(dk_u, 1)
                od.run(sc.activation(dk[0][0:36, :], dk[2][0:36, :], ACT.Ln), dk_ln)
            elif s[0] == "pool":
                evacuate(job, ACT.Copy)
            elif s[0] == "va":
                evacuate(job, ACT.Gelu_apprx_tanh)
            else:
                slot_filled(act, s)
                od.run(sc.activation(in_chunks(u_f[:, s[1], :]), chunked(slot[s] % 2), ACT.Gelu_apprx_tanh), free_of(s))
        act.wait_ge(a_sum, 1)
        od.run(sc.activation(stat[:, 1, :], stat[:, 0, :], ACT.Sqrt, scale=1.0 / CMW, bias=eps[:, :]), a_rms)
        def evacuate_1b(job):
            evacuate(job, ACT.Copy, scale=HD ** -0.5 if job[0] == "q" else 1.0)

        evacuate_1b(jobs_b[0])
        for b in range(2):
            slot_filled(act, ("mixb", b))
            od.run(sc.activation(in_chunks(y_all[:, 2 + b, :]), chunked(slot[("mixb", b)] % 2), ACT.Copy,
                                 scale=pv[:, PV_PS + b:PV_PS + b + 1]), free_of(("mixb", b)))
        for job in jobs_b[1:]:
            evacuate_1b(job)
        def exponentials(n):
            s = ("att",) + steps[n]
            nk = (steps[n][0] + 1) * P
            act.wait_ge(att_max, n + 1)
            od.run(sc.activation(pr[n % 2][:, 0:nk], flat(slot[s] % 2)[:, 0:nk], ACT.Exp, bias=ast[:, 0, n:n + 1],
                                 accum_out=ast[:, 1, n:n + 1]), free_of(s))

        exponentials(0)
        for n, (qb, h) in enumerate(steps):
            if n + 1 < len(steps):
                exponentials(n + 1)
            if n >= 2:
                act.wait_ge(att_pv, n - 1)
            for k, (lo, hi) in enumerate(quads(qb)):
                key = ("p", n, k)
                pt_filled(act, key)
                od.run(sc.activation(pr_t[n % 2][:, lo:hi, :], pt_of(key)[:, 0:(hi - lo) * P].rearrange(
                    "p (t q) -> p t q", q=P), ACT.Copy), ptf_of(key))
        def xbc_act(b):
            act.wait_ge(x_conv, b + 1)
            od.run(sc.activation(xc[:, b, 0:SEQ], x_cv[:, 0:SEQ], ACT.Silu))
            od.run(sc.activation(xc[:, b, SEQ:T].rearrange("p (s n) -> p s n", s=NB),
                                 x_new(x_cv), ACT.Silu), x_act)

        free_of_1b(act)
        def evacuate_1c(n):
            evacuate(jobs_c[n], ACT.Silu if jobs_c[n][0] == "z" else ACT.Copy)

        for n in range(NB):
            if n >= 1:
                evacuate_1c(n - 1)
            key = ("sk", n)
            pt_filled(act, key)
            if n >= 1:
                pt_filled(act, ("ss", n - 1))
            od.run(sc.activation(kt_s[:, :, :], pt_of(key)[:, :].rearrange("p (k n) -> p k n", k=2), ACT.Copy),
                   ptf_of(key))
            if n >= 2:
                xbc_act(n - 2)
            act.wait_ge(ss_max, n + 1)
            if n >= 1:
                pt_filled(act, ("sp", n - 1))
            od.run(sc.activation(p_s[:, :], pt_of(("ss", n))[0:NH * NQ, 0:PAST + NS], ACT.Exp,
                                 bias=ast[0:NH * NQ, 0, n:n + 1], accum_out=ast[0:NH * NQ, 1, n:n + 1]),
                   ptf_of(("ss", n)))
            key = ("sp", n)
            pt_filled(act, key)
            if n >= 1:
                pt_filled(act, ("so", n - 1))
            od.run(sc.activation(pt_s[:, 0:2, :], pt_of(key)[:, 0:32].rearrange("p (k n) -> p k n", k=2), ACT.Copy))
            od.run(sc.activation(pt_s[0:NS, 2, :], pt_of(key)[0:NS, 32:48], ACT.Copy), ptf_of(key))
        evacuate_1c(NB - 1)
        free_of_sx(act)
        od.run(sc.activation(eacs[:, :, :], sdt_t[:, :, 64:64 + NH], ACT.Exp), eacs_done)
        for c in range(NT + 1):
            s = ("ssd", c)
            r = rows_of(c)
            n = c % 2
            key = ("xb", c)
            pt_filled(act, key)
            if c >= 2:
                act.wait_ge(ssd_back, c - 1)
                act.wait_ge(xte_done, c - 1)
            od.run(sc.activation(xb[n][0:r, :], pt_of(key)[0:r, :], ACT.Copy), ptf_of(key))
            slot_filled(act, s)
            act.wait_ge(seg_in, c + 1)
            bc = ps[slot[s] % 2][:, 1, :].rearrange("p (h t) -> p h t", h=NH)
            if c < NT:
                od.run(sc.activation(dec[n][:, 2, :], bc[:, :, P - 1], ACT.Exp))
            else:
                od.run(sc.activation(sdec[:, :, :], ps[slot[s] % 2][:, 1, 100:116].rearrange("p (g b) -> p g b", g=2),
                                     ACT.Exp), sdec_done)
            od.run(sc.activation(dec[n][0:r, 1, :], dec[n][0:r, 0, :], ACT.Exp), dec_exp)
            od.run(sc.activation(seg[n][0:r, :, 0:r], seg[n][0:r, :, 0:r], ACT.Exp), seg_exp)
        for b in range(NB):
            key = ("sh", b)
            pt_filled(act, key)
            if b >= 2:
                pt_filled(act, ("sn", b - 1))
            od.run(sc.activation(h0t[b % 2][:, :, :], pt_of(key)[:, 0:256].rearrange("p (g n) -> p g n", g=2), ACT.Copy),
                   ptf_of(key))
        act.wait_ge(y_gated, NT + 1)
        od.run(sc.activation(stat[:, 1, :], stat[:, 0, :], ACT.Sqrt, scale=1.0 / 256, bias=eps[:, :]), d_rms)
        def gates(j, which=range(4)):
            for q in which:
                act.wait_ge(gate_full, j * 4 + (q + 1))
                if q == 1:
                    act.wait_ge(br_read, j * 4 + 1)
                elif q >= 2:
                    act.wait_ge(merged_done, j * 3 + (q - 1))
                elif not isinstance(j, int):
                    act.wait_ge(merged_done, j * 3)
                od.run(sc.activation(in_chunks(sg[:, :]), chunked(0), ACT.Sigmoid), sg_ready)

        free_of_s1(act)
        for b in range(KD):
            if b == 3:
                gates(0, [0])
            od.run(sc.activation(y_hi[:, b, :], y_all[:, b, :], ACT.Copy), y_hi_done)
        od.peel()
        gates(0, [1, 2, 3])
        with act.Fori(1, KD) as j:
            od.enter(j, 1, [(sg_ready, 4)])
            gates(j)
        od.leave(KD - 1)
        act.wait_ge(gate_full, 4 * KD)
        for k in range(KD):
            act.wait_ge(merged_done, 3 * (k + 1))
            od.run(sc.activation(h_hi[:, k, :], merged[:, k, :], ACT.Copy), m_hi_done)

        def residual(i, blocks=range(2)):
            for s in blocks:
                act.wait_ge(wo_full, i * 2 + (s + 1))
                x1_block = x1[:, bass.ds(i * 2 + s, 1), :].rearrange("p o n -> p (o n)")
                od.run(sc.activation(in_chunks(x1_block), chunked(s), ACT.Copy))
                if not isinstance(i, int) or i + s > 0:
                    act.wait_ge(ssq_done, i * 2 + s)
                od.run(sc.activation(in_chunks(sq[:, :]), chunked(s), ACT.Square), wo_read)

        od.peel()
        residual(0)
        with act.Fori(1, KD // 2 - 1) as i:
            od.enter(i, 1)
            residual(i)
        od.leave(KD // 2 - 2)
        residual(KD // 2 - 1, [0])
        act.wait_ge(merged_used, KD)
        for k in range(KD):
            if k == EARLY_H2:
                residual(KD // 2 - 1, [1])
            od.run(sc.activation(h_hi[:, k, :], x1[:, k, :], ACT.Copy, scale=pv[:, PV_G2 + k:PV_G2 + k + 1]), h2_hi_done)
        act.wait_ge(nm_full, 1)
        od.run(sc.activation(in_chunks(rstd), chunked(1), ACT.Sqrt, scale=1.0 / D, bias=eps[:, :]), nm_rms)
        for n in range(2):
            act.wait_ge(fh_full, n + 1)
            src = pt[n][:, 0:NFF * NB * FH].rearrange("p (b n) -> p b n", b=NFF)
            od.run(sc.activation(fh[:, n * NFF:(n + 1) * NFF, :], src, ACT.Copy), fh_done)
        def param(col, e):
            return pv[:, bass.ds(e + col, 1)]

        def ffn_front(e, s, i, first):
            for k, blk in ffn_kinds(e):
                if first:
                    act.wait_ge(f_zeroed, 1)
                else:
                    act.wait_ge(cv_taps, i * 4 + (2 * s + k - 1))
                x = ext[k]
                new = x[:, FH + SEQ:FE_W].rearrange("p (s n) -> p s n", s=NB)
                od.run(sc.activation(new[:, :, 0:FH], fh[:, bass.ds(blk, 1), :].rearrange("p o (s n) -> p (o s) n", s=NB),
                                     ACT.Copy))
                act.wait_ge(up_read, i * 4 + (2 * s + k + 1))
                if not first:
                    act.wait_ge(act_split, i * 2 + s)
                od.run(sc.activation(cv[k][:, 0:FE_W - FH], x[:, 0:FE_W - FH], ACT.Identity, scale=param(PV_FW, blk),
                                     bias=param(PV_FB, blk)), cv0_done)
            act.wait_ge(cv_taps, i * 4 + (2 * s + 1))
            od.run(sc.activation(cv[0][:, 0:FE_W - FH], cv[0][:, 0:FE_W - FH], ACT.Silu), silu_done)

        def ffn_upper(s, i, downs):
            act.wait_ge(prod_done, i * 2 + (s + 1))
            if downs is not None:
                act.wait_ge(dn_full, downs)
            for n, (dst, src) in enumerate(zip(packed(act_hi[:, s, :]), spaced(cv[0]))):
                od.run(sc.activation(dst, src, ACT.Copy), act_hi_done if n == 1 else None)

        od.peel()
        for s in range(2):
            ffn_front(s, s, 0, s == 0)
            ffn_upper(s, 0, None)
        with act.Fori(1, NFF // 2 - 1) as i:
            od.enter(i, 1)
            for s in range(2):
                ffn_front(i * 2 + s, s, i, False)
                ffn_upper(s, i, i * 24)
        od.leave(NFF // 2 - 2)

        def ffn_state(n):
            act.wait_ge(out_full, n + 1)
            at = 0
            for lo, hi in STATES[n]:
                w = (hi - lo) * P
                od.run(sc.activation(hist_f[:, lo * P:hi * P], flat(n % 2)[0:9 * FH, at:at + w], ACT.Copy),
                       (out_free[n % 2], n // 2 + 1) if hi == STATES[n][-1][1] else None)
                at += w
            od.run(sc.activation(mark[:, 1:2], eps[:, :], ACT.Copy), fs_ready)

        last = NFF // 2 - 1
        ffn_front(2 * last, 0, last, False)
        ffn_upper(0, last, last * 24)
        ffn_front(2 * last + 1, 1, last, False)
        ffn_state(0)
        ffn_state(1)
        ffn_upper(1, last, last * 24)
        for n in range(2, len(STATES)):
            ffn_state(n)
        for t in range(NT + 1):
            r = rows_of(t)
            n = len(STATES) + t
            act.wait_ge(out_full, n + 1)
            act.wait_ge(act_split, NFF)
            od.run(sc.activation(squares[0:r, :], flat(n % 2)[0:r, 0:D], ACT.Square, accum_out=stat7[0:r, 0, t:t + 1]))
            od.run(sc.activation(stat7[0:r, 1, t:t + 1], stat7[0:r, 0, t:t + 1], ACT.Sqrt, scale=1.0 / D, bias=eps[0:r, :]),
                   y_sq)

    @block.vector
    def _(dve):
        od = Order(dve, dve_own)
        v = nc.vector
        od.run(v.memset(eps[:, :], EPS), vec_done)
        pt_filled(dve, ("vec",))
        od.run(v.tensor_copy(pv[:, :], pt_of(("vec",))[:, 0:PV_N]), ptf_of(("vec",)))
        pt_filled(dve, ("hist",))
        od.run(v.tensor_copy(hist_t[:, :], pt_of(("hist",))[:, 0:384]), ptf_of(("hist",)))
        hist_x_t = hist_t[:, 0:144].rearrange("p (b n) -> p b n", b=6)
        hist_p_t = hist_t[:, 144:384].rearrange("p (b n) -> p b n", b=2)

        def h_full(i):
            r = rows_of(i)
            for half in range(2):
                key, ks = ("x", i, half), slice(4 * half, 4 * half + 4)
                pt_filled(dve, key)
                src = pt_of(key)[:, :].rearrange("p (k n) -> p k n", k=4)[:, :, 0:r]
                od.run(v.tensor_tensor(h_f[i % 2][:, ks, 0:r], src, pv[:, PV_G1 + 4 * half:PV_G1 + 4 * half + 4].unsqueeze(2)
                                       .to_broadcast([P, 4, r]), ALU.mult), ptf_of(key))

        def h_lower(i):
            tok = slice(i * P, i * P + rows_of(i))
            dve.wait_ge(h_hi_done, i + 1)
            od.run(v.tensor_tensor(h_lo[:, :, tok], h_f[i % 2][:, :, 0:rows_of(i)], h_hi[:, :, tok].bitcast(F32),
                                   ALU.subtract), h_split)

        def inverse(i):
            r = rows_of(i)
            dve.wait_ge(x_sq, i + 1)
            od.run(v.reciprocal(stat[0:r, 2, i:i + 1], stat[0:r, 1, i:i + 1]), x_inv)

        inverse(0)
        for i in range(NT + 1):
            r = rows_of(i)
            od.run(v.tensor_scalar(x_scaled[i % 2][0:r, D // 2:D], x_tok[i % 3][0:r, D // 2:D], stat[0:r, 2, i:i + 1],
                                   None, ALU.mult), x_normed)
            if i >= 1:
                h_full(i - 1)
            if i < NT:
                inverse(i + 1)
            if i >= 1:
                h_lower(i - 1)
        h_full(NT)
        h_lower(NT)

        s = ("fdt", 0)
        raw = stg[0]
        slot_drained(dve, s)
        od.run(v.scalar_tensor_tensor(dk[0][0:36, :], raw[0:36, :], -1.0, raw[0:36, :], ALU.mult, ALU.max), dk_abs)
        dve.wait_ge(dk_exp, 1)
        od.run(v.tensor_scalar(dk[2][0:36, :], dk[1][0:36, :], 1.0, None, ALU.add), dk_u)
        od.run(v.tensor_scalar(dk[3][0:36, :], dk[2][0:36, :], 1.0, None, ALU.subtract))
        od.run(v.tensor_tensor(dk[3][0:36, :], dk[1][0:36, :], dk[3][0:36, :], ALU.subtract))
        dve.wait_ge(dk_ln, 1)
        od.run(v.reciprocal(dk[2][0:36, :], dk[2][0:36, :]))
        od.run(v.tensor_tensor(dk[3][0:36, :], dk[3][0:36, :], dk[2][0:36, :], ALU.mult))
        od.run(v.tensor_tensor(dk[3][0:36, :], dk[3][0:36, :], dk[0][0:36, :], ALU.add))
        od.run(v.scalar_tensor_tensor(sdt[0:NH, :], raw[0:NH, :], 0.0, dk[3][0:NH, :], ALU.min, ALU.subtract))
        dtr = slice(32, 32 + NH)
        od.run(v.scalar_tensor_tensor(sdt[dtr, :], raw[dtr, :], 0.0, dk[3][dtr, :], ALU.max, ALU.add), stg_free)
        dve.wait_ge(alog_exp, 1)
        od.run(v.tensor_scalar(small[dtr, 3:4], small[dtr, 2:3], -1.0, None, ALU.mult))
        od.run(v.tensor_scalar(dk[0][dtr, :], sdt[dtr, :], small[dtr, 3:4], None, ALU.mult))
        od.run(v.memset(dk[1][dtr, :], 1.0))
        od.run(v.memset(dk[1][dtr, 0:SEQ].rearrange("p (c t) -> p c t", t=P)[:, :, 0:1], 0.0))
        od.run(v.memset(dk[1][dtr, SEQ:T].rearrange("p (c t) -> p c t", t=NQ)[:, :, 0:1], 0.0))
        od.run(v.tensor_tensor_scan(sdt[64:64 + NH, :], dk[1][dtr, :], dk[0][dtr, :], 0.0, ALU.mult, ALU.add))
        od.run(v.memset(dk[2][0:NH, 0:SEQ], 1.0))
        od.run(v.tensor_tensor_scan(sdt[96:96 + NH, 0:SEQ], dk[2][0:NH, 0:SEQ], sdt[0:NH, 0:SEQ], 0.0,
                                    ALU.mult, ALU.add), sdt_done)
        dve.wait_ge(a_zeroed, 1)
        for b in range(2):
            n = ring[("pool", b)]
            slot_drained(dve, ("pool", b))
            od.run(v.tensor_copy(p_ext[:, b, PH:PH + SEQ], stg[n % 2][:, 0:SEQ]))
            od.run(v.tensor_copy(p_ext[:, b, PH + SEQ:PE_W].rearrange("p (s n) -> p s n", s=NB)[:, :, PH:PH + NQ],
                                 stg[n % 2][:, SEQ:T].rearrange("p (s n) -> p s n", s=NB)), stg_free)
            od.run(v.tensor_copy(p_ext[:, b, PH + SEQ:PE_W].rearrange("p (s n) -> p s n", s=NB)[:, :, 0:PH],
                                 hist_p_t[:, b, :].rearrange("p (s n) -> p s n", s=NB)))
        for b in range(2):
            src = p_ext[:, b, SEQ:SEQ + 9 * (PH + NQ)].rearrange("p (s n) -> p s n", s=9)[:, :, 0:PH]
            od.run(v.tensor_copy(p_state[:, b, :].rearrange("p (s n) -> p s n", s=9), src), pstate_in)
        for n, (lo, hi) in enumerate(((0, 5), (5, 9))):
            pt_filled(dve, ("sdt", n))
            src = pt_of(("sdt", n))[:, 0:500].rearrange("p (t c) -> p t c", c=100)
            if n == 0:
                od.run(v.tensor_copy(sdt_t[:, 0:5, :], src), ptf_of(("sdt", n)))
            else:
                od.run(v.tensor_copy(sdt_t[:, 5:8, :], src[:, 0:3, :]))
                od.run(v.tensor_copy(sdt_t[0:NS, 8, :], src[0:NS, 3, :]), ptf_of(("sdt", n)))
        od.run(v.tensor_tensor(win_a[:, :, 1:PE_W], p_ext[:, :, 1:PE_W], p_ext[:, :, 0:PE_W - 1], ALU.add))
        od.run(v.tensor_tensor(win_b[:, :, 3:PE_W], win_a[:, :, 3:PE_W], win_a[:, :, 1:PE_W - 2], ALU.add))

        def pooled(blk, half, win, src):
            r = slice(64 * half, 64 * half + 64)
            fix = const("pfix", r).rearrange("p (b n) -> p b n", b=2)[:, blk, :]
            od.run(v.tensor_tensor(src[r, blk, PH:2 * PH], src[r, blk, PH:2 * PH], fix, ALU.mult))
            return v.scalar_tensor_tensor(p_ext[r, blk, PH:PE_W], src[r, blk, PH:PE_W], 1.0 / win,
                                          p_ext[r, blk, PH:PE_W], ALU.mult, ALU.subtract)

        dve.wait_ge(pstate_in, 2)
        od.run(pooled(0, 0, WINDOWS[0], win_a))
        od.run(pooled(0, 1, WINDOWS[1], win_b))
        od.run(v.tensor_tensor(win_a[:, 1, 7:PE_W], win_b[:, 1, 7:PE_W], win_b[:, 1, 3:PE_W - 4], ALU.add))
        od.run(v.tensor_tensor(win_b[:, 1, 15:PE_W], win_a[:, 1, 15:PE_W], win_a[:, 1, 7:PE_W - 8], ALU.add))
        od.run(pooled(1, 0, WINDOWS[2], win_a))
        od.run(pooled(1, 1, WINDOWS[3], win_b), pd_done)
        for b in range(2):
            for n, (lo, hi) in enumerate(THIRDS):
                key = ("va", b, n)
                pt_filled(dve, key)
                src = pt_of(key)[:, :].rearrange("p (t c) -> p t c", c=P)
                r = P if hi <= NT else NS
                od.run(v.tensor_copy(va[0:r, lo:hi, b * P:(b + 1) * P], src[0:r, 0:hi - lo, :]), ptf_of(key))
            od.run(v.memset(stat[:, 3, 0:1], 0.0), stg_free)
        for t in range(NT + 1):
            ins = v.tensor_tensor_reduce(out=pjunk, in0=va[:, t, :], in1=va[:, t, :], scale=1.0, scalar=0.0,
                                         op0=ALU.mult, op1=ALU.add, accum_out=stat[:, 0, t:t + 1])
            od.run(ins, a_sum if t == NT else None)
        pt_filled(dve, ("ws",))
        od.run(v.tensor_tensor(wst, pt_of(("ws",))[:, :].rearrange("p (g t) -> p g t", g=4),
                               const("tri01").unsqueeze(1).to_broadcast([P, 4, P]), ALU.mult), ptf_of(("ws",)))
        pt_filled(dve, ("wsm",))
        od.run(v.tensor_tensor(wsm, pt_of(("wsm",))[0:NS, 0:4 * NS].rearrange("p (g t) -> p g t", g=4),
                               const("blk01", slice(0, NS)).unsqueeze(1).to_broadcast([NS, 4, NS]), ALU.mult),
               ptf_of(("wsm",)))
        dve.wait_ge(a_rms, 1)
        od.run(v.reciprocal(stat[:, 2, :], stat[:, 1, :]))
        for t in range(NT + 1):
            od.run(v.scalar_tensor_tensor(va[:, t, :], va[:, t, :], stat[:, 2, t:t + 1], cmg, ALU.mult, ALU.mult),
                   va_done if t == NT else None)
        for n in range(2):
            pt_filled(dve, ("pstate", n))
            k = (5 - n) * PH
            od.run(v.tensor_copy(p_out[0:k, n, :], pt_of(("pstate", n))[0:k, 0:2 * P]), ptf_of(("pstate", n)))
            od.run(v.memset(stat[:, 3, 0:1], 0.0), pstate_out)
        for b in range(2):
            s = ("mixa", b)
            slot_filled(dve, s)
            od.run(v.tensor_tensor(y_all[:, b, 0:SEQ], flat(slot[s] % 2)[:, 0:SEQ], u_f[:, b, 0:SEQ], ALU.mult))
            od.run(v.tensor_tensor(y_all[:, b, SEQ:T], flat(slot[s] % 2)[:, SEQ:T], u_f[:, b, SEQ:T], ALU.mult),
                   free_of(s))
        free_of_1a(dve)
        od.run(v.tensor_tensor(lf_new[:, :].rearrange("p (b h) -> p b h", b=NB),
                               sdt_t[0:NS, NT, 0:NH].unsqueeze(1).to_broadcast([NS, NB, NH]),
                               const("bmask", slice(0, NS)).rearrange("p (b h) -> p b h", b=NB), ALU.mult), clog_in)
        od.run(v.tensor_copy(ident_r[:, :], ident))
        od.run(v.tensor_copy(attneg_r[:, :], const("attneg")))
        for b in range(2):
            n = ring[("q", b)]
            slot_drained(dve, ("q", b))
            for half in range(2):
                r = slice(64 * half, 64 * half + 64)
                od.run(v.tensor_copy(q_a[0:HD, 2 * b + half, :], stg[n % 2][r, 0:SEQ]))
            od.run(v.tensor_copy(qs_new[:, b, :], stg[n % 2][:, SEQ:T]), stg_free)
        for b in range(2):
            n = ring[("k", b)]
            slot_drained(dve, ("k", b))
            for half in range(2):
                r = slice(64 * half, 64 * half + 64)
                od.run(v.tensor_copy(k_a[0:HD, 2 * b + half, :], stg[n % 2][r, 0:SEQ]))
            od.run(v.tensor_copy(ks_new[:, b, :], stg[n % 2][:, SEQ:T]), qk_ready)
            for m, (lo, hi) in enumerate(THIRDS):
                key = ("k", b, m)
                j = 3 * b + m
                pt_filled(dve, key)
                if j >= 2:
                    dve.wait_ge(k_sent[j % 2], 16 * (j // 2))
                r = P if hi <= NT else NS
                src = pt_of(key)[:, :].rearrange("p (t c) -> p t c", c=P)
                od.run(v.tensor_copy(k_out[j % 2][0:r, 0:hi - lo, :], src[0:r, 0:hi - lo, :]), ptf_of(key))
                od.run(v.memset(stat[:, 3, 0:1], 0.0), k_ready)
            od.run(v.memset(stat[:, 3, 0:1], 0.0), stg_free)

        def turned(kind, b, dst):
            for m, (lo, hi) in enumerate(THIRDS):
                key = (kind, b, m)
                pt_filled(dve, key)
                r = P if hi <= NT else NS
                src = pt_of(key)[:, :].rearrange("p (t c) -> p t c", c=P)
                od.run(v.tensor_copy(dst[0:r, lo:hi, b * P:(b + 1) * P], src[0:r, 0:hi - lo, :]), ptf_of(key))

        turned("v", 0, v_tok)
        od.run(v.memset(stat[:, 3, 0:1], 0.0), stg_free)
        turned("v", 1, v_tok)
        od.run(v.memset(stat[:, 3, 0:1], 0.0), stg_free)
        od.run(v.tensor_copy(vs_new[:, :], v_tok[0:NS, NT, :]), v_done)

        def att_maximum(n):
            qb, h = steps[n]
            s = ("att", qb, h)
            slot_filled(dve, s)
            od.run(v.reduce_max(ast[:, 2, n:n + 1], flat(slot[s] % 2)[:, 0:(qb + 1) * P], AX.X))
            od.run(v.tensor_scalar(ast[:, 0, n:n + 1], ast[:, 2, n:n + 1], -1.0, None, ALU.mult), att_max)

        def normalize(n):
            nk = (steps[n][0] + 1) * P
            slot_drained(dve, ("att",) + steps[n])
            od.run(v.reciprocal(ast[:, 2, n:n + 1], ast[:, 1, n:n + 1]))
            od.run(v.tensor_scalar(pr[n % 2][:, 0:nk], pr[n % 2][:, 0:nk], ast[:, 2, n:n + 1], None, ALU.mult), att_norm)

        def att_output(n):
            qb, h = steps[n]
            r = slice(64 * (h % 2), 64 * (h % 2) + 64)
            dve.wait_ge(att_pv, n + 1)
            od.run(v.tensor_copy(y_all[r, 4 + h // 2, qb * P:(qb + 1) * P], ps[slot[("att", qb, h)] % 2][r, 2, 0:P]), att_out)

        att_maximum(0)
        key = ("clog",)
        pt_filled(dve, key)
        od.run(v.tensor_tensor_scan(c_s[:, :], const("ones", slice(0, NS)).to_broadcast([NS, PAST + NQ]),
                                    pt_of(key)[0:NS, 0:PAST + NQ], 0.0, ALU.mult, ALU.add), ptf_of(key))
        od.run(v.tensor_scalar(nc_s[:, 0:PAST], c_s[:, 0:PAST], -1.0, None, ALU.mult))
        od.run(v.tensor_scalar(nc_s[:, PAST:PAST + NS].rearrange("p (b q) -> p b q", b=NB),
                               c_s[:, PAST:PAST + NQ].unsqueeze(1).to_broadcast([NS, NB, NQ]), -1.0, None, ALU.mult))
        od.run(v.tensor_tensor(cq_s[:, :].rearrange("p (r q) -> p r q", q=NQ),
                               const("expand", slice(0, NS)).rearrange("p (r q) -> p r q", q=NQ),
                               c_s[:, PAST:PAST + NQ].unsqueeze(1).to_broadcast([NS, NS, NQ]), ALU.mult), clog_done)
        for n in range(len(steps)):
            normalize(n)
            if n + 1 < len(steps):
                att_maximum(n + 1)
            if n >= 1:
                att_output(n - 1)
        att_output(len(steps) - 1)
        free_of_1b(dve)
        dve.wait_ge(c_zeroed, 1)
        for h in range(NH):
            r = slice(64 * (h % 2), 64 * (h % 2) + 64)
            od.run(v.tensor_copy(q_s[r, h // 2, :, h * NQ:(h + 1) * NQ],
                                 qs_new[r, h // 2, :].rearrange("p (b q) -> p b q", b=NB)), sx_ready)
        def sample_out(n):
            key = ("so", n)
            pt_filled(dve, key)
            for h in range(NH):
                r = slice(64 * (h % 2), 64 * (h % 2) + 64)
                col = (h // 2) * NH * NQ + h * NQ
                od.run(v.tensor_copy(y_all[r, 4 + h // 2, SEQ + n * NQ:SEQ + (n + 1) * NQ], pt_of(key)[r, col:col + NQ]),
                       ptf_of(key) if h == NH - 1 else None)

        def convolve(b):
            n = ring[("xbc", b)]
            slot_drained(dve, ("xbc", b))
            od.run(v.tensor_copy(x_ext[:, CV:CV + SEQ], stg[n % 2][:, 0:SEQ]))
            tail = x_ext[:, CV + SEQ:XE_W].rearrange("p (s n) -> p s n", s=NB)
            od.run(v.tensor_copy(tail[:, :, CV:CV + NQ], stg[n % 2][:, SEQ:T].rearrange("p (s n) -> p s n", s=NB)), stg_free)
            od.run(v.tensor_copy(tail[:, :, 0:CV], hist_x_t[:, b, :].rearrange("p (s n) -> p s n", s=NB)))
            last = x_ext[:, SEQ:SEQ + 9 * (CV + NQ)].rearrange("p (s n) -> p s n", s=9)[:, :, 0:CV]
            od.run(v.tensor_copy(xstate[:, b, :].rearrange("p (s n) -> p s n", s=9), last), xstate_in)
            if b >= 1:
                dve.wait_ge(x_act, b)
            w = XE_W - CV

            def tap(j):
                return pv[:, PV_CW + 6 * j + b:PV_CW + 6 * j + b + 1]

            od.run(v.tensor_scalar(x_cv[:, 0:w], x_ext[:, 0:w], tap(0), pv[:, PV_CB + b:PV_CB + b + 1],
                                   ALU.mult, ALU.add))
            for j in range(1, CV + 1):
                od.run(v.scalar_tensor_tensor(x_cv[:, 0:w], x_ext[:, j:j + w], tap(j), x_cv[:, 0:w], ALU.mult, ALU.add),
                       x_conv if j == CV else None)

        for n in range(NB):
            if n >= 1:
                sample_out(n - 1)
            if n < NB:
                key = ("ss", n)
                pt_filled(dve, key)
                rs = slice(0, NH * NQ)
                od.run(v.reduce_max(ast[rs, 2, n:n + 1], pt_of(key)[rs, 0:PAST + NS], AX.X))
                od.run(v.tensor_scalar(ast[rs, 0, n:n + 1], ast[rs, 2, n:n + 1], -1.0, None, ALU.mult), ss_max)
                pt_drained(dve, key)
                od.run(v.reciprocal(ast[rs, 2, n:n + 1], ast[rs, 1, n:n + 1]))
                od.run(v.tensor_scalar(p_s[:, :], p_s[:, :], ast[rs, 2, n:n + 1], None, ALU.mult), ss_done)
            if 1 <= n <= 6:
                convolve(n - 1)
            if n == NB - 1:
                turned("z", 0, zt)
                od.run(v.memset(stat[:, 3, 0:1], 0.0), stg_free)
        sample_out(NB - 1)
        turned("z", 1, zt)
        od.run(v.memset(stat[:, 3, 0:1], 0.0), stg_free)
        for n, (lo, hi) in enumerate(((0, 4), (4, 6))):
            key = ("xst", n)
            pt_filled(dve, key)
            od.run(v.tensor_copy(xst_out[:, lo * P:hi * P], pt_of(key)[0:9 * CV, 0:(hi - lo) * P]), ptf_of(key))
            od.run(v.memset(stat[:, 3, 0:1], 0.0), xst_ready)

        free_of_sx(dve)

        def decays(c):
            s = ("ssd", c)
            r = rows_of(c)
            n = c % 2
            slot_filled(dve, s)
            if c >= 2:
                dve.wait_ge(ssd_back, c - 1)
            bc = ps[slot[s] % 2][:, 1, :].rearrange("p (h t) -> p h t", h=NH)
            mask = const("ssdneg") if c < NT else const("blkneg", slice(0, NS))
            own = sdt_t[0:r, c, 64:64 + NH]
            last = bc[:, :, P - 1] if c < NT else ps[slot[s] % 2][0:NS, 0, 256:260]
            od.run(v.tensor_tensor(dec[n][0:r, 0, :], last, own, ALU.subtract))
            for h in range(NH):
                od.run(v.scalar_tensor_tensor(seg[n][0:r, h, 0:r], bc[0:r, h, 0:r], own[:, h:h + 1], mask,
                                              ALU.subtract, ALU.min), seg_in if h == NH - 1 else None)

        def new_state(b):
            key = ("sn", b)
            pt_filled(dve, key)
            dve.wait_ge(sdec_done, 1)
            if b >= 2:
                dve.wait_ge(h_sent[b % 2], 16 * (b // 2))
            for g in range(2):
                od.run(v.scalar_tensor_tensor(h_out[b % 2][:, g, :], h0[b % 2][:, g, :], sdec[:, g, b:b + 1],
                                              pt_of(key)[:, g * P:(g + 1) * P], ALU.mult, ALU.add),
                       ptf_of(key) if g == 1 else None)
            od.run(v.memset(stat[:, 3, 0:1], 0.0), h_ready)

        decays(0)
        for c in range(NT + 1):
            s = ("ssd", c)
            r = rows_of(c)
            n = c % 2
            dst = ps[slot[s] % 2]
            dve.wait_ge(seg_exp, c + 1)
            cb = dst[0:r, 0, 0:256].rearrange("p (g t) -> p g t", g=2)[:, :, 0:r].unsqueeze(2).to_broadcast([r, 2, 2, r])
            decay = seg[n][0:r, :, 0:r].rearrange("p (g h) t -> p g h t", g=2)
            od.run(v.tensor_tensor(decay, decay, cb, ALU.mult), seg_cb)
            if c + 1 <= NT:
                decays(c + 1)
            dve.wait_ge(ssd_back, c + 1)
            y_off, y_diag = (dst[0:r, 2, 256 * k:256 * k + 256].rearrange("p (h d) -> p h d", h=NH) for k in range(2))
            if c < NT:
                od.run(v.tensor_tensor(hst[:, :, :], hst[:, :, :], dec[n][:, 2, :].unsqueeze(2)
                                       .to_broadcast([P, NH, HD]), ALU.mult))
                od.run(v.tensor_tensor(hst[:, :, :], hst[:, :, :], dst[:, 0, 256:512].rearrange(
                    "p (h d) -> p h d", h=NH), ALU.add), h_next)
            dve.wait_ge(xd_done, c + 1)
            dve.wait_ge(eacs_done, 1)
            od.run(v.tensor_tensor(xd[n][0:r], xd[n][0:r], y_diag, ALU.add))
            od.run(v.tensor_tensor(yoff[0:r], y_off, eacs[0:r, c, :].unsqueeze(2).to_broadcast([r, NH, HD]), ALU.mult),
                   free_of(s))
            od.run(v.tensor_tensor(xd[n][0:r], xd[n][0:r], yoff[0:r], ALU.add))
            gated = zt[0:r, c, :].rearrange("p (h d) -> p h d", h=NH)
            od.run(v.tensor_tensor(gated, gated, xd[n][0:r], ALU.mult))
            od.run(v.tensor_tensor_reduce(out=yoff[0:r].rearrange("p h d -> p (h d)"), in0=zt[0:r, c, :], in1=zt[0:r, c, :],
                                          scale=1.0, scalar=0.0, op0=ALU.mult, op1=ALU.add,
                                          accum_out=stat[0:r, 0, c:c + 1]), y_gated)
            if c == NT - 1:
                dve.wait_ge(d_zeroed, 1)
                for g in range(2):
                    for b in range(NB):
                        od.run(v.tensor_copy(ctm[:, g, b, b * NQ:(b + 1) * NQ], xc[:, 4 + g, SEQ + b * NQ:SEQ + (b + 1) * NQ]),
                               ctm_done)
                for b in range(NB):
                    new_state(b)
        key = ("hp",)
        pt_filled(dve, key)
        dve.wait_ge(h_sent[0], 16 * 4)
        od.run(v.tensor_copy(h_out[0], pt_of(key)[:, 0:256].rearrange("p (g k) -> p g k", g=2)), ptf_of(key))
        od.run(v.memset(stat[:, 3, 0:1], 0.0), h_ready)
        dve.wait_ge(d_rms, 1)
        od.run(v.reciprocal(stat[:, 2, :], stat[:, 1, :]))
        for t in range(NT + 1):
            r = rows_of(t)
            od.run(v.tensor_scalar(zt[0:r, t, :], zt[0:r, t, :], stat[0:r, 2, t:t + 1], None, ALU.mult), yd_ready)
        for t in range(NT + 1):
            r = rows_of(t)
            key = ("yd", t)
            pt_filled(dve, key)
            od.run(v.tensor_tensor(y_all[:, 6:8, t * P:t * P + r],
                                   pt_of(key)[:, 0:256].rearrange("p (b t) -> p b t", b=2)[:, :, 0:r],
                                   pv[:, PV_SG:PV_SG + 2].unsqueeze(2).to_broadcast([P, 2, r]), ALU.mult), ptf_of(key))
        for b in range(KD):
            dve.wait_ge(y_hi_done, b + 1)
            od.run(v.tensor_tensor(y_lo[:, b, :], y_all[:, b, :], y_hi[:, b, :].bitcast(F32), ALU.subtract), y_split)

        def merge(j):
            for q in range(4):
                dst = merged[:, bass.ds(j, 1), :].rearrange("p o n -> p (o n)")
                dve.wait_ge(br_full, j * 4 + (q + 1))
                dve.wait_ge(sg_ready, j * 4 + (q + 1))
                out = dst if q == 0 else sg[:, :]
                od.run(v.tensor_tensor(in_chunks(out), in_chunks(sg[:, :]), chunked(1), ALU.mult), br_read)
                if q > 0:
                    od.run(v.tensor_tensor(dst, dst, sg[:, :], ALU.add), merged_done)

        od.peel()
        merge(0)
        with dve.Fori(1, KD) as j:
            od.enter(j, 1)
            merge(j)
        od.leave(KD - 1)
        for k in range(KD):
            dve.wait_ge(m_hi_done, k + 1)
            od.run(v.tensor_tensor(h_lo[:, k, :], merged[:, k, :], h_hi[:, k, :].bitcast(F32), ALU.subtract), m_split)

        def sum_squares(i, blocks=range(2)):
            for s in blocks:
                dve.wait_ge(wo_read, i * 2 + (s + 1))
                if isinstance(i, int) and i + s == 0:
                    od.run(v.tensor_copy(ssq[:, :], sq[:, :]), ssq_done)
                else:
                    od.run(v.tensor_tensor(ssq[:, :], ssq[:, :], sq[:, :], ALU.add), ssq_done)

        od.peel()
        sum_squares(0)
        with dve.Fori(1, KD // 2 - 1) as i:
            od.enter(i, 1)
            sum_squares(i)
        od.leave(KD // 2 - 2)
        sum_squares(KD // 2 - 1, [0])
        for k in range(KD):
            if k == EARLY_H2:
                sum_squares(KD // 2 - 1, [1])
            dve.wait_ge(h2_hi_done, k + 1)
            od.run(v.scalar_tensor_tensor(h_lo[:, k, :], x1[:, k, :], pv[:, PV_G2 + k:PV_G2 + k + 1],
                                          h_hi[:, k, :].bitcast(F32), ALU.mult, ALU.subtract), h2_split)
        dve.wait_ge(nm_rms, 1)
        od.run(v.reciprocal(rstd, rstd))
        def ffn_tokens(s, i, k):
            dve.wait_ge(up_full, i * 4 + (2 * s + k + 1))
            x = ext[k]
            new = x[:, FH + SEQ:FE_W].rearrange("p (s n) -> p s n", s=NB)[:, :, FH:FH + NQ]
            od.run(v.tensor_tensor(x[:, FH:FH + 2 * CH].rearrange("p (c n) -> p c n", c=2), ps[k][:, 0:2, 0:CH],
                                   rstd[:, 0:2 * CH].rearrange("p (c n) -> p c n", c=2), ALU.mult))
            od.run(v.tensor_tensor(x[:, FH + 2 * CH:FH + SEQ], ps[k][:, 2, 0:SEQ - 2 * CH], rstd[:, 2 * CH:SEQ], ALU.mult))
            od.run(v.tensor_tensor(new, ps[k][:, 2, SEQ - 2 * CH:CH].rearrange("p (s n) -> p s n", s=NB),
                                   rstd[:, SEQ:T].rearrange("p (s n) -> p s n", s=NB), ALU.mult), up_read)

        def ffn_conv(e, s, i, k):
            blk = ffn_kinds(e)[k][1]
            dve.wait_ge(cv0_done, i * 4 + (2 * s + k + 1))
            x, w = ext[k], FE_W - FH
            last = x[:, SEQ:SEQ + 9 * (FH + NQ)].rearrange("p (s n) -> p s n", s=9)[:, :, 0:FH]
            od.run(v.tensor_copy(fstate[:, bass.ds(blk, 1), :].rearrange("p o (s n) -> p (o s) n", s=9), last))
            for j in range(1, FH + 1):
                od.run(v.scalar_tensor_tensor(cv[k][:, 0:w], x[:, j:j + w], pv[:, bass.ds(blk + (PV_FW + 2 * NFF * j), 1)],
                                              cv[k][:, 0:w], ALU.mult, ALU.add), cv_taps if j == FH else None)

        def ffn_product(s, i):
            w = FE_W - FH
            dve.wait_ge(silu_done, i * 2 + (s + 1))
            od.run(v.tensor_tensor(cv[0][:, 0:w], cv[0][:, 0:w], cv[1][:, 0:w], ALU.mult), prod_done)

        def ffn_lower(s, i):
            dve.wait_ge(act_hi_done, i * 2 + (s + 1))
            for n, (dst, src, hi) in enumerate(zip(packed(act_lo[:, s, :]), spaced(cv[0]),
                                                   packed(act_hi[:, s, :].bitcast(F32)))):
                od.run(v.tensor_tensor(dst, src, hi, ALU.subtract), act_split if n == 1 else None)

        def ffn_sums(base, sets, lo=0, hi=24):
            for n in range(lo, hi):
                m, c = sets[n]
                dve.wait_ge(dn_full, base + (n + 1))
                dst = x1[:, m, c * CH:(c + 1) * CH]
                od.run(v.tensor_tensor(dst, dst, pt[n % 2][:, 0:CH], ALU.add), dn_done)

        od.peel()
        for s in range(2):
            if s == 0:
                dve.wait_ge(h2_split, KD)
            ffn_tokens(s, 0, 0)
            ffn_conv(s, s, 0, 0)
            ffn_tokens(s, 0, 1)
            ffn_conv(s, s, 0, 1)
            ffn_product(s, 0)
            ffn_lower(s, 0)
        with dve.Fori(1, NFF // 2) as i:
            od.enter(i, 1, [(dn_done, 24)])
            ffn_tokens(0, i, 0)
            ffn_conv(i * 2, 0, i, 0)
            ffn_tokens(0, i, 1)
            ffn_sums((i - 1) * 24, down_sets())
            ffn_conv(i * 2, 0, i, 1)
            ffn_product(0, i)
            ffn_lower(0, i)
            ffn_tokens(1, i, 0)
            ffn_conv(i * 2 + 1, 1, i, 0)
            ffn_tokens(1, i, 1)
            ffn_conv(i * 2 + 1, 1, i, 1)
            ffn_product(1, i)
            ffn_lower(1, i)
        od.leave(NFF // 2 - 1)
        def output_tile(t):
            r = rows_of(t)
            n = len(STATES) + t
            if t == 0:
                dve.wait_ge(ld_gfin, 16)
                dve.wait_ge(w_split, W6 + 6 * (NFF // 2))
            dve.wait_ge(y_sq, t + 1)
            od.run(v.reciprocal(stat7[0:r, 2, t:t + 1], stat7[0:r, 1, t:t + 1]))
            if t >= 3:
                dve.wait_ge(y_sent[t % 3], 16 * (t // 3))
            od.run(v.scalar_tensor_tensor(y_out[t % 3][0:r, :], flat(n % 2)[0:r, 0:D], stat7[0:r, 2, t:t + 1], gfin[0:r, :],
                                          ALU.mult, ALU.mult), (out_free[n % 2], n // 2 + 1))
            od.run(v.memset(mark[:, 2:3], 0.0), y_ready)

        for what in TAIL_DVE:
            if what[0] == "sums":
                ffn_sums(24 * (NFF // 2 - 1), LAST_SETS, what[1], what[2])
            else:
                output_tile(what[1])

    @block.tensor
    def _(pe):
        mm, tr = nc.tensor.matmul, nc.tensor.transpose

        def product(dst, n, between=None):
            for k in range(KD):
                for piece in (between or {}).get(k, ()):
                    piece()
                for c in range(3):
                    tok = slice(c * CH, (c + 1) * CH)
                    mm(dst[:, c, 0:CH], f_hi[n][:, k, :], h_hi[:, k, tok], start=k == 0, stop=False)
                for c in range(3):
                    tok = slice(c * CH, (c + 1) * CH)
                    mm(dst[:, c, 0:CH], f_hi[n][:, k, :], h_lo[:, k, tok], start=False, stop=False)
                for c in range(3):
                    tok = slice(c * CH, (c + 1) * CH)
                    last = mm(dst[:, c, 0:CH], f_lo[n][:, k, :], h_hi[:, k, tok], start=False, stop=k == KD - 1)
            return last

        def project(n, between=None):
            s = JOBS[n][:2]
            pe.wait_ge(w_split, n + 1)
            slot_open(pe, s)
            product(ps[slot[s] % 2], n % 2, between).then_inc(slot_full, 1)

        def turn(src, keys, block_rows=P):
            for key, (lo, hi) in zip(keys, THIRDS):
                pt_open(pe, key)
                for t in range(lo, hi):
                    r = rows_of(t)
                    last = tr(pt_of(key)[0:r, (t - lo) * P:(t - lo) * P + block_rows],
                              src[:, t * P:t * P + r], ident[0:block_rows, 0:block_rows])
                last.then_inc(pt_full, 1)

        pe.wait_ge(ld_const, 16)
        pe.wait_ge(ld_vec, 16 * 9)
        dst = pt_of(("vec",))
        tr(dst[:, 0:94], vec1[:, :], ident[0:94, 0:94])
        tr(dst[:, 94:182], vec2[:, :], ident[0:88, 0:88])
        tr(dst[:, 182:226], vec3[:, :], ident[0:44, 0:44]).then_inc(pt_full, 1)
        pe.wait_ge(ld_hist, 32)
        dst = pt_of(("hist",))
        for b in range(6):
            tr(dst[:, 24 * b:24 * b + 24], hist_x[:, b * P:(b + 1) * P], ident[0:24, 0:24])
        for b in range(2):
            last = tr(dst[:, 144 + 120 * b:264 + 120 * b], hist_p[:, b * P:(b + 1) * P], ident[0:120, 0:120])
        last.then_inc(pt_full, 1)
        def turn_x(i):
            r = rows_of(i)
            for half in range(2):
                key = ("x", i, half)
                pe.wait_ge((x_half, x_normed)[half], i + 1)
                pt_open(pe, key)
                for k in range(4):
                    lo = half * (D // 2) + k * P
                    last = tr(pt_of(key)[:, k * P:k * P + r], x_scaled[i % 2][0:r, lo:lo + P], ident[0:r, 0:r])
                last.then_inc(pt_full, 1)

        def project_chunk(n, c):
            s = JOBS[n][:2]
            pe.wait_ge(w_split, n + 1)
            pe.wait_ge(h_split, min((c + 1) * CH + P - 1, (NT + 1) * P) // P)
            tok = slice(c * CH, (c + 1) * CH)
            dst = ps[slot[s] % 2][:, c, 0:CH]
            for k in range(KD):
                mm(dst, w_hi[n][:, k, :], h_hi[:, k, tok], start=k == 0, stop=False)
                mm(dst, w_hi[n][:, k, :], h_lo[:, k, tok], start=False, stop=False)
                last = mm(dst, w_lo[n][:, k, :], h_hi[:, k, tok], start=False, stop=k == KD - 1)
            if c == 2:
                last.then_inc(slot_full, 1)

        chunk_after = {3: (0, 0), 4: (1, 0), 6: (0, 1), 7: (1, 1)}
        for i in range(NT + 1):
            turn_x(i)
            if i in chunk_after:
                project_chunk(*chunk_after[i])
        project_chunk(0, 2)
        project_chunk(1, 2)
        project(2)
        project(3)
        pe.wait_ge(sdt_done, 1)
        for n, (lo, hi) in enumerate(((0, 5), (5, 9))):
            key = ("sdt", n)
            pt_open(pe, key)
            for t in range(lo, hi):
                r = rows_of(t)
                last = tr(pt_of(key)[0:r, (t - lo) * 100:(t - lo) * 100 + 100], sdt[0:100, t * P:t * P + r],
                          ident[0:100, 0:100])
            last.then_inc(pt_full, 1)
        project(4)
        project(5)
        slot_drained(pe, ("va", 0))
        turn(stg[ring[("va", 0)] % 2], [("va", 0, n) for n in range(3)])
        slot_drained(pe, ("va", 1))
        turn(stg[ring[("va", 1)] % 2], [("va", 1, n) for n in range(3)])
        project(6)
        pe.wait_ge(ld_ws, 32)
        key = ("ws",)
        pt_open(pe, key)
        for g in range(4):
            last = tr(pt_of(key)[:, g * P:(g + 1) * P], ws[:, g, :], ident)
        last.then_inc(pt_full, 1)
        pt_drained(pe, key)
        key = ("wsm",)
        pt_open(pe, key)
        for g in range(4):
            last = mm(pt_of(key)[0:NS, g * NS:(g + 1) * NS], const("rep4", slice(0, NQ)),
                      wst[0:NQ, g, 0:NQ].unsqueeze(1).to_broadcast([NQ, NB, NQ]), start=True, stop=True)
        last.then_inc(pt_full, 1)
        pe.wait_ge(pstate_in, 2)
        for n in range(2):
            key = ("pstate", n)
            pt_open(pe, key)
            for b in range(2):
                lo, k = n * 5 * PH, (5 - n) * PH
                last = tr(pt_of(key)[0:k, b * P:(b + 1) * P], p_state[:, b, lo:lo + k], ident)
            last.then_inc(pt_full, 1)
        project(N1A)
        pe.wait_ge(ld_pw, 80)
        pe.wait_ge(pd_done, 1)
        for b in range(2):
            s = ("mixb", b)
            slot_open(pe, s)
            dst = ps[slot[s] % 2]
            for c in range(3):
                n = CH if c < 2 else SEQ - 2 * CH
                mm(dst[:, c, 0:n], pw[:, b, :], p_ext[:, b, PH + c * CH:PH + c * CH + n], start=True, stop=True)
            new = p_ext[:, b, PH + SEQ:PE_W].rearrange("p (s n) -> p s n", s=NB)[:, :, PH:PH + NQ]
            mm(dst[:, 2, CH - NS:CH], pw[:, b, :], new, start=True, stop=True).then_inc(slot_full, 1)
        pt_drained(pe, ("wsm",))
        pe.wait_ge(va_done, 1)
        for b in range(2):
            s = ("mixa", b)
            slot_open(pe, s)
            dst = ps[slot[s] % 2]
            sel = const("pairsel", slice(0, 4)).rearrange("p (b n) -> p b n", b=2)[:, b, :]
            for c in range(2):
                mm(dst[:, c, :], sel, cmb[:, :].unsqueeze(1).to_broadcast([4, 4, P]), start=True, stop=False,
                   skip_group_check=True)
            mm(dst[:, 2, 0:NS], sel, cmb[:, 0:NQ].unsqueeze(1).to_broadcast([4, NB, NQ]), start=True, stop=False,
               skip_group_check=True)
            for half in range(2):
                g = 2 * b + half
                r = slice(64 * half, 64 * half + 64)
                for t in range(NT):
                    mm(dst[r, t // 4, (t % 4) * P:(t % 4 + 1) * P], va[:, t, g * 64:(g + 1) * 64], wst[:, g, :],
                       start=False, stop=True, skip_group_check=True)
                last = mm(dst[r, 2, 0:NS], va[0:NS, NT, g * 64:(g + 1) * 64], wsm[:, g, :], start=False, stop=True,
                          skip_group_check=True)
            last.then_inc(slot_full, 1)
        for n in range(N1A + 1, N1A + 4):
            project(n)
        slot_drained(pe, ("k", 0))
        turn(stg[ring[("k", 0)] % 2], [("k", 0, m) for m in range(3)])
        project(N1A + 4)
        slot_drained(pe, ("k", 1))
        turn(stg[ring[("k", 1)] % 2], [("k", 1, m) for m in range(3)])
        project(N1A + 5)
        for b in range(2):
            slot_drained(pe, ("v", b))
            turn(stg[ring[("v", b)] % 2], [("v", b, m) for m in range(3)])

        def scores(n):
            qb, h = steps[n]
            s = ("att", qb, h)
            nk = (qb + 1) * P
            slot_open(pe, s)
            dst = flat(slot[s] % 2)
            for lo in range(0, nk, 512):
                hi = min(lo + 512, nk)
                last = mm(dst[:, lo:hi], q_a[:, h, qb * P:(qb + 1) * P], k_a[:, h, lo:hi], start=True, stop=hi < nk,
                          skip_group_check=True)
            mm(dst[:, qb * P:nk], ident_r[:, :], attneg_r[:, :], start=False, stop=True,
               skip_group_check=True).then_inc(slot_full, 1)

        pe.wait_ge(qk_ready, 2)
        pe.wait_ge(att_rows, 32)
        scores(0)
        pe.wait_ge(ld_lf, 16 * NB * NPG)
        pe.wait_ge(clog_in, 1)
        key = ("clog",)
        pt_open(pe, key)
        for pg in range(NPG):
            tr(pt_of(key)[0:NS, pg * PAGE:(pg + 1) * PAGE], lf_pg[:, pg, :, :].rearrange("p b h -> p (b h)"), ident)
        mm(pt_of(key)[0:NS, PAST:PAST + NQ], lf_new[:, :], const("q4", slice(0, NS)), start=True,
           stop=True).then_inc(pt_full, 1)
        pe.wait_ge(v_done, 1)

        def turn_probabilities(n):
            qb, h = steps[n]
            pe.wait_ge(att_norm, n + 1)
            for k, (lo, hi) in enumerate(quads(qb)):
                key = ("p", n, k)
                pt_open(pe, key)
                for t in range(lo, hi):
                    last = tr(pt_of(key)[:, (t - lo) * P:(t - lo + 1) * P], pr[n % 2][:, t * P:(t + 1) * P], ident)
                last.then_inc(pt_full, 1)

        def values(n):
            qb, h = steps[n]
            r = slice(64 * (h % 2), 64 * (h % 2) + 64)
            if n >= 2:
                pe.wait_ge(att_out, n - 1)
            for k, (lo, hi) in enumerate(quads(qb)):
                pt_drained(pe, ("p", n, k))
                for t in range(lo, hi):
                    last = mm(ps[slot[("att", qb, h)] % 2][r, 2, 0:P], v_tok[:, t, h * HD:(h + 1) * HD],
                              pr_t[n % 2][:, t, :], start=t == 0, stop=t == qb)
            last.then_inc(att_pv, 1)

        for n, (qb, h) in enumerate(steps):
            if n + 1 < len(steps):
                scores(n + 1)
            turn_probabilities(n)
            if n >= 1:
                values(n - 1)
        values(len(steps) - 1)
        pe.wait_ge(att_out, len(steps))
        def sample_keys(n):
            key = ("sk", n)
            pe.wait_ge(ld_k[n % 2], 16 * NPG * (n // 2 + 1))
            pt_open(pe, key)
            for k in range(2):
                for pg in range(NPG):
                    last = tr(pt_of(key)[:, (k * NPG + pg) * P:(k * NPG + pg + 1) * P], k_pg[n % 2][:, pg, k * P:(k + 1) * P],
                              ident)
            last.then_inc(pt_full, 1)

        def sample_scores(n):
            key = ("ss", n)
            rows, cols = NH * NQ, slice(n * NH * NQ, (n + 1) * NH * NQ)
            pe.wait_ge(clog_done, 1)
            pe.wait_ge(sx_ready, NH)
            pt_drained(pe, ("sk", n))
            pt_open(pe, key)
            dst = pt_of(key)
            mm(dst[0:rows, 0:PAST + NS], const("expand", slice(0, NS), cols), nc_s[:, :], start=True, stop=False,
               skip_group_check=True)
            mm(dst[0:rows, 0:PAST + NS], cq_s[:, cols], const("ones", slice(0, NS)).to_broadcast([NS, PAST + NS]),
               start=False, stop=False, skip_group_check=True)
            for k in range(2):
                mm(dst[0:rows, 0:PAST], q_s[:, k, n, :], kt_s[:, k, :], start=False, stop=k == 1, skip_group_check=True)
                mm(dst[0:rows, PAST:PAST + NS], q_s[:, k, n, :], ks_new[:, k, :], start=False, stop=False,
                   skip_group_check=True)
            mm(dst[0:rows, PAST:PAST + NS], const("ident", cols=cols), const("sattneg"), start=False, stop=True,
               skip_group_check=True).then_inc(pt_full, 1)

        def sample_turn(n):
            key = ("sp", n)
            pe.wait_ge(ss_done, n + 1)
            pt_open(pe, key)
            rows = NH * NQ
            idr = const("ident", slice(0, rows), slice(0, rows))
            for pg in range(NPG):
                tr(pt_of(key)[:, pg * rows:(pg + 1) * rows], p_s[:, pg * P:(pg + 1) * P], idr)
            tr(pt_of(key)[0:NS, 2 * rows:3 * rows], p_s[:, PAST:PAST + NS], idr).then_inc(pt_full, 1)

        def sample_values(n):
            key = ("so", n)
            pe.wait_ge(ld_v, 16 * NPG * (n + 1))
            pt_drained(pe, ("sp", n))
            pt_open(pe, key)
            for k in range(2):
                dst = pt_of(key)[:, k * NH * NQ:(k + 1) * NH * NQ]
                for pg in range(NPG):
                    mm(dst, v_pg[:, pg, k * P:(k + 1) * P], pt_s[:, pg, :], start=pg == 0, stop=False)
                last = mm(dst, vs_new[:, k * P:(k + 1) * P], pt_s[0:NS, 2, :], start=False, stop=True)
            last.then_inc(pt_full, 1)

        for n in range(NB):
            project(N1B + n, {1: [lambda: sample_values(n - 1)] if n >= 1 else [], 2: [lambda: sample_keys(n)],
                              4: [lambda: sample_scores(n)], 7: [lambda: sample_turn(n)]})
        slot_drained(pe, ("z", 0))
        turn(stg[ring[("z", 0)] % 2], [("z", 0, m) for m in range(3)])
        sample_values(NB - 1)
        slot_drained(pe, ("z", 1))
        turn(stg[ring[("z", 1)] % 2], [("z", 1, m) for m in range(3)])
        pe.wait_ge(xstate_in, 6)
        for n, (lo, hi) in enumerate(((0, 4), (4, 6))):
            key = ("xst", n)
            pt_open(pe, key)
            for b in range(lo, hi):
                last = tr(pt_of(key)[0:9 * CV, (b - lo) * P:(b - lo + 1) * P], xstate[:, b, :], ident)
            last.then_inc(pt_full, 1)

        def ssd_front(c):
            s = ("ssd", c)
            r = rows_of(c)
            tok = slice(c * P, c * P + r)
            key = ("xb", c)
            pt_open(pe, key)
            for b in range(4):
                last = tr(pt_of(key)[0:r, b * P:(b + 1) * P], xc[:, b, tok], ident)
            last.then_inc(pt_full, 1)
            slot_open(pe, s)
            dst = ps[slot[s] % 2]
            for g in range(2):
                mm(dst[0:r, 0, g * P:g * P + r], xc[:, 2 + g, tok], xc[:, 4 + g, tok], start=True, stop=True)
            sel = const("acssel", slice(64, 64 + NH)).rearrange("p (h n) -> p h n", h=NH)
            for h in range(NH):
                last = mm(dst[0:r, 1, h * P:h * P + r], sel[:, h, 0:r], sdt[64:64 + NH, tok], start=True, stop=True)
            if c == NT:
                mm(dst[0:NS, 0, 256:260], const("lastsel", slice(0, NS)), sdt_t[0:NS, NT, 64:64 + NH], start=True, stop=True)
                pair = const("pairsel", slice(64, 64 + NH)).rearrange("p (g n) -> p g n", g=2)
                ends = sdt[64:64 + NH, SEQ:T].rearrange("p (b q) -> p b q", q=NQ)[:, :, NQ - 1]
                for g in range(2):
                    last = mm(dst[:, 1, 100 + NB * g:100 + NB * (g + 1)], pair[:, g, :], ends, start=True, stop=True)
            last.then_inc(slot_full, 1)

        def ssd_diag(c, first):
            s = ("ssd", c)
            r = rows_of(c)
            pe.wait_ge(xdt_done, c + 1)
            pe.wait_ge(seg_cb, c + 1)
            for h in range(NH):
                last = mm(ps[slot[s] % 2][0:r, 2, 256 + h * HD:256 + (h + 1) * HD], seg[c % 2][0:r, h, 0:r],
                          xdt[c % 2][0:r, h, :], start=first, stop=True, skip_group_check=True)
            return last

        def ssd_back_of(c):
            s = ("ssd", c)
            dst = ps[slot[s] % 2]
            tok = slice(c * P, (c + 1) * P)
            pe.wait_ge(d_zeroed, 1)
            if c >= 1:
                pe.wait_ge(h_next, c)
            for g in range(2):
                mm(dst[:, 2, g * P:(g + 1) * P], xc[:, 4 + g, tok], hst[:, 2 * g:2 * g + 2, :], start=True, stop=True)
            ssd_diag(c, True)
            pe.wait_ge(xte_done, c + 1)
            for g in range(2):
                last = mm(dst[:, 0, 256 + g * P:256 + (g + 1) * P], xb[c % 2][:, 256 + g * P:256 + (g + 1) * P],
                          xte[c % 2][:, 2 * g:2 * g + 2, :], start=True, stop=True)
            last.then_inc(ssd_back, 1)

        free_of_sx(pe)
        ssd_front(0)
        for c in range(NT):
            ssd_front(c + 1)
            ssd_back_of(c)
        dst = ps[slot[("ssd", NT)] % 2]

        def turn_state(b):
            pe.wait_ge(ld_h0[b % 2], 16 * (b // 2 + 1))
            key = ("sh", b)
            pt_open(pe, key)
            for g in range(2):
                last = tr(pt_of(key)[:, g * P:(g + 1) * P], h0[b % 2][:, g, :], ident)
            last.then_inc(pt_full, 1)

        turn_state(0)
        for b in range(NB):
            key = ("sn", b)
            pe.wait_ge(xtm_done, b + 1)
            pt_open(pe, key)
            for g in range(2):
                last = mm(pt_of(key)[:, g * P:(g + 1) * P], xtm[b % 2][:, g * P:(g + 1) * P],
                          xb[NT % 2][0:NS, 256 + g * P:256 + (g + 1) * P], start=True, stop=True)
            last.then_inc(pt_full, 1)
            if b + 1 < NB:
                turn_state(b + 1)
            pt_drained(pe, ("sh", b))
            if b == 0:
                pe.wait_ge(ctm_done, 2 * NB)
            for g in range(2):
                mm(dst[0:NS, 2, g * P:(g + 1) * P], ctm[:, g, b, :], h0t[b % 2][:, g, :], start=b == 0 and g == 0,
                   stop=b == NB - 1, skip_group_check=True)
        ssd_diag(NT, False).then_inc(ssd_back, 1)
        key = ("hp",)
        pe.wait_ge(h_next, NT)
        pt_open(pe, key)
        for g in range(2):
            last = tr(pt_of(key)[:, g * P:(g + 1) * P], hst[:, 2 * g:2 * g + 2, :].rearrange("p h d -> p (h d)"), ident)
        last.then_inc(pt_full, 1)

        def turn_branch_d(t):
            r = rows_of(t)
            key = ("yd", t)
            pe.wait_ge(yd_ready, t + 1)
            pt_open(pe, key)
            for b in range(2):
                last = tr(pt_of(key)[:, b * P:b * P + r], zt[0:r, t, b * P:(b + 1) * P], ident[0:r, 0:r])
            last.then_inc(pt_full, 1)
        def gate(j, q, between=None):
            n = W3 + q
            pe.wait_ge(w_split, j * 4 + (n + 1))
            if isinstance(j, int) and q == 0:
                slot_drained(pe, slots[-2])
                slot_drained(pe, slots[-1])
            else:
                pe.wait_ge(sg_ready, j * 4 + q)
            product(ps[0], n % 2, between).then_inc(gate_full, 1)

        def branch(j, q):
            pe.wait_ge(b_split, j * 4 + (q + 1))
            if isinstance(j, int):
                pe.wait_ge(y_split, 2 * q + 2)
            if not isinstance(j, int) or q >= 1:
                pe.wait_ge(br_read, j * 4 + q)
            parts = [(bw_hi, y_hi), (bw_hi, y_lo), (bw_lo, y_hi)]
            for k in range(2):
                for n, (w, y) in enumerate(parts):
                    for c in range(3):
                        last = mm(ps[1][:, c, 0:CH], w[q % 2][:, k, :], y[:, 2 * q + k, c * CH:(c + 1) * CH],
                                  start=k == 0 and n == 0, stop=k == 1 and n == 2)
            last.then_inc(br_full, 1)

        turns = {k: [] for k in range(KD)}
        for t in range(NT + 1):
            turns[min(3 + t // 2, KD - 1)].append(lambda t=t: turn_branch_d(t))
        for q in range(4):
            gate(0, q, turns if q == 0 else None)
            branch(0, q)
        with pe.Fori(1, KD) as j:
            for q in range(4):
                gate(j, q)
                branch(j, q)

        def out_block(i, s):
            first = isinstance(i, int)
            n = W4 + s
            pe.wait_ge(w_split, i * 2 + (n + 1))
            if not first:
                pe.wait_ge(wo_read, i * 2 + (s - 1))
            elif s == 0:
                pe.wait_ge(sg_ready, 4 * KD)
            else:
                pe.wait_ge(br_read, 4 * KD)
            stairs = {k: [lambda k=k: pe.wait_ge(m_split, k + 1)] for k in range(KD)} if first and s == 0 else None
            product(ps[s], n % 2, stairs).then_inc(merged_used, 1)
            pe.wait_ge(ld_res[s], i * 32 + 32)
            for t in range(NT + 1):
                lo, hi = t * P, t * P + rows_of(t)
                while lo < hi:
                    c = lo // CH
                    end = min(hi, (c + 1) * CH)
                    last = mm(ps[s][:, c, lo - c * CH:end - c * CH], x_res[s][0:rows_of(t), t, :],
                              ident[0:rows_of(t), lo - t * P:end - t * P], start=False, stop=True,
                              skip_group_check=True)
                    lo = end
            last.then_inc(wo_full, 1)

        for s in range(2):
            out_block(0, s)
        pe.wait_ge(ld_fh, 16)
        pt_drained(pe, batches[-2])
        pt_drained(pe, batches[-1])
        for n in range(2):
            for b in range(NFF):
                blk = n * NFF + b
                last = tr(pt[n][:, b * NB * FH:(b + 1) * NB * FH], hist_f[0:NB * FH, blk * P:(blk + 1) * P],
                          ident[0:NB * FH, 0:NB * FH])
            last.then_inc(fh_full, 1)
        with pe.Fori(1, KD // 2) as i:
            for s in range(2):
                out_block(i, s)
        def sum_of_squares():
            pe.wait_ge(ones_done, 1)
            pe.wait_ge(ssq_done, KD)
            pe.wait_ge(wo_read, KD)
            for c in range(3):
                last = mm(ps[1][:, c, 0:CH], ones_m[:, :], ssq[:, c * CH:(c + 1) * CH], start=True, stop=True)
            last.then_inc(nm_full, 1)

        def up(s, i, f):
            for k in range(2):
                pe.wait_ge(w_split, i * 6 + (W6 + f + k + 1))
                start = isinstance(i, int) and i == 0 and s == 0
                if not start:
                    pe.wait_ge(up_read, i * 4 + (2 * s + k - 1))
                elif k == 1:
                    pe.wait_ge(nm_rms, 1)
                stairs = {q: [lambda q=q: pe.wait_ge(h2_split, q + 1)] for q in range(KD)} \
                    if start and k == 0 else None
                if stairs:
                    stairs[5].append(sum_of_squares)
                product(ps[k], ring_slot(f + k), stairs).then_inc(up_full, 1)

        def down(i, f, base_split, sets=down_sets(), lo=0, hi=24):
            pe.wait_ge(act_split, i * 2 + 2)
            pe.wait_ge(w_split, base_split)
            for n in range(lo, hi):
                m, c = sets[n]
                if isinstance(i, int) and i == 0 and n < 2:
                    pe.wait_ge(fh_done, 2)
                else:
                    pe.wait_ge(dn_done, i * 24 + (n - 1))
                tok = slice(c * CH, (c + 1) * CH)
                for k in range(2):
                    w, w_rest = f_hi[ring_slot(f + k)], f_lo[ring_slot(f + k)]
                    dst = pt[n % 2][:, 0:CH]
                    mm(dst, w[:, m, :], act_hi[:, k, tok], start=k == 0, stop=False)
                    mm(dst, w[:, m, :], act_lo[:, k, tok], start=False, stop=False)
                    last = mm(dst, w_rest[:, m, :], act_hi[:, k, tok], start=False, stop=k == 1)
                last.then_inc(dn_full, 1)

        up(0, 0, 0)
        up(1, 0, 2)
        up(0, 1, -2)
        down(0, 6, W6 + 4 + 4)
        up(1, 1, 2)
        with pe.Fori(2, NFF // 2) as i:
            up(0, i, -2)
            down(i - 1, 6, i * 6 + (W6 + 4 + 4 - 6))
            up(1, i, 2)
        n_ring = 4 + 6 * (NFF // 2 - 1)
        last_pair = NFF // 2 - 1

        def turn_ffn_state(n):
            pe.wait_ge(cv_taps, 2 * NFF if n == len(STATES) - 1 else 2 * (NFF - 1))
            if n < 2:
                pe.wait_ge(up_read, 2 * NFF - 1 + n)
            else:
                pe.wait_ge(out_free[n % 2], n // 2)
            at = 0
            for lo, hi in STATES[n]:
                for b in range(lo, hi):
                    last = tr(flat(n % 2)[0:9 * FH, at * P:(at + 1) * P], fstate[:, b, :], ident)
                    at += 1
            last.then_inc(out_full, 1)

        def turn_tile(t):
            r = rows_of(t)
            n = len(STATES) + t
            pe.wait_ge(dn_done, 24 * last_pair + KD * min(3, (t * P + r - 1) // CH + 1))
            pe.wait_ge(out_free[n % 2], n // 2)
            for k in range(KD):
                last = tr(flat(n % 2)[0:r, k * P:(k + 1) * P], x1[:, k, t * P:t * P + r], ident)
            last.then_inc(out_full, 1)

        for n in range(4):
            turn_ffn_state(n)
        for what in TAIL:
            if what[0] == "sums":
                down(last_pair, n_ring, W6 + n_ring + 2, LAST_SETS, what[1], what[2])
            elif what[0] == "state":
                turn_ffn_state(what[1])
            else:
                turn_tile(what[1])
    top.close()


INPUTS = ["x_prompt", "x_sample", "cache_k", "cache_v", "cache_logf", "page_table", "state_pool", "state_ssd_conv",
          "state_ssd", "state_ffn_conv", "norm1_g", "w_in", "cm_norm_g", "cm_ws", "cm_b", "pool_w", "pool_scale",
          "fox_bf", "ssd_conv_w", "ssd_conv_b", "ssd_dt_bias", "ssd_a_log", "ssd_d", "ssd_norm_g", "w_branch",
          "w_out", "norm2_g", "ffn_up", "ffn_conv_w", "ffn_conv_b", "ffn_down", "final_norm_g"]
OUTPUTS = [("y_prompt", (1, SEQ, D)), ("y_sample", (NB, NQ, D)), ("k_prompt", (1, 1, SEQ, NH, HD)),
           ("v_prompt", (1, 1, SEQ, NH, HD)), ("logf_prompt", (1, 1, SEQ, NH)), ("k_sample", (1, NB, NQ, NH, HD)),
           ("v_sample", (1, NB, NQ, NH, HD)), ("logf_sample", (1, NB, NQ, NH)), ("chunk_v_sample", (1, NB, NQ, CMW)),
           ("pool_prompt", (1, 1, PH, PLW)), ("pool_sample", (1, NB, PH, PLW)), ("ssd_conv_prompt", (1, 1, CV, XBC)),
           ("ssd_conv_sample", (1, NB, CV, XBC)), ("ssd_prompt", (1, 1, NH, HD, SST)),
           ("ssd_sample", (1, NB, NH, HD, SST)), ("ffn_conv_prompt", (1, 1, FH, 2 * FF)),
           ("ffn_conv_sample", (1, NB, FH, 2 * FF))]


def kernel(**inputs):
    import concourse.bacc as bacc
    from concourse.bass_utils import run_bass_kernel_spmd

    nc = bacc.Bacc("TRN2", target_bir_lowering=False, num_devices=1)
    arrays, a, o = {}, {}, {}
    given = {name: np.ascontiguousarray(inputs[name]) for name in INPUTS}
    given["consts"] = constants()
    for name, x in given.items():
        arrays[f"in_{name}"] = x
        a[name] = nc.dram_tensor(f"in_{name}", x.shape, mybir.dt.from_np(x.dtype), kind="ExternalInput").ap()
    for name, shape in OUTPUTS:
        o[name] = nc.dram_tensor(f"out_{name}", shape, F32, kind="ExternalOutput").ap()
    decoder_layer(nc, a, o)
    r = run_bass_kernel_spmd(nc, [arrays], core_ids=[0])
    return tuple(r.results[0][f"out_{name}"] for name, _ in OUTPUTS)
```
